# Optimizing a Trainium2 kernel written in Bass

```python
import jax, jax.numpy as jnp
from jax import lax
import numpy as np

D_MODEL = 1024
BATCH = 1
SEQ = 256
DEPTH = 2

N_MIXERS = 2
HEAD_DIM = 64
N_HEADS = D_MODEL // HEAD_DIM
MIX_WIDTH = N_HEADS * HEAD_DIM
N_KV_A = max(1, N_HEADS // 8)
N_KV_B = max(1, N_HEADS // 4)
WINDOW = 128
MOBA_BLOCK = 256
MOBA_TOPK = 3
MOBA_Q_CHUNK = 16
ROPE_THETA = 10000.0
NORM_EPS = 1e-5
NEG = -1e30
N_LAYERS_A = (DEPTH + 1) // 2
N_LAYERS_B = DEPTH // 2
IN_A = 2 * MIX_WIDTH + 2 * N_KV_A * HEAD_DIM
IN_B = 2 * MIX_WIDTH + 2 * N_KV_B * HEAD_DIM


def rmsnorm(x, g):
    xf = x.astype(jnp.float32)
    y = xf * lax.rsqrt(jnp.mean(xf * xf, axis=-1, keepdims=True) + NORM_EPS)
    return (y * g.astype(jnp.float32)).astype(x.dtype)

def rope_tables(seq):
    pos = jnp.arange(seq, dtype=jnp.float32)
    inv = ROPE_THETA ** (-jnp.arange(0, HEAD_DIM, 2, dtype=jnp.float32) / HEAD_DIM)
    ang = pos[:, None] * inv[None, :]
    return jnp.cos(ang), jnp.sin(ang)

def apply_rope(x, cos, sin):
    half = HEAD_DIM // 2
    x1, x2 = x[..., :half], x[..., half:]
    c, s = cos[None, :, None, :], sin[None, :, None, :]
    out = jnp.concatenate([x1 * c - x2 * s, x2 * c + x1 * s], axis=-1)
    return out.astype(x.dtype)

def split_proj(h, w_in, n_kv):
    B, S, _ = h.shape
    proj = h @ w_in
    kvw = n_kv * HEAD_DIM
    q = proj[..., :MIX_WIDTH].reshape(B, S, N_HEADS, HEAD_DIM)
    k = proj[..., MIX_WIDTH:MIX_WIDTH + kvw].reshape(B, S, n_kv, HEAD_DIM)
    v = proj[..., MIX_WIDTH + kvw:MIX_WIDTH + 2 * kvw].reshape(B, S, n_kv, HEAD_DIM)
    z = proj[..., MIX_WIDTH + 2 * kvw:]
    return q, k, v, z

def sliding_window_sink_attention(q, k, v, sinks):
    B, S, H, d = q.shape
    kvh = k.shape[2]
    G = H // kvh
    nq = S // WINDOW
    scale = 1.0 / np.sqrt(d)
    qb = q.reshape(B, nq, WINDOW, kvh, G, d)
    pad = ((0, 0), (WINDOW, 0), (0, 0), (0, 0))
    kb = jnp.pad(k, pad).reshape(B, nq + 1, WINDOW, kvh, d)
    vb = jnp.pad(v, pad).reshape(B, nq + 1, WINDOW, kvh, d)
    kband = jnp.concatenate([kb[:, :-1], kb[:, 1:]], axis=2)
    vband = jnp.concatenate([vb[:, :-1], vb[:, 1:]], axis=2)
    s = jnp.einsum('bnikgd,bnjkd->bnkgij', qb, kband).astype(jnp.float32) * scale
    i = jnp.arange(WINDOW)[:, None]
    j = jnp.arange(2 * WINDOW)[None, :]
    band = (j > i) & (j <= i + WINDOW)
    not_pad = (jnp.arange(nq)[:, None, None] > 0) | (j[None] >= WINDOW)
    mask = band[None] & not_pad
    s = jnp.where(mask[None, :, None, None], s, NEG)
    sink = jnp.broadcast_to(sinks.astype(jnp.float32).reshape(kvh, G)[None, None, :, :, None, None],
                            s.shape[:-1] + (1,))
    p = jax.nn.softmax(jnp.concatenate([s, sink], axis=-1), axis=-1)[..., :-1]
    o = jnp.einsum('bnkgij,bnjkd->bnikgd', p.astype(v.dtype), vband)
    return o.reshape(B, S, H, d)

def moba_attention(q, k, v):
    B, S, H, d = q.shape
    kvh = k.shape[2]
    G = H // kvh
    nb = -(-S // MOBA_BLOCK)
    Sp = nb * MOBA_BLOCK
    scale = 1.0 / np.sqrt(d)
    pad = ((0, 0), (0, Sp - S), (0, 0), (0, 0))
    kblk = jnp.pad(k, pad).reshape(B, nb, MOBA_BLOCK, kvh, d).transpose(0, 3, 1, 2, 4)
    vblk = jnp.pad(v, pad).reshape(B, nb, MOBA_BLOCK, kvh, d).transpose(0, 3, 1, 2, 4)
    kmean = jnp.mean(kblk.astype(jnp.float32), axis=3)
    qg = q.reshape(B, S, kvh, G, d)
    gate = jnp.einsum('bskgd,bknd->bskgn', qg.astype(jnp.float32), kmean)
    qblock = jnp.arange(S) // MOBA_BLOCK
    past = jnp.arange(nb)[None, :] < qblock[:, None]
    gate = jnp.where(past[None, :, None, None, :], gate, NEG)
    kk = min(MOBA_TOPK, nb)
    _, idx = lax.top_k(gate, kk)
    nc = S // MOBA_Q_CHUNK
    q_c = qg.reshape(B, nc, MOBA_Q_CHUNK, kvh, G, d).transpose(1, 0, 2, 3, 4, 5)
    idx_c = idx.reshape(B, nc, MOBA_Q_CHUNK, kvh, G, kk).transpose(1, 0, 2, 3, 4, 5)
    bi = jnp.arange(B)[:, None, None, None, None]
    ki = jnp.arange(kvh)[None, None, :, None, None]

    def chunk(args):
        ci, qc, ic = args
        t0 = ci * MOBA_Q_CHUNK
        t = t0 + jnp.arange(MOBA_Q_CHUNK)
        cblk = t0 // MOBA_BLOCK
        ksel = kblk[bi, ki, ic]
        vsel = vblk[bi, ki, ic]
        s_sel = jnp.einsum('bqkgd,bqkgsnd->bqkgsn', qc, ksel).astype(jnp.float32) * scale
        slot_ok = jnp.arange(kk) < cblk
        s_sel = jnp.where(slot_ok[:, None], s_sel, NEG)
        kown = lax.dynamic_index_in_dim(kblk, cblk, axis=2, keepdims=False)
        vown = lax.dynamic_index_in_dim(vblk, cblk, axis=2, keepdims=False)
        s_own = jnp.einsum('bqkgd,bknd->bqkgn', qc, kown).astype(jnp.float32) * scale
        kpos = cblk * MOBA_BLOCK + jnp.arange(MOBA_BLOCK)
        causal = kpos[None, :] <= t[:, None]
        s_own = jnp.where(causal[None, :, None, None, :], s_own, NEG)
        nsel = kk * MOBA_BLOCK
        logits = jnp.concatenate([s_sel.reshape(B, MOBA_Q_CHUNK, kvh, G, nsel), s_own], axis=-1)
        p = jax.nn.softmax(logits, axis=-1).astype(v.dtype)
        o = jnp.einsum('bqkgm,bqkgmd->bqkgd', p[..., :nsel],
                       vsel.reshape(B, MOBA_Q_CHUNK, kvh, G, nsel, d))
        o = o + jnp.einsum('bqkgn,bknd->bqkgd', p[..., nsel:], vown)
        return o

    out = lax.map(chunk, (jnp.arange(nc), q_c, idx_c))
    return out.transpose(1, 0, 2, 3, 4, 5).reshape(B, S, H, d)

def first_inputs(seed: int = 0) -> dict:
    key = jax.random.key(seed)
    ks = jax.random.split(key, 7)
    x = jax.random.normal(ks[0], (BATCH, SEQ, D_MODEL), jnp.float32)
    norm_g = 1.0 + 0.02 * jax.random.normal(ks[1], (DEPTH, D_MODEL), jnp.float32)
    w_in_a = jax.random.normal(ks[2], (N_LAYERS_A, D_MODEL, IN_A), jnp.float32) * D_MODEL ** -0.5
    sinks_a = jax.random.normal(ks[3], (N_LAYERS_A, N_HEADS), jnp.float32)
    w_in_b = jax.random.normal(ks[4], (N_LAYERS_B, D_MODEL, IN_B), jnp.float32) * D_MODEL ** -0.5
    w_out = jax.random.normal(ks[5], (DEPTH, MIX_WIDTH, D_MODEL), jnp.float32) * MIX_WIDTH ** -0.5
    final_g = 1.0 + 0.02 * jax.random.normal(ks[6], (D_MODEL,), jnp.float32)
    return {"x": x, "norm_g": norm_g, "w_in_a": w_in_a, "sinks_a": sinks_a,
            "w_in_b": w_in_b, "w_out": w_out, "final_g": final_g}

def first_block(x, norm_g, w_in_a, sinks_a, w_in_b, w_out, final_g):
    B, S, _ = x.shape
    cos, sin = rope_tables(S)
    h = x
    for i in range(DEPTH):
        hn = rmsnorm(h, norm_g[i])
        j = i // N_MIXERS
        if i % N_MIXERS == 0:
            q, k, v, z = split_proj(hn, w_in_a[j], N_KV_A)
            q, k = apply_rope(q, cos, sin), apply_rope(k, cos, sin)
            o = sliding_window_sink_attention(q, k, v, sinks_a[j])
        else:
            q, k, v, z = split_proj(hn, w_in_b[j], N_KV_B)
            q, k = apply_rope(q, cos, sin), apply_rope(k, cos, sin)
            o = moba_attention(q, k, v)
        o = o.reshape(B, S, MIX_WIDTH) * jax.nn.silu(z)
        h = h + o @ w_out[i]
    return rmsnorm(h, final_g)


N_ATTN_HEADS = 8
N_KV_HEADS = 2
GQA_GROUP = N_ATTN_HEADS // N_KV_HEADS
ATTN_WIDTH = N_ATTN_HEADS * HEAD_DIM
KV_WIDTH = N_KV_HEADS * HEAD_DIM
ROPE_DIM = HEAD_DIM // 4
ROPE_THETA_2 = 500000.0
DILATED_PATTERNS = ((128, 1), (512, 4), (2048, 16))
ATTN_BLOCK = 128

SSM_HEAD_DIM = 64
SSM_HEADS = 16
SSM_INNER = SSM_HEADS * SSM_HEAD_DIM
SSM_GROUPS = 2
D_STATE = 128
CONV_WIDTH = 4
CHUNK = 128
CONV_CH = SSM_INNER + 2 * SSM_GROUPS * D_STATE

MIX_WIDTH_2 = ATTN_WIDTH + SSM_INNER
Q_END = ATTN_WIDTH
K_END = Q_END + KV_WIDTH
V_END = K_END + KV_WIDTH
Z_END = V_END + SSM_INNER
XBC_END = Z_END + CONV_CH
IN_PROJ = XBC_END + SSM_HEADS

FFN_HIDDEN = ((8 * D_MODEL + 3 * 256 - 1) // (3 * 256)) * 256
EPS = 1e-5


def rmsnorm_2(x, w):
    xf = x.astype(jnp.float32)
    y = xf * lax.rsqrt(jnp.mean(xf * xf, axis=-1, keepdims=True) + EPS)
    return (y * w.astype(jnp.float32)).astype(x.dtype)

def rotary_tables(positions, dtype):
    inv_freq = ROPE_THETA_2 ** (-jnp.arange(0, ROPE_DIM, 2, dtype=jnp.float32) / ROPE_DIM)
    ang = positions.astype(jnp.float32)[..., None] * inv_freq
    return jnp.cos(ang)[:, :, None, :].astype(dtype), jnp.sin(ang)[:, :, None, :].astype(dtype)

def partial_rotary(t, cos, sin):
    half = ROPE_DIM // 2
    t1, t2, rest = t[..., :half], t[..., half:ROPE_DIM], t[..., ROPE_DIM:]
    return jnp.concatenate([t1 * cos - t2 * sin, t2 * cos + t1 * sin, rest], axis=-1)

def dilated_window_branch(q, k, v, window, dilation):
    bsz, s = q.shape[0], q.shape[1]
    length = s // dilation
    w_d = window // dilation
    nb = -(-length // ATTN_BLOCK)
    lp = nb * ATTN_BLOCK
    qd = q.reshape((bsz, length, dilation) + q.shape[2:])
    kd = k.reshape((bsz, length, dilation) + k.shape[2:])
    vd = v.reshape((bsz, length, dilation) + v.shape[2:])
    qd = jnp.pad(qd, [(0, 0), (0, lp - length)] + [(0, 0)] * (qd.ndim - 2))
    kv_pad = [(0, 0), (ATTN_BLOCK, lp - length)] + [(0, 0)] * (kd.ndim - 2)
    kd = jnp.pad(kd, kv_pad)
    vd = jnp.pad(vd, kv_pad)
    qb = qd.reshape((bsz, nb, ATTN_BLOCK) + qd.shape[2:])
    kb = kd.reshape((bsz, nb + 1, ATTN_BLOCK) + kd.shape[2:])
    vb = vd.reshape((bsz, nb + 1, ATTN_BLOCK) + vd.shape[2:])
    kb = jnp.concatenate([kb[:, :-1], kb[:, 1:]], axis=2)
    vb = jnp.concatenate([vb[:, :-1], vb[:, 1:]], axis=2)
    scores = jnp.einsum('bnqrhgc,bnkrhc->bnrhgqk', qb, kb).astype(jnp.float32)
    qi = jnp.arange(ATTN_BLOCK)[:, None]
    ki = jnp.arange(2 * ATTN_BLOCK)[None, :]
    delta = qi + ATTN_BLOCK - ki
    kpos = jnp.arange(nb)[:, None, None] * ATTN_BLOCK - ATTN_BLOCK + ki[None]
    valid = (delta >= 0)[None] & (delta <= w_d)[None] & (kpos >= 0)
    scores = jnp.where(valid[None, :, None, None, None], scores, -jnp.inf)
    m = jnp.max(scores, axis=-1, keepdims=True)
    p = jnp.exp(scores - m)
    den = jnp.sum(p, axis=-1, keepdims=True)
    o = jnp.einsum('bnrhgqk,bnkrhc->bnrhgqc', p, vb.astype(jnp.float32)) / den
    lse = (m + jnp.log(den))[..., 0]
    o = jnp.transpose(o, (0, 1, 5, 2, 3, 4, 6)).reshape((bsz, lp, dilation) + q.shape[2:])
    lse = jnp.transpose(lse, (0, 1, 5, 2, 3, 4)).reshape((bsz, lp, dilation) + q.shape[2:4])
    o = o[:, :length].reshape(q.shape)
    lse = lse[:, :length].reshape(q.shape[:4])
    return o, lse

def dilated_attention(q, k, v):
    outs, lses = [], []
    for window, dilation in DILATED_PATTERNS:
        o, l = dilated_window_branch(q, k, v, window, dilation)
        outs.append(o)
        lses.append(l)
    wts = jax.nn.softmax(jnp.stack(lses, axis=0), axis=0)
    return jnp.einsum('ibshg,ibshgc->bshgc', wts, jnp.stack(outs, axis=0))

def causal_depthwise_conv(u, w, b):
    y = lax.conv_general_dilated(u, w[:, None, :], window_strides=(1,),
                                 padding=[(CONV_WIDTH - 1, 0)],
                                 dimension_numbers=('NWC', 'WIO', 'NWC'),
                                 feature_group_count=u.shape[-1])
    return y + b

def segsum_exp(a):
    cs = jnp.cumsum(a, axis=-1)
    diff = cs[..., :, None] - cs[..., None, :]
    t = a.shape[-1]
    mask = jnp.tril(jnp.ones((t, t), dtype=bool))
    return jnp.exp(jnp.where(mask, diff, -jnp.inf))

def ssd_chunked(xs, dt, a_neg, bm, cm):
    bsz, s, nh, hp = xs.shape
    nc = s // CHUNK
    e = nh // SSM_GROUPS
    xg = (xs.astype(jnp.float32) * dt[..., None]).reshape(bsz, nc, CHUNK, SSM_GROUPS, e, hp)
    a = jnp.transpose((dt * a_neg).reshape(bsz, nc, CHUNK, SSM_GROUPS, e), (0, 1, 3, 4, 2))
    bc = bm.astype(jnp.float32).reshape(bsz, nc, CHUNK, SSM_GROUPS, D_STATE)
    cc = cm.astype(jnp.float32).reshape(bsz, nc, CHUNK, SSM_GROUPS, D_STATE)
    a_cs = jnp.cumsum(a, axis=-1)
    cb = jnp.einsum('bclgn,bcsgn->bcgls', cc, bc)
    m_mat = cb[:, :, :, None] * segsum_exp(a)
    y_diag = jnp.einsum('bcgels,bcsgep->bclgep', m_mat, xg)
    decay_states = jnp.exp(a_cs[..., -1:] - a_cs)
    states = jnp.einsum('bclgn,bcgel,bclgep->bcgepn', bc, decay_states, xg)
    chunk_decay = jnp.exp(a_cs[..., -1])

    def step(h, inp):
        dec, st = inp
        return h * dec[..., None, None] + st, h

    h0 = jnp.zeros((bsz, SSM_GROUPS, e, hp, D_STATE), jnp.float32)
    _, prev = lax.scan(step, h0, (jnp.moveaxis(chunk_decay, 1, 0), jnp.moveaxis(states, 1, 0)))
    prev_states = jnp.moveaxis(prev, 0, 1)
    y_off = jnp.einsum('bclgn,bcgepn,bcgel->bclgep', cc, prev_states, jnp.exp(a_cs))
    return (y_diag + y_off).reshape(bsz, s, nh, hp)

def hybrid_mixer(h, w_in, conv_w, conv_b, dt_bias, a_log, d_skip, ssm_norm, w_out, cos, sin):
    bsz, s, _ = h.shape
    proj = h @ w_in
    q, k, v, z, xbc, dt = jnp.split(proj, [Q_END, K_END, V_END, Z_END, XBC_END], axis=-1)
    q = partial_rotary(q.reshape(bsz, s, N_ATTN_HEADS, HEAD_DIM), cos, sin)
    k = partial_rotary(k.reshape(bsz, s, N_KV_HEADS, HEAD_DIM), cos, sin)
    v = v.reshape(bsz, s, N_KV_HEADS, HEAD_DIM)
    q = (q * (HEAD_DIM ** -0.5)).reshape(bsz, s, N_KV_HEADS, GQA_GROUP, HEAD_DIM)
    attn = dilated_attention(q, k, v).reshape(bsz, s, ATTN_WIDTH).astype(h.dtype)
    xbc = jax.nn.silu(causal_depthwise_conv(xbc, conv_w, conv_b))
    xs, bm, cm = jnp.split(xbc, [SSM_INNER, SSM_INNER + SSM_GROUPS * D_STATE], axis=-1)
    xs = xs.reshape(bsz, s, SSM_HEADS, SSM_HEAD_DIM)
    bm = bm.reshape(bsz, s, SSM_GROUPS, D_STATE)
    cm = cm.reshape(bsz, s, SSM_GROUPS, D_STATE)
    dt = jax.nn.softplus(dt.astype(jnp.float32) + dt_bias.astype(jnp.float32))
    a_neg = -jnp.exp(a_log.astype(jnp.float32))
    y = ssd_chunked(xs, dt, a_neg, bm, cm) + d_skip.astype(jnp.float32)[:, None] * xs.astype(jnp.float32)
    y = y.reshape(bsz, s, SSM_INNER).astype(h.dtype) * jax.nn.silu(z)
    gsize = SSM_INNER // SSM_GROUPS
    y = rmsnorm_2(y.reshape(bsz, s, SSM_GROUPS, gsize), ssm_norm.reshape(SSM_GROUPS, gsize))
    y = y.reshape(bsz, s, SSM_INNER)
    return jnp.concatenate([attn, y], axis=-1) @ w_out

def swiglu(h, w_gate, w_up, w_down):
    return (jax.nn.silu(h @ w_gate) * (h @ w_up)) @ w_down

def second_inputs(seed: int = 0) -> dict:
    key = jax.random.key(seed)
    ks = jax.random.split(key, 16)
    f32 = jnp.float32
    x = jax.random.normal(ks[0], (BATCH, SEQ, D_MODEL), f32)
    positions = jnp.broadcast_to(jnp.arange(SEQ, dtype=jnp.int32), (BATCH, SEQ))
    norm_mix = 1.0 + 0.02 * jax.random.normal(ks[1], (DEPTH, D_MODEL), f32)
    w_in = jax.random.normal(ks[2], (DEPTH, D_MODEL, IN_PROJ), f32) * D_MODEL ** -0.5
    conv_w = jax.random.normal(ks[3], (DEPTH, CONV_WIDTH, CONV_CH), f32) * CONV_WIDTH ** -0.5
    conv_b = 0.01 * jax.random.normal(ks[4], (DEPTH, CONV_CH), f32)
    dt0 = jnp.exp(jax.random.uniform(ks[5], (DEPTH, SSM_HEADS), f32, np.log(1e-3), np.log(1e-1)))
    dt_bias = dt0 + jnp.log(-jnp.expm1(-dt0))
    a_log = jnp.log(jax.random.uniform(ks[6], (DEPTH, SSM_HEADS), f32, 1.0, 16.0))
    d_skip = 1.0 + 0.1 * jax.random.normal(ks[7], (DEPTH, SSM_HEADS), f32)
    ssm_norm = 1.0 + 0.02 * jax.random.normal(ks[8], (DEPTH, SSM_INNER), f32)
    w_out = jax.random.normal(ks[9], (DEPTH, MIX_WIDTH_2, D_MODEL), f32) * MIX_WIDTH_2 ** -0.5
    norm_ffn = 1.0 + 0.02 * jax.random.normal(ks[10], (DEPTH, D_MODEL), f32)
    w_gate = jax.random.normal(ks[11], (DEPTH, D_MODEL, FFN_HIDDEN), f32) * D_MODEL ** -0.5
    w_up = jax.random.normal(ks[12], (DEPTH, D_MODEL, FFN_HIDDEN), f32) * D_MODEL ** -0.5
    w_down = jax.random.normal(ks[13], (DEPTH, FFN_HIDDEN, D_MODEL), f32) * FFN_HIDDEN ** -0.5
    final_norm = 1.0 + 0.02 * jax.random.normal(ks[14], (D_MODEL,), f32)
    return {"x": x, "positions": positions, "norm_mix": norm_mix, "w_in": w_in,
            "conv_w": conv_w, "conv_b": conv_b, "dt_bias": dt_bias, "a_log": a_log,
            "d_skip": d_skip, "ssm_norm": ssm_norm, "w_out": w_out, "norm_ffn": norm_ffn,
            "w_gate": w_gate, "w_up": w_up, "w_down": w_down, "final_norm": final_norm}

def second_block(x, positions, norm_mix, w_in, conv_w, conv_b, dt_bias, a_log, d_skip, ssm_norm,
              w_out, norm_ffn, w_gate, w_up, w_down, final_norm):
    cos, sin = rotary_tables(positions, x.dtype)
    h = x
    for layer in range(DEPTH):
        h = h + hybrid_mixer(rmsnorm_2(h, norm_mix[layer]), w_in[layer], conv_w[layer],
                             conv_b[layer], dt_bias[layer], a_log[layer], d_skip[layer],
                             ssm_norm[layer], w_out[layer], cos, sin)
        h = h + swiglu(rmsnorm_2(h, norm_ffn[layer]), w_gate[layer], w_up[layer], w_down[layer])
    return rmsnorm_2(h, final_norm)


def setup_inputs(seed=0):
    out = dict(first_inputs(seed))
    for name, value in second_inputs(seed + 1).items():
        if name != "x":
            out[name + "_2"] = value
    return out


def reference(
    x, norm_g, w_in_a, sinks_a, w_in_b, w_out, final_g, positions_2, norm_mix_2, w_in_2,
    conv_w_2, conv_b_2, dt_bias_2, a_log_2, d_skip_2, ssm_norm_2, w_out_2, norm_ffn_2, w_gate_2,
    w_up_2, w_down_2, final_norm_2,
):
    x = first_block(
        x, norm_g, w_in_a, sinks_a, w_in_b, w_out, final_g,
    )
    return second_block(
        x, positions_2, norm_mix_2, w_in_2, conv_w_2, conv_b_2, dt_bias_2, a_log_2, d_skip_2,
        ssm_norm_2, w_out_2, norm_ffn_2, w_gate_2, w_up_2, w_down_2, final_norm_2,
    )


_drawn_inputs = setup_inputs


def setup_inputs(seed=0):
    import zlib

    import numpy as np

    out = dict(_drawn_inputs(seed))
    spreads = {}
    factors = {'norm_g': 4.859,
     'conv_b_2': 4.152,
     'ssm_norm_2': 2.849,
     'norm_ffn_2': 3.151,
     'final_norm_2': 2.86}
    for name, (base, spread) in spreads.items():
        noise = np.random.default_rng([zlib.crc32(name.encode()), seed]).standard_normal(out[name].shape)
        drawn = base * np.exp(spread * noise) if base else spread * noise
        out[name] = __import__('jax').numpy.asarray(drawn.astype(out[name].dtype))
    for name, factor in factors.items():
        out[name] = (out[name] * factor).astype(out[name].dtype)
    return out
```

```python
import math
from contextlib import ExitStack

import numpy as np
import concourse.bass as bass
from concourse import mybir

F32 = mybir.dt.float32
F32R = mybir.dt.float32r
BF16 = mybir.dt.bfloat16
I32 = mybir.dt.int32
ALU = mybir.AluOpType
ACT = mybir.ActivationFunctionType
AXX = mybir.AxisListType.X

S, D, P = 256, 1024, 128
M = S // P
KD = D // P
HD = 64
NEG = -1e30
EPS = 1e-5
SCALE = HD ** -0.5
FF = 2816
KF = FF // P
UPW = 256
NUP = FF // UPW
SSM = 1024
CONV = SSM + 512
NST = 128
SH = 16
NCT = CONV // P
RAW, SPLIT = 3, 3
SETUP_AT = 13
AHEAD = 2
CH = 8 * 272
NSCR = 4
QC = 3 * P

C_ID, C_U, C_CT = 0, P, 2 * P
C_COS, C_SIN, C_INV = C_CT + QC, C_CT + QC + 2 * HD, C_CT + QC + 4 * HD
C_KEEP = C_INV + 8
C_MASK = C_KEEP
C_ALL = C_MASK + 3 * QC + P


def constants():
    t, u = np.arange(P)[:, None], np.arange(P)[None, :]
    tiles = ((0, 0), (1, 0), (1, 1))
    delta = [t + P * q - u - P * k for q, k in tiles]
    c = np.zeros((P, C_ALL), np.float32)
    c[:, C_ID:C_ID + P] = np.eye(P)
    c[:, C_U:C_U + P] = t <= u
    mult = [(d >= 0) * ((d <= 128).astype(np.float32) + (d % 4 == 0) + (d % 16 == 0)) for d in delta]
    for i, x in enumerate(mult):
        c[:, C_CT + i * P:C_CT + (i + 1) * P] = x.T
    inv = np.float32(10000.0) ** (-np.arange(0, HD, 2, dtype=np.float32) / np.float32(HD))
    for m in range(M):
        ang = (np.arange(P, dtype=np.float32) + P * m)[:, None] * inv[None, :]
        cos, sin = np.cos(ang), np.sin(ang)
        c[:, C_COS + m * HD:C_COS + (m + 1) * HD] = np.concatenate([cos, cos], 1)
        c[:, C_SIN + m * HD:C_SIN + (m + 1) * HD] = np.concatenate([-sin, sin], 1)
    c[:, C_INV:C_INV + 8] = np.float32(500000.0) ** (-np.arange(0, 16, 2, dtype=np.float32) / np.float32(16))
    seen = (
        [(d >= 0) & (d < 128) for d in delta],
        [d >= 0 for d in delta],
        [x > 0 for x in mult],
    )
    for n, per in enumerate(seen):
        for i, x in enumerate(per):
            at = C_MASK + n * QC + i * P
            c[:, at:at + P] = np.where(x, 0.0, NEG)
    c[:, C_MASK + 3 * QC:] = np.where(t > u, NEG, 0.0)
    return c


class Step:

    def __init__(self, kind, i, *, loads=None, outs=None, needs=None, first=None, last=None, size=None,
                 buf=None, before=None, src=None, dst=None, k0=None, m=None, n=None, u=None, g=None, j=None,
                 t=None, q=None, bank=None, banks=None, obank=None, block=None, gain=None, added=None,
                 of=None, what=None, rstd=None, att=None, head=None, pair=None, half=None, p=None, pv=None,
                 oev=None, den=None, es=None, z=None, nkv=None, dt=None, kind_of=None, ev=None, rope=None,
                 layer=None, conv=None, soft=None, sums=None, xback=None, bback=None, state=None,
                 decay=None, mg=None):
        self.kind, self.i = kind, i
        self.loads, self.outs, self.needs, self.size = loads, outs, needs, size
        self.first, self.last = first, last
        self.buf, self.before, self.src, self.dst, self.k0 = buf, before, src, dst, k0
        self.bank, self.banks, self.obank, self.block = bank, banks, obank, block
        self.m, self.n, self.u, self.g, self.j, self.t, self.q, self.mg = m, n, u, g, j, t, q, mg
        self.gain, self.added, self.of, self.what, self.rstd = gain, added, of, what, rstd
        self.att, self.head, self.pair, self.half, self.p, self.pv = att, head, pair, half, p, pv
        self.oev, self.den, self.es, self.z = oev, den, es, z
        self.nkv, self.dt, self.kind_of, self.ev, self.rope = nkv, dt, kind_of, ev, rope
        self.layer, self.conv, self.soft, self.sums = layer, conv, soft, sums
        self.xback, self.bback, self.state, self.decay = xback, bback, state, decay


class Bank:

    def __init__(self, at, before):
        self.at, self.before, self.freed = at, before, None


class Schedule:

    def __init__(self):
        self.steps, self.count, self.blocks, self.banks = [], {}, [], []
        self.parts, self.quarters, self.gains = 0, [], []

    def step(self, kind, **of):
        s = Step(kind, self.count.get(kind, 0), **of)
        self.count[kind] = s.i + 1
        self.steps.append(s)
        return s

    def bank(self):
        n = len(self.banks)
        b = Bank(n % NSCR, self.banks[n - NSCR] if n >= NSCR else None)
        assert b.before is None or b.before.freed is not None, "a bank is taken before it is freed"
        self.banks.append(b)
        return b

    def block(self, width):
        g = len(self.blocks)
        b = {"pair": g % 2, "width": width, "before": self.blocks[g - 2] if g >= 2 else None,
             "evac": [None, None], "ready": [None, None]}
        self.blocks.append(b)
        return b

    def chunk(self, loads, outs, needs, first, last):
        s = self.step("chunk", loads=loads, outs=outs, needs=needs, first=first, last=last,
                      size=sum(x[0] for x in loads))
        if last:
            order = [(b, m) for b, _, _ in outs for m in range(M)]
            for b, m in order[:-1]:
                self.parts += 1
                b["ready"][m] = ("part", self.parts)
            b, m = order[-1]
            b["ready"][m] = ("chunk_tensor", s.i + 1)
        return s

    def quarter(self, kind, **of):
        n = len(self.quarters)
        s = self.step(kind, buf=n % 2, before=self.quarters[n - 2] if n >= 2 else None, **of)
        self.quarters.append(None)
        return s

    def turn(self, src, dst, k0, m):
        b = self.bank()
        s = self.step("turn", src=src, dst=dst, k0=k0, m=m, bank=b)
        b.freed = (s, "vector")
        self.quarters[self.quarters.index(None)] = s
        return s

    def gain(self, src):
        g = {"src": src, "i": len(self.gains), "users": []}
        self.gains.append(g)
        return g


def attention(sc, n, h0):
    a = sc.att
    if n < a["heads"]:
        b = sc.bank()
        s = sc.step("scores", head=n, att=a, bank=b, p=a["base"] + n)
        b.freed = (s, "scalar")
        a["scores"].append(s)
    if 1 <= n <= a["heads"]:
        b = sc.bank()
        s = sc.step("flip", head=n - 1, att=a, bank=b, p=a["base"] + n - 1)
        b.freed = (s, "vector")
        a["flip"].append(s)
    if 2 <= n <= a["heads"] + 1:
        head = n - 2
        if head % 2 == 0:
            a["obank"] = sc.bank()
        s = sc.step("pv", head=head, att=a, bank=a["obank"], p=a["base"] + head)
        a["pv"].append(s)
        if head % 2 == 1:
            o = sc.step("oev", att=a, pair=head // 2, bank=a["obank"], pv=s)
            a["obank"].freed = (o, "scalar")
            a["oev"].append(o)


def add(sc, block, n, m):
    block["evac"][m] = sc.added[n, m] = sc.step("added", n=n, m=m, block=block)


def times_gain(sc, gain, n, m):
    s = sc.quarter("gained", n=n, m=m, gain=gain, added=sc.added.get((n, m)))
    gain["users"].append(s)
    return s


def turn_x(sc, s):
    sc.turned[s.n, s.m] = sc.turn(s, "x", 4 * s.n, s.m)


def turn_norm(sc, gain, filled):
    for m in range(M):
        turn_x(sc, filled[m])
        filled.append(times_gain(sc, gain, 1, m))
    for m in range(M):
        turn_x(sc, filled[M + m])


def statistics(sc):
    for n in range(2):
        for m in range(M):
            sc.step("square", n=n, m=m, added=sc.added.get((n, m)))
    a = sc.step("meansq", what="h", of=sc.count["square"])
    sc.rstd = sc.step("newton", what="h", before=a)


def project_chunk(sc, w, cols, ks, block, first, last):
    src = [(len(ks) * cw, ("k", len(ks), cw), (w, c0, cw, ks)) for c0, cw in cols]
    width = sum(cw for _, cw in cols)
    outs = [(block, width, [("x", k, i * width) for i, k in enumerate(ks)])]
    need = [sc.turned[k // 4, m] for k in ks for m in range(M) if k % 4 == 0]
    return sc.chunk(src, outs, need, first, last)


def normed_residual(sc, gain):
    for m in range(M):
        s = sc.step("final", m=m, gain=gain, rstd=sc.rstd)
        gain["users"].append(s)
        for n in range(2):
            sc.added[n, m] = s


def out_product(sc, w, kt, turned, gain, mid=None):
    for n in range(2):
        b = sc.block(512)
        for k0 in range(0, kt, 4):
            ks = list(range(k0, k0 + 4))
            need = [turned[k0 // 4, m] for m in range(M)]
            sc.chunk([(4 * 512, ("k", 4, 512), (w, n * 512, 512, ks))],
                     [(b, 512, [("o", k, i * 512) for i, k in enumerate(ks)])],
                     need, k0 == 0, k0 + 4 == kt)
            if n == 1 and k0 == 0 and not mid:
                for s in filled:
                    turn_x(sc, s)
        for m in range(M):
            add(sc, b, n, m)
        if not mid:
            filled = [times_gain(sc, gain, n, m) for m in range(M)]
    if mid:
        statistics(sc)
        normed_residual(sc, mid)
        turn_norm(sc, gain, [times_gain(sc, gain, 0, m) for m in range(M)])
    else:
        for s in filled:
            turn_x(sc, s)
    statistics(sc)


def mixer_ab(sc, which, w_in, w_out, gain_next, nkv, kv_chunks, mid=None):
    kvw = nkv * HD
    a = sc.att = {"kind": which, "heads": 16, "nkv": nkv, "scores": [], "flip": [], "pv": [], "oev": [],
                  "base": sc.heads, "tk": [], "tq": [], "gates": {}}
    sc.heads += 16
    b = sc.block(2 * kvw)
    per = KD // kv_chunks
    for c in range(kv_chunks):
        project_chunk(sc, w_in, [(D, 2 * kvw)], list(range(c * per, (c + 1) * per)), b, c == 0, c == kv_chunks - 1)
    for m in range(M):
        b["evac"][m] = sc.step("ev_kv", m=m, block=b, nkv=nkv, rstd=sc.rstd, dt=None)
    kr = sc.step("rope_k", nkv=nkv, kind_of=which, ev=b["evac"][1])
    for j in range(2):
        b = sc.block(512)
        project_chunk(sc, w_in, [(j * 512, 512)], [0, 1, 2, 3], b, True, False)
        if j == 0:
            for t in range(nkv // 2):
                bk = sc.bank()
                s = sc.step("turn_k", t=t, rope=kr, bank=bk)
                bk.freed = (s, "scalar")
                a["tk"].append(s)
        else:
            turn_q(sc, a, 0, rq)
            attention(sc, 0, 0)
            attention(sc, 1, 0)
        project_chunk(sc, w_in, [(j * 512, 512)], [4, 5, 6, 7], b, False, True)
        for m in range(M):
            b["evac"][m] = sc.step("ev_q", j=j, m=m, block=b, kind_of=which)
        rq = sc.step("rope_q", j=j, kind_of=which, ev=b["evac"][1])
        if j == 1:
            attention(sc, 2, 0)
    done = 3
    zs = []
    for j in range(2):
        b = sc.block(512)
        for half in range(2):
            project_chunk(sc, w_in, [(D + 2 * kvw + j * 512, 512)], list(range(4 * half, 4 * half + 4)), b,
                          half == 0, half == 1)
            if half == 1:
                for m in range(M):
                    b["evac"][m] = sc.step("ev_z", j=j, m=m, block=b, kind_of=which)
                zs.append(b["evac"][1])
            for _ in range(4):
                if done <= 17:
                    attention(sc, done, 0)
                    done += 1
                if done == 4:
                    turn_q(sc, a, 1, rq)
                if done == 10:
                    gates(sc, a, 0, zs[0])
    while done <= 17:
        attention(sc, done, 0)
        done += 1
    gates(sc, a, 1, zs[1])
    out_product(sc, w_out, KD, sc.oturned, gain_next, mid)


def turn_q(sc, a, j, rq):
    for t in range(2):
        bk = sc.bank()
        s = sc.step("turn_q", j=j, t=t, rope=rq, bank=bk)
        bk.freed = (s, "scalar")
        a["tq"].append(s)


def gates(sc, a, half, z):
    es = sc.step("sink", att=a, half=half) if a["kind"] == "a" else None
    den = sc.step("den", att=a, half=half, es=es, oev=a["oev"][4 * half + 3])
    a["gates"][half] = den
    filled = [sc.quarter("gate", att=a, half=half, m=m, z=z, den=den) for m in range(M)]
    for m in range(M):
        sc.oturned[half, m] = sc.turn(filled[m], "o", 4 * half, m)


def hybrid(sc, layer, w, gains):
    a = sc.att = {"kind": "h", "heads": 8, "nkv": 2, "scores": [], "flip": [], "pv": [], "oev": [],
                  "base": sc.heads, "tk": [], "tq": [], "gates": {}}
    sc.heads += 8
    w_in, q0, kv0, z0, x0, dt0 = w["in"], 0, 512, 768, 1792, 3328

    def att(*ns):
        for n in ns:
            attention(sc, n, 0)

    def two(col, first=None, second=None):
        b = sc.block(512)
        project_chunk(sc, w_in, [(col, 512)], [0, 1, 2, 3], b, True, False)
        if first:
            first()
        project_chunk(sc, w_in, [(col, 512)], [4, 5, 6, 7], b, False, True)
        return b

    b = sc.block(272)
    project_chunk(sc, w_in, [(kv0, 256), (dt0, 16)], list(range(8)), b, True, True)
    for m in range(M):
        b["evac"][m] = sc.step("ev_kv", m=m, block=b, nkv=2, rstd=sc.rstd, dt=layer)
    kr = sc.step("rope_k", nkv=2, kind_of="h", ev=b["evac"][1])
    sp = sc.step("soft1", layer=layer, ev=b["evac"][1])
    scan = {}

    def early():
        bk = sc.bank()
        s = sc.step("turn_k", t=0, rope=kr, bank=bk)
        bk.freed = (s, "scalar")
        a["tk"].append(s)
        scan["soft2"] = sc.step("soft2", before=sp)
        scan["soft3"] = sc.step("soft3", before=scan["soft2"], layer=layer)

    b = two(q0, early)
    for m in range(M):
        b["evac"][m] = sc.step("ev_q", j=0, m=m, block=b, kind_of="h")
    rq = sc.step("rope_q", j=0, kind_of="h", ev=b["evac"][1])
    bk = sc.bank()
    scan["sums"] = sc.step("sums", bank=bk, before=scan["soft3"])
    bk.freed = (scan["sums"], "vector")

    def conv_blocks(j):
        b1, b2 = sc.bank(), sc.bank()
        s = sc.step("conv", j=j, banks=(b1, b2), layer=layer, ev=scan["ev", j])
        b1.freed = b2.freed = (s, "vector")
        scan["conv", j] = s

    def evac_x(b, j):
        for m in range(M):
            b["evac"][m] = sc.step("ev_x", j=j, m=m, block=b, rstd=sc.rstd,
                                   conv=scan["conv", j - 1] if j else None)
        scan["ev", j] = b["evac"][1]

    def back(j):
        b1, b2 = sc.bank(), sc.bank()
        s = sc.step("xback", j=j, banks=(b1, b2), conv=scan["conv", j + 1], soft=scan["soft3"],
                    sums=scan["sums"])
        b1.freed = b2.freed = (s, "scalar")
        scan["xback", j] = s

    def decay(q):
        bk = sc.bank()
        s = sc.step("decay", q=q, bank=bk, sums=scan["sums"], bback=scan["bback"],
                    last=scan["xback", 1])
        bk.freed = (s, "scalar")
        scan["decay", q] = s

    b = two(x0 + SSM, lambda: (turn_q(sc, a, 0, rq), att(0, 1)))
    evac_x(b, 0)
    att(2, 3)
    b = two(x0, lambda: conv_blocks(0))
    evac_x(b, 1)
    att(4, 5)
    b1, b2 = sc.bank(), sc.bank()
    s = sc.step("bback", banks=(b1, b2), conv=scan["conv", 0])
    b1.freed = b2.freed = (s, "scalar")
    scan["bback"] = s
    b = two(x0 + 512, lambda: (conv_blocks(1), back(0)))
    evac_x(b, 2)
    att(6, 7)
    b = two(z0, lambda: (conv_blocks(2), back(1)))
    for m in range(M):
        b["evac"][m] = sc.step("ev_z", j=0, m=m, block=b, kind_of="h")
    zs = [b["evac"][1]]
    att(8, 9)
    decay(0)

    def states():
        for g in range(2):
            bk = sc.bank()
            s = sc.step("state", g=g, bank=bk, xback=scan["xback", 1], bback=scan["bback"])
            bk.freed = (s, "scalar")
            scan["state", g] = s
        decay(1)
        den = sc.step("den", att=a, half=0, es=None, oev=a["oev"][3])
        filled = [sc.quarter("gate", att=a, half=0, m=m, z=None, den=den) for m in range(M)]
        for m in range(M):
            sc.oturned[0, m] = sc.turn(filled[m], "o", 0, m)

    b = two(z0 + 512, states)
    for m in range(M):
        b["evac"][m] = sc.step("ev_z", j=1, m=m, block=b, kind_of="h")
    zs.append(b["evac"][1])

    order = [(m, g) for g in range(2) for m in range(M)]
    def redecay(n):
        if n < 8 and ("decay", n) not in scan:
            decay(n)

    ys = []
    for n, (m, g) in enumerate(order):
        redecay(2 * n + 1)
        redecay(2 * n + 2)
        yb = sc.bank()
        for i in range(2):
            d = scan["decay", 2 * n + i]
            sc.step("diag", q=2 * n + i, m=m, g=g, bank=yb, decay=d, xback=scan["xback", g])
        last = sc.steps[-1]
        ob = None
        if m == 1:
            ob = sc.bank()
            last = sc.step("off", g=g, bank=ob, state=scan["state", g])
        y = sc.step("join", m=m, g=g, bank=yb, obank=ob, last=last, z=zs[g], xback=scan["xback", g])
        yb.freed = (y, "vector")
        if ob:
            ob.freed = (y, "vector")
        ys.append(y)
    for d in range(8):
        scan["decay", d].mg = order[d // 2]
    ra = sc.step("meansq", what="y", of=sc.count["join"])
    rb = sc.step("newton", what="y", before=ra)
    filled = []
    for n in range(6):
        if n < 4:
            g, m = divmod(n, 2)
            filled.append(sc.quarter("ynorm", m=m, g=g, rstd=rb, gain=gains[0]))
            gains[0]["users"].append(filled[-1])
        if n >= 1 and n <= 4:
            f = filled[n - 1]
            sc.oturned[1 + f.g, f.m] = sc.turn(f, "o", 4 + 4 * f.g, f.m)
    out_product(sc, w["out"], 12, sc.oturned, gains[1])

    pend = None
    hturn = []
    for u in range(NUP):
        b = sc.block(2 * UPW)
        for half in range(2):
            ks = list(range(4 * half, 4 * half + 4))
            sc.chunk([(4 * UPW, ("i", 0, 2), (w["gate"], u * UPW, UPW, ks)),
                      (4 * UPW, ("i", 1, 2), (w["up"], u * UPW, UPW, ks))],
                     [(b, 2 * UPW, [("x", k, i * 2 * UPW) for i, k in enumerate(ks)])],
                     [sc.turned[half, m] for m in range(M)], half == 0, half == 1)
            if half == 0 and pend is not None:
                hturn.append(sc.turn(pend, "h", 2 * pend.u, 0))
                pend = None
        pend = sc.quarter("ev_up", u=u, block=b, rstd=sc.rstd)
        b["evac"] = [pend, pend]
    b0, b1 = sc.block(512), sc.block(512)
    for j in range(KF // 2):
        if j == 1:
            hturn.append(sc.turn(pend, "h", 2 * pend.u, 0))
        sc.chunk([(2 * D, ("k", 2, D), (w["down"], 0, D, [2 * j, 2 * j + 1]))],
                 [(b, 512, [("h", 2 * j + i, i * D + n * 512) for i in range(2)]) for n, b in enumerate((b0, b1))],
                 [hturn[j]], j == 0, j == KF // 2 - 1)
    filled = []
    for m in range(M):
        add(sc, b0, 0, m)
        if gains[2] is not None:
            filled.append(times_gain(sc, gains[2], 0, m))
    for m in range(M):
        add(sc, b1, 1, m)
    if gains[2] is not None:
        turn_norm(sc, gains[2], filled)
    statistics(sc)


def build_schedule(w):
    sc = Schedule()
    sc.heads, sc.turned, sc.oturned = 0, {}, {}
    ga, gb = sc.gain(("norm_g", 0)), sc.gain(("norm_g", 1))
    sc.added = {}
    turn_norm(sc, ga, [times_gain(sc, ga, 0, m) for m in range(M)])
    statistics(sc)
    gmid = sc.gain(("final_g", 0))
    gh = []
    for layer in range(2):
        gh.append([sc.gain(("norm_mix", layer)), sc.gain(("ssm_norm", layer)), sc.gain(("norm_ffn", layer))])
    gfin = sc.gain(("final", 0))
    mixer_ab(sc, "a", w["in_a"], w["out0"], gb, 2, 1)
    mixer_ab(sc, "b", w["in_b"], w["out1"], gh[0][0], 4, 2, gmid)
    hybrid(sc, 0, w["h"][0], [gh[0][1], gh[0][2], gh[1][0]])
    hybrid(sc, 1, w["h"][1], [gh[1][1], gh[1][2], None])
    normed_residual(sc, gfin)
    return sc


PARTS = {
    "chunk": ("tensor", "scalar", "vector"), "gained": ("vector",), "turn": ("tensor", "scalar", "vector"),
    "square": ("scalar",), "meansq": ("vector", "scalar"), "newton": ("vector",), "added": ("vector",),
    "ev_kv": ("scalar",), "ev_q": ("scalar",), "ev_z": ("scalar",), "ev_x": ("scalar",),
    "ev_up": ("scalar", "vector"), "rope_k": ("vector",), "rope_q": ("vector",),
    "turn_k": ("tensor", "scalar"), "turn_q": ("tensor", "scalar"),
    "scores": ("tensor", "vector", "scalar"), "flip": ("tensor", "vector"), "pv": ("tensor",),
    "oev": ("scalar",), "sink": ("vector", "scalar"), "den": ("vector",), "gate": ("vector",),
    "soft1": ("vector", "scalar"), "soft2": ("vector", "scalar"), "soft3": ("vector",),
    "sums": ("tensor", "vector", "scalar"), "conv": ("tensor", "vector", "scalar"),
    "bback": ("tensor", "scalar"), "xback": ("tensor", "scalar", "gpsimd"), "state": ("tensor", "scalar"),
    "decay": ("tensor", "scalar", "vector"), "diag": ("tensor",), "off": ("tensor",),
    "join": ("vector", "scalar"), "ynorm": ("vector",), "final": ("vector",),
}


def build(nc, t):
    def w3(ap):
        return ap.rearrange("(k p) n -> p k n", p=P)

    w = {"in_a": w3(t["w_in_a"][0]), "in_b": w3(t["w_in_b"][0]), "out0": w3(t["w_out"][0]), "out1": w3(t["w_out"][1]),
         "h": [{"in": w3(t["w_in_2"][i]), "out": w3(t["w_out_2"][i]), "gate": w3(t["w_gate_2"][i]),
                "up": w3(t["w_up_2"][i]), "down": w3(t["w_down_2"][i])} for i in range(2)]}
    sc = build_schedule(w)
    chunks = [s for s in sc.steps if s.kind == "chunk"]
    gain_rows = {"norm_g": t["norm_g"], "norm_mix": t["norm_mix_2"], "ssm_norm": t["ssm_norm_2"],
                 "norm_ffn": t["norm_ffn_2"]}

    place = [16512]

    def at(name, shape, dt, where=None):
        size = math.prod(shape[1:]) * (2 if dt == BF16 else 4)
        size = -(-size // 32) * 32
        if where is None:
            where = place[0]
            place[0] += size
        else:
            at.end = max(at.end, where + size)
        return nc.alloc_sbuf_tensor_at(name, shape, dt, offset=where), where + size

    def keep(name, shape, dt=F32):
        return at(name, shape, dt)[0]

    at.end = 0
    h = keep("h", [P, M, D])
    xT = [keep("xT_hi", [P, KD, S], F32R), keep("xT_lo", [P, KD, S], F32R)]
    oT = [keep("oT_hi", [P, 12, S], F32R), keep("oT_lo", [P, 12, S], F32R)]
    raw = [keep(f"raw{i}", [P, CH]) for i in range(RAW)]
    hi = [keep(f"hi{i}", [P, CH], F32R) for i in range(SPLIT)]
    lo = [keep(f"lo{i}", [P, CH], F32R) for i in range(SPLIT)]
    quarter = [keep(f"quarter{i}", [P, 512]) for i in range(2)]
    gains = keep("gains", [P, D])
    cst = keep("cst", [P, C_KEEP])
    masks = keep("masks", [P, 3 * QC + P], BF16)
    identb = keep("identb", [P, P], BF16)
    ones = keep("ones", [P, P])
    junk = keep("junk", [P, 512], BF16)
    sumsq = keep("sumsq", [P, 4])
    rms = keep("rms", [P, 2, M])
    rmy = keep("rmy", [P, 3, 4])
    newt = keep("newt", [P, 4])
    posi = keep("posi", [P, M], I32)
    posf = keep("posf", [P, M])
    trig = keep("trig", [P, M, 2, 16])
    sinks = keep("sinks", [P, 2, 16])
    small = keep("small", [P, 2, 3, 16])
    convw = keep("convw", [P, 2, 4, NCT])
    convb = keep("convb", [P, 2, NCT])
    rowmax = keep("rowmax", [P, 2, 4])
    shift = keep("shift", [P, 16, M])
    esink = keep("esink", [P, 16, M])
    dens = keep("dens", [P, M, 8])
    ident, upper = cst[:, C_ID:C_ID + P], cst[:, C_U:C_U + P]
    mult = cst[:, C_CT:C_CT + QC]

    base = place[0]
    hT = []
    end = base
    for i in range(2):
        x, end = at(f"hT{i}", [P, KF, S], F32R, end)
        hT.append(x)
    sil = []
    for i in range(2):
        x, end = at(f"silu_gate{i}", [P, M, UPW], F32, end)
        sil.append(x)

    def plan(tag, hybrid_):
        b = {}
        p = [base]

        def put(name, shape, dt=F32, where=None):
            x, e = at(f"{tag}_{name}", shape, dt, p[0] if where is None else where)
            b[name + "_at"] = (p[0] if where is None else where)
            if where is None:
                p[0] = e
            b[name] = x
            return e

        nkv, heads = (2, 8) if hybrid_ else (4, 16)
        put("v1", [P, M, nkv, HD + 1])
        put("kT", [P, nkv, S])
        put("qT", [P, heads // 2, S])
        put("prob0", [P, QC])
        put("prob1", [P, QC])
        put("probT0", [P, QC])
        put("probT1", [P, QC])
        put("z", [P, M, D])
        e = put("k", [P, M, nkv, HD])
        e = put("kdup", [P, M, nkv, 2, HD])
        put("rot1", [P, 512])
        e = put("rot2", [P, 512])
        put("o", [P, M, heads, HD + 1], where=b["k_at"])
        e = b["k_at"] + 4 * M * heads * (HD + 1)
        p[0] = max(p[0], -(-e // 32) * 32)
        q_at = p[0]
        put("q", [P, M, heads * HD])
        if hybrid_:
            e = put("cb", [P, M, 2, P], where=q_at)
            put("bt", [P, 2, P], where=e)
            put("xin", [P, M, 512])
            put("st", [P, SSM], where=b["xin_at"])
            put("cT", [P, NCT, S])
            e = b["cT_at"]
            for i in range(2):
                e = put(f"E{i}", [P, 4, P], where=e)
            for i in range(2):
                e = put(f"MT{i}", [P, 4, P], where=e)
            put("acc", [P, 4, S], where=b["z_at"])
            put("xgd", [P, SSM], where=b["kT_at"])
            put("xs", [P, M, SSM])
            put("xg", [P, M, SSM])
            for name in ("dtr", "dt", "da", "sa", "sb", "sc", "sd"):
                put(name, [P, M, SH])
            put("ncs", [P, M, SH])
            put("dif", [P, SH])
            put("dec", [P, SH])
            put("ecs", [P, SH])
        return b

    A, Hb = plan("attn", False), plan("hyb", True)
    stage, _ = at("mask_stage", [P, C_ALL - C_KEEP], F32, base)
    angle, e = at("trig_stage", [P, M, 2, 8], F32, base + 8192)
    sine, e = at("trig_stage2", [P, M, 2, 8], F32, e)
    turns, _ = at("trig_stage3", [P, M, 2, 8], F32, e)
    outb = [quarter[0], quarter[1]]
    assert max(place[0], at.end) <= 229344, (place[0], at.end)

    psum = [nc.alloc_psum_tensor(f"bank{i}", [P, 512], F32) for i in range(8)]

    sem = {}
    for kind, who in PARTS.items():
        for e in who:
            sem[kind, e] = nc.alloc_semaphore(f"{kind}_{e}")
    raw_in = [nc.alloc_semaphore(f"raw_in{i}") for i in range(RAW)]
    part_done = nc.alloc_semaphore("part_done")
    x_in = nc.alloc_semaphore("x_in")
    const_in = nc.alloc_semaphore("const_in")
    masks_in = nc.alloc_semaphore("masks_in")
    sinks_in = nc.alloc_semaphore("sinks_in")
    small_in = nc.alloc_semaphore("small_in")
    gain_in = nc.alloc_semaphore("gain_in")
    setup_dve = nc.alloc_semaphore("setup_vector")
    setup_act = nc.alloc_semaphore("setup_scalar")
    out_done = nc.alloc_semaphore("out_done")
    chain = {e: nc.alloc_semaphore(f"chain_{e}") for e in ("vector", "scalar", "gpsimd")}
    links = {"vector": 0, "scalar": 0, "gpsimd": 0}

    def ended(eng, step, who):
        eng.wait_ge(sem[step.kind, who], step.i + 1)

    def freed(eng, bank):
        if bank.before is not None:
            ended(eng, bank.before.freed[0], bank.before.freed[1])
        return psum[4 + bank.at]

    def ready(eng, block, m):
        name, v = block["ready"][m]
        eng.wait_ge(part_done if name == "part" else sem["chunk", "tensor"], v)
        return psum[2 * block["pair"] + m]

    def link(eng, who, ins):
        links[who] += 1
        ins.then_inc(chain[who], 1)
        eng.wait_ge(chain[who], links[who])

    def spread(ap, shape):
        return ap.broadcast_to(shape)

    arrived, total = {}, [0] * RAW
    for c in chunks:
        total[c.i % RAW] += 16 * len(c.loads)
        arrived[c.i] = total[c.i % RAW]

    NSMALL = 1 + 2 * (3 + 4 + 1)
    program = ExitStack()
    blk = program.enter_context(nc.Block())

    @blk.sync
    def _(sp):
        with nc.allow_non_contiguous_dma("small rows and weights by columns"):
            sp.dma_start(h[:, :, :], t["x"][0].rearrange("(m p) d -> p m d", p=P)).then_inc(x_in, 16)
            sp.dma_start(cst[:, :], t["cst"][:, 0:C_KEEP]).then_inc(const_in, 16)

            def load(c):
                slot = raw[c.i % RAW]
                if c.i >= RAW:
                    sp.wait_ge(sem["chunk", "vector"], c.i - RAW + 1)
                off = 0
                for n, (size, how, (wt, c0, cw, ks)) in enumerate(c.loads):
                    src = wt[:, ks[0]:ks[-1] + 1, c0:c0 + cw]
                    if len(c.loads) == 1:
                        dst = slot[:, 0:size].rearrange("p (k n) -> p k n", n=cw)
                    else:
                        full = c.size // len(ks)
                        dst = slot[:, 0:c.size].rearrange("p (k n) -> p k n", n=full)[:, :, off:off + cw]
                        off += cw
                    sp.dma_start(dst, src).then_inc(raw_in[c.i % RAW], 16)

            load(chunks[0])
            load(chunks[1])
            sp.dma_start(stage[:, :], t["cst"][:, C_KEEP:C_ALL]).then_inc(masks_in, 16)
            sp.dma_start(posi[:, :], t["positions_2"][0].rearrange("(m p) -> p m", p=P)).then_inc(small_in, 16)
            sp.dma_start(sinks[:, 0, :], t["sinks_a"][0].partition_broadcast(P)).then_inc(sinks_in, 16)
            load(chunks[2])
            for i in range(2):
                for n, name in enumerate(("dt_bias_2", "a_log_2", "d_skip_2")):
                    sp.dma_start(small[:, i, n, :], t[name][i].partition_broadcast(P)).then_inc(small_in, 16)
                for tap in range(4):
                    sp.dma_start(convw[:, i, tap, :], t["conv_w_2"][i, tap].rearrange("(c p) -> p c", p=P))\
                      .then_inc(small_in, 16)
                sp.dma_start(convb[:, i, :], t["conv_b_2"][i].rearrange("(c p) -> p c", p=P)).then_inc(small_in, 16)
            for s in sc.steps:
                if s.kind == "chunk" and s.i + RAW < len(chunks):
                    load(chunks[s.i + RAW])
            for i in range(M):
                sp.wait_ge(sem["final", "vector"], M + i + 1)
                sp.dma_start(t["out"][0, i * P:(i + 1) * P, :], h[:, i, :]).then_inc(out_done, 16)
            sp.wait_ge(out_done, 16 * M)

    @blk.tensor
    def _(pe):
        def transpose(out, in_):
            return nc.tensor.transpose(out, in_, ident)

        pe.wait_ge(const_in, 16)
        for s in sc.steps:
            if s.kind == "chunk":
                for x in s.needs:
                    ended(pe, x, "vector")
                pe.wait_ge(sem["chunk", "vector"], s.i + 1)
                if s.first:
                    for b, _, _ in s.outs:
                        if b["before"]:
                            for e in b["before"]["evac"]:
                                ended(pe, e, "vector" if e.kind in ("added", "ev_up") else "scalar")
                src = {"x": xT, "o": oT, "h": hT}
                r = s.i % SPLIT
                outs = [(b, wd, ts, m) for b, wd, ts in s.outs for m in range(M)]
                for n, (b, wd, ts, m) in enumerate(outs):
                    bank = psum[2 * b["pair"] + m]
                    for i, (name, k, off) in enumerate(ts):
                        still = [x[:, k, m * P:(m + 1) * P] for x in src[name]]
                        for j, (a, mv) in enumerate(((0, hi), (0, lo), (1, hi))):
                            last = nc.tensor.matmul(
                                bank[:, 0:wd], still[a], mv[r][:, off:off + wd],
                                start=s.first and i == 0 and j == 0,
                                stop=s.last and i == len(ts) - 1 and j == 2)
                    if s.last and n < len(outs) - 1:
                        last.then_inc(part_done, 1)
                last.then_inc(sem["chunk", "tensor"], 1)
            elif s.kind == "turn":
                ended(pe, s.src, "vector")
                bank = freed(pe, s.bank)
                q = quarter[s.src.buf]
                for i in range(4):
                    j = (i % 2) * 2 + i // 2 if s.dst == "h" else i
                    last = transpose(bank[:, i * P:(i + 1) * P], q[:, j * P:(j + 1) * P])
                last.then_inc(sem["turn", "tensor"], 1)
            elif s.kind == "turn_k":
                B = A if s.rope.kind_of != "h" else Hb
                ended(pe, s.rope, "vector")
                bank = freed(pe, s.bank)
                for g in range(2):
                    for m in range(M):
                        kd = B["kdup"][:, m, 2 * s.t + g, :, :].rearrange("p a d -> p (a d)")
                        last = transpose(bank[:, (2 * g + m) * P:(2 * g + m + 1) * P], kd)
                last.then_inc(sem["turn_k", "tensor"], 1)
            elif s.kind == "turn_q":
                B = A if s.rope.kind_of != "h" else Hb
                ended(pe, s.rope, "vector")
                bank = freed(pe, s.bank)
                for g in range(2):
                    for m in range(M):
                        c0 = s.j * 512 + (2 * s.t + g) * P
                        last = transpose(bank[:, (2 * g + m) * P:(2 * g + m + 1) * P], B["q"][:, m, c0:c0 + P])
                last.then_inc(sem["turn_q", "tensor"], 1)
            elif s.kind == "scores":
                a, hd = s.att, s.head
                B = Hb if a["kind"] == "h" else A
                kv = hd // (a["heads"] // a["nkv"])
                ended(pe, a["tk"][-1], "scalar")
                ended(pe, a["tq"][hd // 4], "scalar")
                bank = freed(pe, s.bank)
                mk = {"a": 0, "b": 1, "h": 2}[a["kind"]]
                nc.tensor.matmul(bank[:, 0:QC], identb[:, :], masks[:, mk * QC:(mk + 1) * QC], start=True, stop=False)
                r = 64 * (hd % 2)
                q, k = B["qT"], B["kT"]
                nc.tensor.matmul(bank[:, 0:P], q[r:r + 64, hd // 2, 0:P], k[r:r + 64, kv, 0:P], start=False, stop=False)
                nc.tensor.matmul(bank[:, P:QC], q[r:r + 64, hd // 2, P:S], k[r:r + 64, kv, 0:S],
                                 start=False, stop=True).then_inc(sem["scores", "tensor"], 1)
            elif s.kind == "flip":
                a = s.att
                B = Hb if a["kind"] == "h" else A
                ended(pe, a["scores"][s.head], "scalar")
                bank = freed(pe, s.bank)
                pr = B[f"prob{s.p % 2}"]
                for i in range(3):
                    last = transpose(bank[:, i * P:(i + 1) * P], pr[:, i * P:(i + 1) * P])
                last.then_inc(sem["flip", "tensor"], 1)
            elif s.kind == "pv":
                a, hd = s.att, s.head
                B = Hb if a["kind"] == "h" else A
                kv = hd // (a["heads"] // a["nkv"])
                ended(pe, a["flip"][hd], "vector")
                bank = freed(pe, s.bank) if hd % 2 == 0 else psum[4 + s.bank.at]
                pt, v = B[f"probT{s.p % 2}"], B["v1"]
                W1 = HD + 1
                c0 = (hd % 2) * 2 * W1
                nc.tensor.matmul(bank[:, c0:c0 + W1], pt[:, 0:P], v[:, 0, kv, :], start=True, stop=True)
                nc.tensor.matmul(bank[:, c0 + W1:c0 + 2 * W1], pt[:, P:2 * P], v[:, 0, kv, :], start=True, stop=False)
                nc.tensor.matmul(bank[:, c0 + W1:c0 + 2 * W1], pt[:, 2 * P:QC], v[:, 1, kv, :],
                                 start=False, stop=True).then_inc(sem["pv", "tensor"], 1)
            elif s.kind == "sums":
                ended(pe, s.before, "vector")
                bank = freed(pe, s.bank)
                da = Hb["da"][:, :, :].rearrange("p m s -> p (m s)")
                nc.tensor.matmul(bank[:, 0:32], upper, da, start=True, stop=True)
                nc.tensor.matmul(bank[:, 32:64], ones[:, :], da, start=True, stop=True)\
                  .then_inc(sem["sums", "tensor"], 1)
            elif s.kind == "conv":
                ended(pe, s.ev, "scalar")
                for u in range(2):
                    bank = freed(pe, s.banks[u])
                    for i in range(2):
                        for m in range(M):
                            c0 = (2 * u + i) * P
                            last = transpose(bank[:, (2 * i + m) * P:(2 * i + m + 1) * P], Hb["xin"][:, m, c0:c0 + P])
                last.then_inc(sem["conv", "tensor"], 1)
            elif s.kind == "bback":
                ended(pe, s.conv, "scalar")
                ct = Hb["cT"]
                bank = freed(pe, s.banks[0])
                for m in range(M):
                    for g in range(2):
                        c0 = (2 * m + g) * P
                        nc.tensor.matmul(bank[:, c0:c0 + P], ct[:, 8 + g, m * P:(m + 1) * P],
                                         ct[:, 10 + g, m * P:(m + 1) * P], start=True, stop=True)
                bank = freed(pe, s.banks[1])
                for g in range(2):
                    last = transpose(bank[:, g * P:(g + 1) * P], ct[:, 8 + g, 0:P])
                last.then_inc(sem["bback", "tensor"], 1)
            elif s.kind == "xback":
                ended(pe, s.conv, "scalar")
                for m in range(M):
                    bank = freed(pe, s.banks[m])
                    for i in range(4):
                        last = transpose(bank[:, i * P:(i + 1) * P], Hb["cT"][:, 4 * s.j + i, m * P:(m + 1) * P])
                last.then_inc(sem["xback", "tensor"], 1)
            elif s.kind == "state":
                ended(pe, s.xback, "gpsimd")
                ended(pe, s.bback, "scalar")
                bank = freed(pe, s.bank)
                nc.tensor.matmul(bank[:, :], Hb["bt"][:, s.g, :], Hb["xgd"][:, s.g * 512:(s.g + 1) * 512],
                                 start=True, stop=True).then_inc(sem["state", "tensor"], 1)
            elif s.kind == "decay":
                m, g = s.mg
                ended(pe, s.sums, "scalar")
                bank = freed(pe, s.bank)
                for i in range(4):
                    hh = 8 * g + 4 * (s.q % 2) + i
                    seg = bank[:, i * P:(i + 1) * P]
                    nc.tensor.matmul(seg, identb[:, :], masks[:, 3 * QC:3 * QC + P], start=True, stop=False)
                    last = nc.tensor.matmul(seg, spread(Hb["da"][:, m, hh:hh + 1], [P, P]), upper,
                                            start=False, stop=True)
                last.then_inc(sem["decay", "tensor"], 1)
            elif s.kind == "diag":
                ended(pe, s.decay, "vector")
                ended(pe, s.xback, "gpsimd")
                bank = freed(pe, s.bank) if s.i % 2 == 0 else psum[4 + s.bank.at]
                for i in range(4):
                    hh = 8 * s.g + 4 * (s.q % 2) + i
                    c0 = (4 * (s.q % 2) + i) * HD
                    last = nc.tensor.matmul(bank[:, c0:c0 + HD], Hb[f"MT{s.decay.i % 2}"][:, i, :],
                                            Hb["xg"][:, s.m, hh * HD:(hh + 1) * HD], start=True, stop=True)
                last.then_inc(sem["diag", "tensor"], 1)
            elif s.kind == "off":
                ended(pe, s.state, "scalar")
                bank = freed(pe, s.bank)
                nc.tensor.matmul(bank[:, :], Hb["cT"][:, 10 + s.g, P:S], Hb["st"][:, s.g * 512:(s.g + 1) * 512],
                                 start=True, stop=True).then_inc(sem["off", "tensor"], 1)

    @blk.scalar
    def _(act):
        def split(c):
            act.wait_ge(raw_in[c.i % RAW], arrived[c.i])
            if c.i >= SPLIT:
                act.wait_ge(sem["chunk", "tensor"], c.i - SPLIT + 1)
            nc.scalar.activation(hi[c.i % SPLIT][:, 0:c.size], raw[c.i % RAW][:, 0:c.size], ACT.Copy)\
              .then_inc(sem["chunk", "scalar"], 1)

        def done(ins, s):
            ins.then_inc(sem[s.kind, "scalar"], 1)

        junked = []

        def square_sum(x, out, s):
            if junked:
                ended(act, junked[-1], "scalar")
            done(nc.scalar.activation(junk[:, :], x, ACT.Square, accum_out=out), s)
            junked.append(s)

        for c in chunks[:AHEAD]:
            split(c)
        act.wait_ge(x_in, 16)
        for s in sc.steps:
            if s.kind == "chunk":
                if s.i == SETUP_AT:
                    act.wait_ge(setup_dve, 2)
                    nc.scalar.activation(sine[:, :, :, :], angle[:, :, :, :], ACT.Sin).then_inc(setup_act, 1)
                    nc.scalar.activation(small[:, :, 1, :], small[:, :, 1, :], ACT.Exp).then_inc(setup_act, 1)
                if s.i + AHEAD < len(chunks):
                    split(chunks[s.i + AHEAD])
            elif s.kind == "turn":
                act.wait_ge(sem["turn", "tensor"], s.i + 1)
                bank = psum[4 + s.bank.at]
                if s.dst == "h":
                    out = hT[0][:, s.k0:s.k0 + 2, :].rearrange("p k t -> p (k t)")
                    done(nc.scalar.activation(out, bank[:, :], ACT.Copy), s)
                else:
                    dst = (xT if s.dst == "x" else oT)[0]
                    done(nc.scalar.activation(dst[:, s.k0:s.k0 + 4, s.m * P:(s.m + 1) * P],
                                              bank[:, :].rearrange("p (k t) -> p k t", k=4), ACT.Copy), s)
            elif s.kind == "square":
                if s.added is not None:
                    ended(act, s.added, "vector")
                square_sum(h[:, s.m, s.n * 512:(s.n + 1) * 512], sumsq[:, 2 * s.m + s.n:2 * s.m + s.n + 1], s)
            elif s.kind == "meansq":
                act.wait_ge(sem["meansq", "vector"], s.i + 1)
                ms, rs = (rms[:, 0, :], rms[:, 1, :]) if s.what == "h" else (rmy[:, 1, :], rmy[:, 2, :])
                link(act, "scalar", nc.scalar.activation(rs, ms, ACT.Ln))
                done(nc.scalar.activation(rs, rs, ACT.Exp, scale=-0.5), s)
            elif s.kind == "ev_kv":
                ended(act, s.rstd, "vector")
                act.wait_ge(setup_dve, 1)
                bank = ready(act, s.block, s.m)
                B = Hb if s.dt is not None else A
                rs = rms[:, 1, s.m:s.m + 1]
                kw = s.nkv * HD
                nc.scalar.activation(B["k"][:, s.m, 0:s.nkv, :], bank[:, 0:kw].rearrange("p (g d) -> p g d", d=HD),
                                     ACT.Copy, scale=rs)
                if s.dt is not None:
                    nc.scalar.activation(B["dtr"][:, s.m, :], bank[:, 256:272], ACT.Copy, scale=rs)
                done(nc.scalar.activation(B["v1"][:, s.m, 0:s.nkv, 0:HD],
                                          bank[:, kw:2 * kw].rearrange("p (g d) -> p g d", d=HD),
                                          ACT.Copy, scale=rs), s)
            elif s.kind == "ev_q":
                bank = ready(act, s.block, s.m)
                B = Hb if s.kind_of == "h" else A
                done(nc.scalar.activation(B["q"][:, s.m, s.j * 512:(s.j + 1) * 512], bank[:, :], ACT.Copy,
                                          scale=rms[:, 1, s.m:s.m + 1]), s)
            elif s.kind == "ev_z":
                bank = ready(act, s.block, s.m)
                B = Hb if s.kind_of == "h" else A
                done(nc.scalar.activation(B["z"][:, s.m, s.j * 512:(s.j + 1) * 512], bank[:, :], ACT.Silu,
                                          scale=rms[:, 1, s.m:s.m + 1]), s)
            elif s.kind == "ev_x":
                bank = ready(act, s.block, s.m)
                if s.conv is not None:
                    ended(act, s.conv, "tensor")
                done(nc.scalar.activation(Hb["xin"][:, s.m, :], bank[:, :], ACT.Copy,
                                          scale=rms[:, 1, s.m:s.m + 1]), s)
            elif s.kind == "ev_up":
                ended(act, s.rstd, "vector")
                if s.i >= 2:
                    act.wait_ge(sem["ev_up", "vector"], s.i - 1)
                for m in range(M):
                    bank = ready(act, s.block, m)
                    last = nc.scalar.activation(sil[s.i % 2][:, m, :], bank[:, 0:UPW], ACT.Silu,
                                                scale=rms[:, 1, m:m + 1])
                done(last, s)
            elif s.kind == "turn_k":
                B = A if s.rope.kind_of != "h" else Hb
                act.wait_ge(sem["turn_k", "tensor"], s.i + 1)
                done(nc.scalar.activation(B["kT"][:, 2 * s.t:2 * s.t + 2, :],
                                          psum[4 + s.bank.at][:, :].rearrange("p (g t) -> p g t", g=2), ACT.Copy), s)
            elif s.kind == "turn_q":
                B = A if s.rope.kind_of != "h" else Hb
                act.wait_ge(sem["turn_q", "tensor"], s.i + 1)
                c0 = 4 * s.j + 2 * s.t
                done(nc.scalar.activation(B["qT"][:, c0:c0 + 2, :],
                                          psum[4 + s.bank.at][:, :].rearrange("p (g t) -> p g t", g=2), ACT.Copy), s)
            elif s.kind == "scores":
                a, hd = s.att, s.head
                B = Hb if a["kind"] == "h" else A
                act.wait_ge(sem["scores", "vector"], s.i + 1)
                if s.i >= 2:
                    act.wait_ge(sem["flip", "tensor"], s.i - 1)
                bank, pr = psum[4 + s.bank.at], B[f"prob{s.p % 2}"]
                nc.scalar.activation(pr[:, 0:P], bank[:, 0:P], ACT.Exp, scale=SCALE, bias=shift[:, hd, 0:1])
                done(nc.scalar.activation(pr[:, P:QC], bank[:, P:QC], ACT.Exp, scale=SCALE,
                                          bias=shift[:, hd, 1:2]), s)
            elif s.kind == "oev":
                a = s.att
                B = Hb if a["kind"] == "h" else A
                ended(act, s.pv, "tensor")
                W1 = HD + 1
                src = psum[4 + s.bank.at][:, 0:4 * W1].rearrange("p (g m d) -> p m g d", g=2, m=2)
                done(nc.scalar.activation(B["o"][:, :, 2 * s.pair:2 * s.pair + 2, :], src, ACT.Copy), s)
            elif s.kind == "sink":
                act.wait_ge(sem["sink", "vector"], s.i + 1)
                e = esink[:, 8 * s.half:8 * s.half + 8, :]
                done(nc.scalar.activation(e, e, ACT.Exp), s)
            elif s.kind == "soft1":
                act.wait_ge(sem["soft1", "vector"], s.i + 1)
                done(nc.scalar.activation(Hb["sb"][:, :, :], Hb["sb"][:, :, :], ACT.Exp, scale=-1.0), s)
            elif s.kind == "soft2":
                act.wait_ge(sem["soft2", "vector"], s.i + 1)
                done(nc.scalar.activation(Hb["sd"][:, :, :], Hb["sc"][:, :, :], ACT.Ln), s)
            elif s.kind == "sums":
                act.wait_ge(sem["sums", "vector"], s.i + 1)
                nc.scalar.activation(Hb["dec"][:, :], Hb["dif"][:, :], ACT.Exp)
                done(nc.scalar.activation(Hb["ecs"][:, :], Hb["ncs"][:, 1, :], ACT.Exp, scale=-1.0), s)
            elif s.kind == "conv":
                act.wait_ge(sem["conv", "vector"], s.i + 1)
                for i in range(4):
                    ct = (8 + i) if s.j == 0 else 4 * (s.j - 1) + i
                    last = nc.scalar.activation(Hb["cT"][:, ct, :], Hb["acc"][:, i, :], ACT.Silu,
                                                bias=convb[:, s.layer, ct:ct + 1])
                done(last, s)
            elif s.kind == "bback":
                act.wait_ge(sem["bback", "tensor"], s.i + 1)
                nc.scalar.activation(Hb["cb"][:, :, :, :].rearrange("p m g l -> p (m g l)"),
                                     psum[4 + s.banks[0].at][:, :], ACT.Copy)
                done(nc.scalar.activation(Hb["bt"][:, :, :].rearrange("p g n -> p (g n)"),
                                          psum[4 + s.banks[1].at][:, 0:2 * P], ACT.Copy), s)
            elif s.kind == "xback":
                act.wait_ge(sem["xback", "tensor"], s.i + 1)
                for m in range(M):
                    last = nc.scalar.activation(Hb["xs"][:, m, s.j * 512:(s.j + 1) * 512],
                                                psum[4 + s.banks[m].at][:, :], ACT.Copy)
                done(last, s)
            elif s.kind == "state":
                act.wait_ge(sem["state", "tensor"], s.i + 1)
                done(nc.scalar.activation(Hb["st"][:, s.g * 512:(s.g + 1) * 512], psum[4 + s.bank.at][:, :],
                                          ACT.Copy), s)
            elif s.kind == "decay":
                m, g = s.mg
                act.wait_ge(sem["decay", "tensor"], s.i + 1)
                ended(act, s.last, "tensor")
                if s.i >= 2:
                    act.wait_ge(sem["decay", "vector"], s.i - 1)
                for i in range(4):
                    hh = 8 * g + 4 * (s.q % 2) + i
                    last = nc.scalar.activation(Hb[f"E{s.i % 2}"][:, i, :], psum[4 + s.bank.at][:, i * P:(i + 1) * P],
                                                ACT.Exp, bias=Hb["ncs"][:, m, hh:hh + 1])
                done(last, s)
            elif s.kind == "join":
                act.wait_ge(sem["join", "vector"], s.i + 1)
                square_sum(Hb["xs"][:, s.m, s.g * 512:(s.g + 1) * 512], rmy[:, 0, 2 * s.m + s.g:2 * s.m + s.g + 1], s)

    @blk.gpsimd
    def _(pool):
        def load_gain(g):
            if g["i"]:
                ended(pool, sc.gains[g["i"] - 1]["users"][-1], "vector")
            name, layer = g["src"]
            row = {"final": t["final_norm_2"], "final_g": t["final_g"]}.get(name)
            row = gain_rows[name][layer] if row is None else row
            pool.dma_start(gains[:, :], row.partition_broadcast(P)).then_inc(gain_in, 16)

        load_gain(sc.gains[0])
        after = {id(sc.gains[g["i"] - 1]["users"][-1]): g for g in sc.gains[1:]}
        for s in sc.steps:
            if id(s) in after:
                load_gain(after[id(s)])
            if s.kind != "xback":
                continue
            pool.wait_ge(sem["xback", "scalar"], s.i + 1)
            ended(pool, s.sums, "scalar")
            hs, cols = slice(8 * s.j, 8 * s.j + 8), slice(s.j * 512, (s.j + 1) * 512)
            for m in range(M):
                xs = Hb["xs"][:, m, cols].rearrange("p (s d) -> p s d", d=HD)
                xg = Hb["xg"][:, m, cols].rearrange("p (s d) -> p s d", d=HD)
                link(pool, "gpsimd", nc.gpsimd.tensor_tensor(
                    xg, xs, spread(Hb["dt"][:, m, hs].unsqueeze(2), [P, 8, HD]), ALU.mult))
                link(pool, "gpsimd", nc.gpsimd.tensor_tensor(
                    xs, xs, spread(small[:, s.conv.layer, 2, hs].unsqueeze(2), [P, 8, HD]), ALU.mult))
            if s.j == 0:
                nc.gpsimd.memset(Hb["dif"][:, 0:1], 0.0).then_inc(sem["xback", "gpsimd"], 1)
            else:
                nc.gpsimd.tensor_tensor(
                    Hb["xgd"][:, :].rearrange("p (s d) -> p s d", d=HD),
                    Hb["xg"][:, 0, :].rearrange("p (s d) -> p s d", d=HD),
                    spread(Hb["dec"][:, :].unsqueeze(2), [P, SH, HD]), ALU.mult).then_inc(sem["xback", "gpsimd"], 1)

    @blk.vector
    def _(dve):
        tt, ts, stt = nc.vector.tensor_tensor, nc.vector.tensor_scalar, nc.vector.scalar_tensor_tensor

        def chained(ins):
            link(dve, "vector", ins)

        def split(c):
            dve.wait_ge(sem["chunk", "scalar"], c.i + 1)
            r = c.i % SPLIT
            tt(lo[r][:, 0:c.size], raw[c.i % RAW][:, 0:c.size], hi[r][:, 0:c.size].bitcast(F32), ALU.subtract)\
              .then_inc(sem["chunk", "vector"], 1)

        def done(ins, s):
            ins.then_inc(sem[s.kind, "vector"], 1)

        def rope(x, cos, sin, t1, t2, half):
            tt(t1, x, cos, ALU.mult)
            tt(t2[..., 0:half], x[..., half:2 * half], sin[..., 0:half], ALU.mult)
            chained(tt(t2[..., half:2 * half], x[..., 0:half], sin[..., half:2 * half], ALU.mult))
            return tt(x, t1, t2, ALU.add)

        rotated = [None]

        def rotate(B, x, m, n, kind):
            if kind == "h":
                cos = spread(trig[:, m, 0, :].unsqueeze(1), [P, n, 16])
                sin = spread(trig[:, m, 1, :].unsqueeze(1), [P, n, 16])
                x, wd, half = x[:, :, 0:16], 16, 8
            else:
                cos = spread(cst[:, C_COS + m * HD:C_COS + (m + 1) * HD].unsqueeze(1), [P, n, HD])
                sin = spread(cst[:, C_SIN + m * HD:C_SIN + (m + 1) * HD].unsqueeze(1), [P, n, HD])
                wd, half = HD, HD // 2
            if rotated[0] is not None:
                ended(dve, rotated[0], "vector")
                rotated[0] = None
            t1 = B["rot1"][:, 0:n * wd].rearrange("p (a d) -> p a d", d=wd)
            t2 = B["rot2"][:, 0:n * wd].rearrange("p (a d) -> p a d", d=wd)
            return rope(x, cos, sin, t1, t2, half)

        def set_up():
            dve.wait_ge(const_in, 16)
            dve.wait_ge(masks_in, 16)
            dve.wait_ge(sinks_in, 16)
            nc.vector.memset(ones[:, :], 1.0)
            ts(sinks[:, 1, :], sinks[:, 0, :], -1.0, None, ALU.mult)
            nc.vector.tensor_copy(identb[:, :], ident)
            chained(nc.vector.tensor_copy(masks[:, :], stage[:, :]))
            nc.vector.memset(A["v1"][:, :, :, :], 1.0).then_inc(setup_dve, 1)

        def angles():
            dve.wait_ge(small_in, 16 * NSMALL)
            chained(nc.vector.tensor_copy(posf[:, :], posi[:, :]))
            two_pi = 2 * math.pi
            c1 = 6.28125
            c2 = float(np.float32(two_pi - c1))
            for m in range(M):
                for f in range(2):
                    last = ts(angle[:, m, f, :], cst[:, C_INV:C_INV + 8], posf[:, m:m + 1], None, ALU.mult)
            chained(last)
            for f in range(2):
                last = ts(turns[:, :, f, :], angle[:, :, f, :], 1.0 / two_pi, 0.25 * (1 - f), ALU.mult, ALU.add)
            chained(last)
            chained(ts(turns[:, :, :, :], turns[:, :, :, :], 12582912.0, None, ALU.add))
            chained(ts(turns[:, :, :, :], turns[:, :, :, :], 12582912.0, None, ALU.subtract))
            for c in (c1, c2, two_pi - c1 - c2):
                chained(stt(angle[:, :, :, :], turns[:, :, :, :], -c, angle[:, :, :, :], ALU.mult, ALU.add))
            chained(ts(angle[:, :, 0, :], angle[:, :, 0, :], math.pi / 2, None, ALU.add))
            lim = float(np.nextafter(np.float32(math.pi), np.float32(0)))
            ts(angle[:, :, :, :], angle[:, :, :, :], lim, -lim, ALU.min, ALU.max).then_inc(setup_dve, 1)

        def tables():
            dve.wait_ge(setup_act, 2)
            for f, sign in enumerate((1.0, -1.0)):
                ts(trig[:, :, f, 0:8], sine[:, :, f, :], sign, None, ALU.mult)
                ts(trig[:, :, f, 8:16], sine[:, :, f, :], 1.0, None, ALU.mult)
            chained(ts(small[:, :, 1, :], small[:, :, 1, :], -1.0, None, ALU.mult))

        for c in chunks[:AHEAD]:
            split(c)
        dve.wait_ge(x_in, 16)
        for s in sc.steps:
            if s.kind == "chunk":
                if s.i == 0:
                    set_up()
                if s.i == SETUP_AT:
                    angles()
                if s.i == SETUP_AT + 1:
                    tables()
                if s.i + AHEAD < len(chunks):
                    split(chunks[s.i + AHEAD])
            elif s.kind == "gained":
                dve.wait_ge(gain_in, 16 * (s.gain["i"] + 1))
                if s.added is not None:
                    ended(dve, s.added, "vector")
                if s.before is not None:
                    ended(dve, s.before, "tensor")
                c = slice(s.n * 512, (s.n + 1) * 512)
                done(tt(quarter[s.buf][:, :], h[:, s.m, c], gains[:, c], ALU.mult), s)
            elif s.kind == "turn":
                dve.wait_ge(sem["turn", "scalar"], s.i + 1)
                bank = psum[4 + s.bank.at]
                if s.dst == "h":
                    a, b = (x[:, s.k0:s.k0 + 2, :].rearrange("p k t -> p (k t)") for x in hT)
                    done(tt(b, bank[:, :], a.bitcast(F32), ALU.subtract), s)
                else:
                    a, b = (x[:, s.k0:s.k0 + 4, s.m * P:(s.m + 1) * P] for x in (xT if s.dst == "x" else oT))
                    done(tt(b, bank[:, :].rearrange("p (k t) -> p k t", k=4), a.bitcast(F32), ALU.subtract), s)
            elif s.kind == "meansq":
                if s.what == "h":
                    dve.wait_ge(sem["square", "scalar"], s.of)
                    q = sumsq[:, :].rearrange("p (m n) -> p m n", n=2)
                    chained(tt(rms[:, 0, :], q[:, :, 0], q[:, :, 1], ALU.add))
                    done(ts(rms[:, 0, :], rms[:, 0, :], 1.0 / D, EPS, ALU.mult, ALU.add), s)
                else:
                    dve.wait_ge(sem["join", "scalar"], s.of)
                    done(ts(rmy[:, 1, :], rmy[:, 0, :], 1.0 / 512, EPS, ALU.mult, ALU.add), s)
            elif s.kind == "newton":
                ended(dve, s.before, "scalar")
                ms, rs, n = (rms[:, 0, :], rms[:, 1, :], 2) if s.what == "h" else (rmy[:, 1, :], rmy[:, 2, :], 4)
                y = newt[:, 0:n]
                chained(tt(y, rs, rs, ALU.mult))
                chained(tt(y, y, ms, ALU.mult))
                chained(ts(y, y, -0.5, 1.5, ALU.mult, ALU.add))
                done(tt(rs, rs, y, ALU.mult), s)
            elif s.kind == "added":
                bank = ready(dve, s.block, s.m)
                x = h[:, s.m, s.n * 512:(s.n + 1) * 512]
                done(tt(x, bank[:, :], x, ALU.add), s)
            elif s.kind == "ev_up":
                dve.wait_ge(sem["ev_up", "scalar"], s.i + 1)
                if s.before is not None:
                    ended(dve, s.before, "tensor")
                for m in range(M):
                    last = stt(quarter[s.buf][:, m * UPW:(m + 1) * UPW], psum[2 * s.block["pair"] + m][:, UPW:2 * UPW],
                               rms[:, 1, m:m + 1], sil[s.i % 2][:, m, :], ALU.mult, ALU.mult)
                done(last, s)
            elif s.kind == "rope_k":
                B = Hb if s.kind_of == "h" else A
                ended(dve, s.ev, "scalar")
                if s.kind_of == "h":
                    nc.vector.memset(B["v1"][:, :, :, HD:HD + 1], 1.0)
                for m in range(M):
                    x = B["k"][:, m, 0:s.nkv, :]
                    chained(rotate(B, x, m, s.nkv, s.kind_of))
                    for a in range(2):
                        last = nc.vector.tensor_copy(B["kdup"][:, m, 0:s.nkv, a, :], x)
                done(last, s)
            elif s.kind == "rope_q":
                B = Hb if s.kind_of == "h" else A
                ended(dve, s.ev, "scalar")
                for m in range(M):
                    x = B["q"][:, m, s.j * 512:(s.j + 1) * 512].rearrange("p (a d) -> p a d", d=HD)
                    last = rotate(B, x, m, 8, s.kind_of)
                    if m == 0:
                        chained(last)
                done(last, s)
                rotated[0] = s
            elif s.kind == "scores":
                a, hd = s.att, s.head
                dve.wait_ge(sem["scores", "tensor"], s.i + 1)
                rm = rowmax[:, s.i % 2, :]
                chained(nc.vector.tensor_reduce(rm[:, 0:3], psum[4 + s.bank.at][:, 0:QC].rearrange("p (a k) -> p a k", a=3),
                                                AXX, ALU.max))
                chained(tt(rm[:, 1:2], rm[:, 1:2], rm[:, 2:3], ALU.max))
                if a["kind"] == "a":
                    done(ts(shift[:, hd, :], rm[:, 0:2], -SCALE, sinks[:, 1, hd:hd + 1], ALU.mult, ALU.min), s)
                else:
                    done(ts(shift[:, hd, :], rm[:, 0:2], -SCALE, None, ALU.mult), s)
            elif s.kind == "flip":
                a = s.att
                B = Hb if a["kind"] == "h" else A
                dve.wait_ge(sem["flip", "tensor"], s.i + 1)
                if s.i >= 2:
                    dve.wait_ge(sem["pv", "tensor"], s.i - 1)
                pt, bank = B[f"probT{s.p % 2}"], psum[4 + s.bank.at]
                if a["kind"] == "h":
                    done(tt(pt[:, :], bank[:, 0:QC], mult, ALU.mult), s)
                else:
                    done(nc.vector.tensor_copy(pt[:, :], bank[:, 0:QC]), s)
            elif s.kind == "sink":
                dve.wait_ge(sem["scores", "vector"], s.att["scores"][8 * s.half + 7].i + 1)
                e = slice(8 * s.half, 8 * s.half + 8)
                done(tt(esink[:, e, :], shift[:, e, :], spread(sinks[:, 0, e].unsqueeze(2), [P, 8, M]), ALU.add), s)
            elif s.kind == "den":
                B = Hb if s.att["kind"] == "h" else A
                ended(dve, s.oev, "scalar")
                d = B["o"][:, :, 8 * s.half:8 * s.half + 8, HD]
                if s.es is not None:
                    ended(dve, s.es, "scalar")
                    e = esink[:, 8 * s.half:8 * s.half + 8, :].rearrange("p s m -> p m s")
                    chained(tt(dens[:, :, :], d, e, ALU.add))
                    d = dens[:, :, :]
                done(nc.vector.reciprocal(dens[:, :, :], d), s)
            elif s.kind == "gate":
                B = Hb if s.att["kind"] == "h" else A
                if s.before is not None:
                    ended(dve, s.before, "tensor")
                ended(dve, s.den, "vector")
                q = quarter[s.buf][:, :]
                o = B["o"][:, s.m, 8 * s.half:8 * s.half + 8, 0:HD]
                first = tt(q.rearrange("p (a d) -> p a d", d=HD), o, spread(dens[:, s.m, :].unsqueeze(2), [P, 8, HD]),
                           ALU.mult)
                if s.z is None:
                    done(first, s)
                else:
                    chained(first)
                    ended(dve, s.z, "scalar")
                    done(tt(q, q, B["z"][:, s.m, s.half * 512:(s.half + 1) * 512], ALU.mult), s)
            elif s.kind == "soft1":
                ended(dve, s.ev, "scalar")
                for m in range(M):
                    last = tt(Hb["dtr"][:, m, :], Hb["dtr"][:, m, :], small[:, s.layer, 0, :], ALU.add)
                chained(last)
                ts(Hb["sa"][:, :, :], Hb["dtr"][:, :, :], 0.0, None, ALU.max)
                done(stt(Hb["sb"][:, :, :], Hb["dtr"][:, :, :], -1.0, Hb["dtr"][:, :, :], ALU.mult, ALU.max), s)
            elif s.kind == "soft2":
                ended(dve, s.before, "scalar")
                done(ts(Hb["sc"][:, :, :], Hb["sb"][:, :, :], 1.0, None, ALU.add), s)
            elif s.kind == "soft3":
                ended(dve, s.before, "scalar")
                e, u, l, dt = (Hb[x][:, :, :] for x in ("sb", "sc", "sd", "dt"))
                same = Hb["dtr"][:, :, :]
                ts(same, u, 1.0, None, ALU.is_equal)
                chained(ts(dt, u, 1.0, None, ALU.subtract))
                chained(tt(dt, dt, same, ALU.add))
                chained(tt(l, l, same, ALU.add))
                chained(nc.vector.reciprocal(dt, dt))
                chained(tt(l, l, e, ALU.mult))
                chained(tt(dt, dt, l, ALU.mult))
                chained(tt(dt, dt, Hb["sa"][:, :, :], ALU.add))
                for m in range(M):
                    last = tt(Hb["da"][:, m, :], Hb["dt"][:, m, :], small[:, s.layer, 1, :], ALU.mult)
                done(last, s)
            elif s.kind == "sums":
                dve.wait_ge(sem["sums", "tensor"], s.i + 1)
                bank = psum[4 + s.bank.at]
                chained(ts(Hb["ncs"][:, :, :].rearrange("p m s -> p (m s)"), bank[:, 0:32], -1.0, None, ALU.mult))
                done(tt(Hb["dif"][:, :], bank[:, 32:48], Hb["ncs"][:, 0, :], ALU.add), s)
            elif s.kind == "conv":
                dve.wait_ge(sem["conv", "tensor"], s.i + 1)
                if s.i % 3:
                    dve.wait_ge(sem["conv", "scalar"], s.i)
                cw = convw[:, s.layer, :, :]

                def bank_of(i):
                    return psum[4 + s.banks[i // 2].at][:, (i % 2) * S:(i % 2 + 1) * S]

                for tap in range(4):
                    for i in range(4):
                        ct = (8 + i) if s.j == 0 else 4 * (s.j - 1) + i
                        acc = Hb["acc"][:, i, :]
                        if tap:
                            dve.wait_ge(chain["vector"], links["vector"] - 3)
                            ins = stt(acc[:, tap:S], bank_of(i)[:, 0:S - tap], cw[:, 3 - tap, ct:ct + 1],
                                      acc[:, tap:S], ALU.mult, ALU.add)
                        else:
                            ins = ts(acc, bank_of(i), cw[:, 3, ct:ct + 1], None, ALU.mult)
                        if tap < 3 or i < 3:
                            ins.then_inc(chain["vector"], 1)
                            links["vector"] += 1
                        else:
                            done(ins, s)
            elif s.kind == "decay":
                m, g = s.mg
                ended(dve, s.bback, "scalar")
                dve.wait_ge(sem["decay", "scalar"], s.i + 1)
                if s.i >= 2:
                    dve.wait_ge(sem["diag", "tensor"], s.i - 1)
                done(tt(Hb[f"MT{s.i % 2}"][:, :, :], Hb[f"E{s.i % 2}"][:, :, :],
                        spread(Hb["cb"][:, m, g, :].unsqueeze(1), [P, 4, P]), ALU.mult), s)
            elif s.kind == "join":
                ended(dve, s.last, "tensor")
                ended(dve, s.xback, "gpsimd")
                c = slice(s.g * 512, (s.g + 1) * 512)
                y = Hb["xs"][:, s.m, c]
                chained(tt(y, psum[4 + s.bank.at][:, :], y, ALU.add))
                if s.obank is not None:
                    t_ = Hb["rot1"][:, :]
                    chained(tt(t_.rearrange("p (s d) -> p s d", d=HD),
                               psum[4 + s.obank.at][:, :].rearrange("p (s d) -> p s d", d=HD),
                               spread(Hb["ecs"][:, 8 * s.g:8 * s.g + 8].unsqueeze(2), [P, 8, HD]), ALU.mult))
                    chained(tt(y, y, t_, ALU.add))
                ended(dve, s.z, "scalar")
                done(tt(y, y, Hb["z"][:, s.m, c], ALU.mult), s)
            elif s.kind == "ynorm":
                ended(dve, s.rstd, "vector")
                dve.wait_ge(gain_in, 16 * (s.gain["i"] + 1))
                if s.before is not None:
                    ended(dve, s.before, "tensor")
                c = slice(s.g * 512, (s.g + 1) * 512)
                n = 2 * s.m + s.g
                done(stt(quarter[s.buf][:, :], Hb["xs"][:, s.m, c], rmy[:, 2, n:n + 1], gains[:, c],
                         ALU.mult, ALU.mult), s)
            elif s.kind == "final":
                ended(dve, s.rstd, "vector")
                dve.wait_ge(gain_in, 16 * (s.gain["i"] + 1))
                done(stt(h[:, s.m, :], h[:, s.m, :], rms[:, 1, s.m:s.m + 1], gains[:, :], ALU.mult, ALU.mult), s)

    program.close()


_INS = ["x", "norm_g", "w_in_a", "sinks_a", "w_in_b", "w_out", "positions_2", "norm_mix_2", "w_in_2", "conv_w_2",
        "conv_b_2", "dt_bias_2", "a_log_2", "d_skip_2", "ssm_norm_2", "w_out_2", "norm_ffn_2", "w_gate_2",
        "w_up_2", "w_down_2", "final_norm_2", "final_g"]


def kernel(**inputs):
    from concourse import bacc
    from concourse.bass_utils import run_bass_kernel_spmd

    nc = bacc.Bacc("TRN2", target_bir_lowering=False, num_devices=1)
    arrays, t = {}, {}
    for name in _INS:
        a = np.ascontiguousarray(inputs[name])
        arrays[f"in_{name}"] = a
        t[name] = nc.dram_tensor(f"in_{name}", a.shape, mybir.dt.from_np(a.dtype), kind="ExternalInput").ap()
    c = constants()
    arrays["in_cst"] = c
    t["cst"] = nc.dram_tensor("in_cst", c.shape, F32, kind="ExternalInput").ap()
    t["out"] = nc.dram_tensor("out", (1, S, D), F32, kind="ExternalOutput").ap()
    build(nc, t)
    r = run_bass_kernel_spmd(nc, [arrays], core_ids=[0])
    return r.results[0]["out"]
```

```python
import math
from contextlib import ExitStack

import numpy as np
import concourse.bass as bass
from concourse import mybir

F32 = mybir.dt.float32
F32R = mybir.dt.float32r
BF16 = mybir.dt.bfloat16
I32 = mybir.dt.int32
ALU = mybir.AluOpType
ACT = mybir.ActivationFunctionType
AXX = mybir.AxisListType.X

S, D, P = 256, 1024, 128
M = S // P
KD = D // P
HD = 64
NEG = -1e30
EPS = 1e-5
SCALE = HD ** -0.5
FF = 2816
KF = FF // P
UPW = 256
NUP = FF // UPW
SSM = 1024
CONV = SSM + 512
NST = 128
SH = 16
NCT = CONV // P
RAW, SPLIT = 3, 3
SETUP_AT = 11
AHEAD = 2
CH = 8 * 272
NSCR = 4
QC = 3 * P

C_ID, C_U, C_CT = 0, P, 2 * P
C_COS, C_SIN, C_INV = C_CT + QC, C_CT + QC + 2 * HD, C_CT + QC + 4 * HD
C_KEEP = C_INV + 8
C_MASK = C_KEEP
C_ALL = C_MASK + 3 * QC + P


def constants():
    t, u = np.arange(P)[:, None], np.arange(P)[None, :]
    tiles = ((0, 0), (1, 0), (1, 1))
    delta = [t + P * q - u - P * k for q, k in tiles]
    c = np.zeros((P, C_ALL), np.float32)
    c[:, C_ID:C_ID + P] = np.eye(P)
    c[:, C_U:C_U + P] = t <= u
    mult = [(d >= 0) * ((d <= 128).astype(np.float32) + (d % 4 == 0) + (d % 16 == 0)) for d in delta]
    for i, x in enumerate(mult):
        c[:, C_CT + i * P:C_CT + (i + 1) * P] = x.T
    inv = np.float32(10000.0) ** (-np.arange(0, HD, 2, dtype=np.float32) / np.float32(HD))
    for m in range(M):
        ang = (np.arange(P, dtype=np.float32) + P * m)[:, None] * inv[None, :]
        cos, sin = np.cos(ang), np.sin(ang)
        c[:, C_COS + m * HD:C_COS + (m + 1) * HD] = np.concatenate([cos, cos], 1)
        c[:, C_SIN + m * HD:C_SIN + (m + 1) * HD] = np.concatenate([-sin, sin], 1)
    c[:, C_INV:C_INV + 8] = np.float32(500000.0) ** (-np.arange(0, 16, 2, dtype=np.float32) / np.float32(16))
    seen = (
        [(d >= 0) & (d < 128) for d in delta],
        [d >= 0 for d in delta],
        [x > 0 for x in mult],
    )
    for n, per in enumerate(seen):
        for i, x in enumerate(per):
            at = C_MASK + n * QC + i * P
            c[:, at:at + P] = np.where(x, 0.0, NEG)
    c[:, C_MASK + 3 * QC:] = np.where(t > u, NEG, 0.0)
    return c


class Step:

    def __init__(self, kind, i, *, loads=None, outs=None, needs=None, first=None, last=None, size=None,
                 buf=None, before=None, src=None, dst=None, k0=None, m=None, n=None, u=None, g=None, j=None,
                 t=None, q=None, bank=None, banks=None, obank=None, block=None, gain=None, added=None,
                 of=None, what=None, rstd=None, att=None, head=None, pair=None, half=None, p=None, pv=None,
                 oev=None, den=None, es=None, z=None, nkv=None, dt=None, kind_of=None, ev=None, rope=None,
                 layer=None, conv=None, soft=None, sums=None, xback=None, bback=None, state=None,
                 decay=None, mg=None):
        self.kind, self.i = kind, i
        self.loads, self.outs, self.needs, self.size = loads, outs, needs, size
        self.first, self.last = first, last
        self.buf, self.before, self.src, self.dst, self.k0 = buf, before, src, dst, k0
        self.bank, self.banks, self.obank, self.block = bank, banks, obank, block
        self.m, self.n, self.u, self.g, self.j, self.t, self.q, self.mg = m, n, u, g, j, t, q, mg
        self.gain, self.added, self.of, self.what, self.rstd = gain, added, of, what, rstd
        self.att, self.head, self.pair, self.half, self.p, self.pv = att, head, pair, half, p, pv
        self.oev, self.den, self.es, self.z = oev, den, es, z
        self.nkv, self.dt, self.kind_of, self.ev, self.rope = nkv, dt, kind_of, ev, rope
        self.layer, self.conv, self.soft, self.sums = layer, conv, soft, sums
        self.xback, self.bback, self.state, self.decay = xback, bback, state, decay


class Bank:

    def __init__(self, at, before):
        self.at, self.before, self.freed = at, before, None


class Schedule:

    def __init__(self):
        self.steps, self.count, self.blocks, self.banks = [], {}, [], []
        self.parts, self.quarters, self.gains = 0, [], []
        self.soon, self.filled, self.added, self.turned, self.oturned = [], {}, {}, {}, {}
        self.heads, self.loaded = 0, 0

    def step(self, kind, **of):
        s = Step(kind, self.count.get(kind, 0), **of)
        self.count[kind] = s.i + 1
        self.steps.append(s)
        return s

    def bank(self):
        n = len(self.banks)
        b = Bank(n % NSCR, self.banks[n - NSCR] if n >= NSCR else None)
        assert b.before is None or b.before.freed is not None, "a bank is taken before it is freed"
        self.banks.append(b)
        return b

    def block(self, width):
        g = len(self.blocks)
        b = {"pair": g % 2, "width": width, "before": self.blocks[g - 2] if g >= 2 else None,
             "evac": [None, None], "ready": [None, None]}
        self.blocks.append(b)
        return b

    def goes_on(self, work=()):
        if self.soon:
            self.soon.pop(0)()
        for f in work:
            f()

    def chunk(self, loads, outs, needs, first, last, beside=()):
        order = [(b, wd, ts, m) for b, wd, ts in outs for m in range(M)]
        s = self.step("chunk", loads=loads, outs=order, needs=needs, first=first, last=last,
                      size=sum(x[0] for x in loads))
        self.goes_on(beside)
        self.step("rest", of=s)
        if last:
            for b, _, _, m in order[:-1]:
                self.parts += 1
                b["ready"][m] = ("part", self.parts)
            order[-1][0]["ready"][M - 1] = ("chunk_tensor", s.i + 1)
        return s

    def quarter(self, kind, **of):
        n = len(self.quarters)
        s = self.step(kind, buf=n % 2, before=self.quarters[n - 2] if n >= 2 else None, **of)
        self.quarters.append(None)
        return s

    def turn(self, src, dst, k0, m):
        b = self.bank()
        s = self.step("turn", src=src, dst=dst, k0=k0, m=m, bank=b)
        b.freed = (s, "vector")
        self.quarters[self.quarters.index(None)] = s
        return s

    def gain(self, src):
        if src is not None:
            self.loaded += 1
        g = {"src": src, "i": len(self.gains), "loaded": self.loaded, "users": [], "made": None}
        self.gains.append(g)
        return g


def attention(sc, n):
    a = sc.att
    if n < a["heads"]:
        b = sc.bank()
        s = sc.step("scores", head=n, att=a, bank=b, p=a["base"] + n)
        b.freed = (s, "scalar")
        a["scores"].append(s)
    if 2 <= n <= a["heads"] + 1:
        b = sc.bank()
        s = sc.step("flip", head=n - 2, att=a, bank=b, p=a["base"] + n - 2)
        b.freed = (s, "vector")
        a["flip"].append(s)
    if 3 <= n <= a["heads"] + 2:
        head = n - 3
        if head % 2 == 0:
            a["obank"] = sc.bank()
        s = sc.step("pv", head=head, att=a, bank=a["obank"], p=a["base"] + head)
        a["pv"].append(s)
        if head % 2 == 1:
            o = sc.step("oev", att=a, pair=head // 2, bank=a["obank"], pv=s)
            a["obank"].freed = (o, "scalar")
            a["oev"].append(o)


def add(sc, block, n, m):
    block["evac"][m] = sc.added[n, m] = sc.step("added", n=n, m=m, block=block)


def times_gain(sc, n, m):
    gain = sc.gain_now
    s = sc.quarter("gained", n=n, m=m, gain=gain, added=sc.added.get((n, m)))
    gain["users"].append(s)
    sc.filled[n, m] = s


def turn_x(sc, n):
    for m in range(M):
        sc.turned[n, m] = sc.turn(sc.filled[n, m], "x", 4 * n, m)


def squares(sc, n):
    for m in range(M):
        sc.step("square", n=n, m=m, added=sc.added.get((n, m)))


def factor(sc, what):
    a = sc.step("meansq", what=what, of=sc.count["square"])
    sc.rstd = sc.step("newton", what=what, before=a)


def norm_goes_on(sc, mid):
    def second_half():
        turn_x(sc, 1)
        if not mid:
            squares(sc, 0)

    def factors():
        if mid:
            squares(sc, 0)
            squares(sc, 1)
            factor(sc, "first")
            normed_residual(sc, "mid")
            squares(sc, 0)
            squares(sc, 1)
            factor(sc, "both")
        else:
            squares(sc, 1)
            factor(sc, "h")

    sc.soon += [second_half, factors]


def normed_residual(sc, what):
    for m in range(M):
        s = sc.step("final", m=m, what=what, gain=sc.gain_now, rstd=sc.rstd)
        for n in range(2):
            sc.added[n, m] = s


def project_chunk(sc, w, cols, ks, block, first, last, beside=(), then=()):
    src = [(len(ks) * cw, (w, c0, cw, ks)) for c0, cw in cols]
    width = sum(cw for _, cw in cols)
    outs = [(block, width, [("x", k, i * width) for i, k in enumerate(ks)])]
    need = [[sc.turned[n, m] for n in range(2) if 4 * n in ks] for m in range(M)]
    sc.chunk(src, outs, need, first, last, beside)
    sc.goes_on(then)


def halves(sc, w, cols, a=(), b=(), c=()):
    blk = sc.block(sum(cw for _, cw in cols))
    project_chunk(sc, w, cols, [0, 1, 2, 3], blk, True, False, a, b)
    project_chunk(sc, w, cols, [4, 5, 6, 7], blk, False, True, c)
    return blk


def out_product(sc, w, kt, beside, mid=False):
    bs = [sc.block(512), sc.block(512)]
    c = 0
    for k0 in range(0, kt, 4):
        ks = list(range(k0, k0 + 4))
        end = k0 + 4 == kt
        for n in range(2):
            need = [[sc.oturned[k0 // 4, m]] for m in range(M)]

            def begin():
                add(sc, bs[1], 1, 0)
                turn_x(sc, 0)
                times_gain(sc, 1, 0)

            between, after = beside.get(c, ((), ()))
            if end and n:
                between = list(between) + [begin]
            sc.chunk([(4 * 512, (w, n * 512, 512, ks))],
                     [(bs[n], 512, [("o", k, i * 512) for i, k in enumerate(ks)])],
                     need, k0 == 0, end, between)
            sc.goes_on(after)
            c += 1
            if end and n == 0:
                for m in range(M):
                    add(sc, bs[0], 0, m)
                    times_gain(sc, 0, m)
    add(sc, bs[1], 1, 1)
    times_gain(sc, 1, 1)
    norm_goes_on(sc, mid)


def evacs(sc, b, kind, **of):
    for m in range(M):
        b["evac"][m] = sc.step(kind, m=m, block=b, rstd=sc.rstd, **of)
    return b["evac"][1]


def turn_keys(sc, a, kr):
    for t in range(a["nkv"] // 2):
        bk = sc.bank()
        s = sc.step("turn_k", t=t, rope=kr, bank=bk)
        bk.freed = (s, "scalar")
        a["tk"].append(s)


def turn_queries(sc, a, j, rq):
    for t in range(2):
        bk = sc.bank()
        s = sc.step("turn_q", j=j, t=t, rope=rq, bank=bk)
        bk.freed = (s, "scalar")
        a["tq"].append(s)


def fill_gates(sc, a, half, z):
    es = sc.step("sink", att=a, half=half) if a["kind"] == "a" else None
    den = sc.step("den", att=a, half=half, es=es, oev=a["oev"][4 * half + 3])
    a["gates"][half] = [sc.quarter("gate", att=a, half=half, m=m, z=z, den=den) for m in range(M)]


def turn_gates(sc, a, half):
    for m in range(M):
        sc.oturned[half, m] = sc.turn(a["gates"][half][m], "o", 4 * half, m)


def new_attention(sc, which, heads, nkv):
    a = sc.att = {"kind": which, "heads": heads, "nkv": nkv, "scores": [], "flip": [], "pv": [], "oev": [],
                  "base": sc.heads, "tk": [], "tq": [], "gates": {}}
    sc.heads += heads
    return a


def mixer_ab(sc, which, w_in, w_out, nkv, mid=False):
    kvw = nkv * HD
    a = new_attention(sc, which, 16, nkv)

    def att(*ns):
        return [lambda n=n: attention(sc, n) for n in ns]

    kv = [(D, 2 * kvw)]
    b = halves(sc, w_in, [(0, 512)])
    ev = evacs(sc, b, "ev_q", j=0, kind_of=which)
    rq0 = sc.step("rope_q", j=0, kind_of=which, ev=ev)
    if nkv == 2:
        b = sc.block(2 * kvw)
        project_chunk(sc, w_in, kv, list(range(KD)), b, True, True)
    else:
        b = halves(sc, w_in, kv)
    ev = evacs(sc, b, "ev_kv", nkv=nkv, dt=None)
    kr = sc.step("rope_k", nkv=nkv, kind_of=which, ev=ev)
    b = halves(sc, w_in, [(512, 512)], [lambda: turn_queries(sc, a, 0, rq0)],
               [lambda: turn_keys(sc, a, kr)], att(0))
    ev = evacs(sc, b, "ev_q", j=1, kind_of=which)
    rq1 = sc.step("rope_q", j=1, kind_of=which, ev=ev)
    sc.goes_on(att(1))

    def queries():
        turn_queries(sc, a, 1, rq1)
        if mid:
            sc.step("mid_load", before=a["tq"][-1])

    b = halves(sc, w_in, [(D + 2 * kvw, 512)], att(2), [queries] + att(3), att(4, 5))
    za = evacs(sc, b, "ev_z", j=0, kind_of=which)
    sc.goes_on(att(6))
    if mid:
        sc.gain_now = sc.gain(None)
        sc.gain_now["made"] = sc.step("mid_gain")
    b = halves(sc, w_in, [(D + 2 * kvw + 512, 512)], att(7, 8), att(9, 10),
               [lambda: fill_gates(sc, a, 0, za)] + att(11, 12))
    zb = evacs(sc, b, "ev_z", j=1, kind_of=which)
    sc.goes_on(att(13, 14) + [lambda: turn_gates(sc, a, 0)])
    out_product(sc, w_out, KD, {
        0: (att(15, 16), att(17, 18) + [lambda: fill_gates(sc, a, 1, zb)]),
        1: ((), [lambda: turn_gates(sc, a, 1)])}, mid)


def hybrid(sc, layer, w, last_gain):
    a = new_attention(sc, "h", 8, 2)
    w_in, q0, kv0, z0, x0, dt0 = w["in"], 0, 512, 768, 1792, 3328
    scan = {}

    def att(*ns):
        return [lambda n=n: attention(sc, n) for n in ns]

    def conv(j):
        b1, b2 = sc.bank(), sc.bank()
        s = sc.step("conv", j=j, banks=(b1, b2), layer=layer, ev=scan["ev", j])
        b1.freed = b2.freed = (s, "vector")
        scan["conv", j] = s

    def evac_x(b, j):
        scan["ev", j] = evacs(sc, b, "ev_x", j=j, conv=scan["conv", j - 1] if j else None)

    def back(j):
        b1, b2 = sc.bank(), sc.bank()
        s = sc.step("xback", j=j, banks=(b1, b2), conv=scan["conv", j + 1], sums=scan["sums"])
        b1.freed = b2.freed = (s, "scalar")
        scan["xback", j] = s

    def bback():
        b1, b2 = sc.bank(), sc.bank()
        s = sc.step("bback", banks=(b1, b2), conv=scan["conv", 0])
        b1.freed = b2.freed = (s, "scalar")
        scan["bback"] = s

    def sums():
        bk = sc.bank()
        scan["sums"] = sc.step("sums", bank=bk, before=scan["soft3"])
        bk.freed = (scan["sums"], "vector")

    def decay(g, m, i):
        bk = sc.bank()
        s = sc.step("decay", q=i, mg=(m, g), bank=bk, sums=scan["sums"], bback=scan["bback"])
        bk.freed = (s, "scalar")
        scan["decay", g, m, i] = s

    def state(g):
        bk = sc.bank()
        s = sc.step("state", g=g, bank=bk, xback=scan["xback", g], bback=scan["bback"])
        bk.freed = (s, "scalar")
        scan["state", g] = s

    def scanned(g, m):
        yb = sc.bank()
        for i in range(2):
            last = sc.step("diag", q=i, m=m, g=g, bank=yb, decay=scan["decay", g, m, i], xback=scan["xback", g])
        ob = None
        if m == 1:
            ob = sc.bank()
            last = sc.step("off", g=g, bank=ob, state=scan["state", g])
        y = sc.step("join", m=m, g=g, bank=yb, obank=ob, last=last, z=scan["z", g], xback=scan["xback", g])
        yb.freed = (y, "vector")
        if ob:
            ob.freed = (y, "vector")

    def group_norm(g):
        ra = sc.step("meansq", what="y", g=g, of=sc.count["join"])
        rb = sc.step("newton", what="y", g=g, before=ra)
        scan["y", g] = []
        for m in range(M):
            s = sc.quarter("ynorm", m=m, g=g, rstd=rb, gain=scan["gain"])
            scan["gain"]["users"].append(s)
            scan["y", g].append(s)

    def turn_y(g):
        for m in range(M):
            sc.oturned[1 + g, m] = sc.turn(scan["y", g][m], "o", 4 + 4 * g, m)

    def do(f, *x):
        return [lambda: f(*x)]

    b = halves(sc, w_in, [(q0, 512)])
    ev = evacs(sc, b, "ev_q", j=0, kind_of="h")
    rq = sc.step("rope_q", j=0, kind_of="h", ev=ev)
    b = sc.block(272)
    project_chunk(sc, w_in, [(kv0, 256), (dt0, 16)], list(range(8)), b, True, True)
    ev = evacs(sc, b, "ev_kv", nkv=2, dt=layer)
    kr = sc.step("rope_k", nkv=2, kind_of="h", ev=ev)
    sp = sc.step("soft1", layer=layer, ev=ev)
    s2 = sc.step("soft2", before=sp)
    scan["soft3"] = sc.step("soft3", before=s2, layer=layer)
    b = halves(sc, w_in, [(x0 + SSM, 512)], do(turn_queries, sc, a, 0, rq), do(turn_keys, sc, a, kr), do(sums) + att(0))
    evac_x(b, 0)
    b = halves(sc, w_in, [(x0, 512)], att(1, 2), do(conv, 0), att(3))
    evac_x(b, 1)
    sc.goes_on(att(4))
    b = halves(sc, w_in, [(x0 + 512, 512)], att(5, 6), do(conv, 1), att(7))
    evac_x(b, 2)
    sc.goes_on(att(8) + do(bback))
    scan["gain"] = sc.gain(("ssm_norm", layer))
    b = halves(sc, w_in, [(z0, 512)], att(9, 10), do(conv, 2), do(back, 0) + do(fill_gates, sc, a, 0, None))
    scan["z", 0] = evacs(sc, b, "ev_z", j=0, kind_of="h")
    sc.goes_on(do(turn_gates, sc, a, 0) + do(decay, 0, 0, 0))
    b = halves(sc, w_in, [(z0 + 512, 512)], do(decay, 0, 0, 1) + do(state, 0), do(back, 1) + do(scanned, 0, 0),
               do(decay, 0, 1, 0) + do(decay, 0, 1, 1))
    scan["z", 1] = evacs(sc, b, "ev_z", j=1, kind_of="h")
    sc.goes_on(do(scanned, 0, 1) + do(group_norm, 0))

    def next_gain():
        sc.gain_now = sc.gain(("norm_ffn", layer))

    out_product(sc, w["out"], 12, {
        0: (do(decay, 1, 0, 0) + do(state, 1), do(decay, 1, 0, 1)),
        1: (do(turn_y, 0) + do(scanned, 1, 0) + do(decay, 1, 1, 0), do(decay, 1, 1, 1)),
        2: (do(scanned, 1, 1) + do(group_norm, 1) + do(next_gain), ()),
        3: ((), do(turn_y, 1))})

    pend = None
    hturn = []
    for u in range(NUP):
        b = sc.block(2 * UPW)
        for half in range(2):
            ks = list(range(4 * half, 4 * half + 4))
            sc.chunk([(4 * UPW, (w["gate"], u * UPW, UPW, ks)), (4 * UPW, (w["up"], u * UPW, UPW, ks))],
                     [(b, 2 * UPW, [("x", k, i * 2 * UPW) for i, k in enumerate(ks)])],
                     [[sc.turned[half, m]] for m in range(M)], half == 0, half == 1)
            sc.goes_on()
            if half == 0 and pend is not None:
                hturn.append(sc.turn(pend, "h", 2 * pend.u, 0))
                pend = None
        pend = sc.quarter("ev_up", u=u, block=b, rstd=sc.rstd)
        b["evac"] = [pend, pend]
    sc.gain_now = sc.gain(last_gain)
    b0, b1 = sc.block(512), sc.block(512)
    for j in range(KF // 2):
        if j == 1:
            hturn.append(sc.turn(pend, "h", 2 * pend.u, 0))

        def first_block_ends():
            for m in range(M):
                add(sc, b0, 0, m)
            for m in range(M):
                if layer == 0:
                    times_gain(sc, 0, m)

        last = j == KF // 2 - 1
        sc.chunk([(2 * D, (w["down"], 0, D, [2 * j, 2 * j + 1]))],
                 [(b, 512, [("h", 2 * j + i, i * D + n * 512) for i in range(2)]) for n, b in enumerate((b0, b1))],
                 [[hturn[j]], []], j == 0, last, [first_block_ends] if last else ())
    if layer == 0:
        add(sc, b1, 1, 0)
        turn_x(sc, 0)
        add(sc, b1, 1, 1)
        for m in range(M):
            times_gain(sc, 1, m)
        norm_goes_on(sc, False)
    else:
        squares(sc, 0)
        for m in range(M):
            add(sc, b1, 1, m)
        squares(sc, 1)
        factor(sc, "h")
        normed_residual(sc, "end")


def build_schedule(w):
    sc = Schedule()
    sc.gain_now = sc.gain(("norm_g", 0))
    for m in range(M):
        times_gain(sc, 0, m)
    turn_x(sc, 0)
    for m in range(M):
        times_gain(sc, 1, m)
    norm_goes_on(sc, False)
    sc.gain_now = sc.gain(("norm_g", 1))
    mixer_ab(sc, "a", w["in_a"], w["out0"], 2)
    mixer_ab(sc, "b", w["in_b"], w["out1"], 4, True)
    hybrid(sc, 0, w["h"][0], ("norm_mix", 1))
    hybrid(sc, 1, w["h"][1], ("final", 0))
    return sc


def due(s):
    if s.kind == "chunk":
        return [0] if s.i == 0 else [2, 3] if s.i == 1 else [s.i + AHEAD]
    return [1] if s.kind == "rest" and s.i == 0 else []


PARTS = {
    "chunk": ("tensor", "scalar", "vector"), "gained": ("vector",), "turn": ("tensor", "scalar", "vector"),
    "mid_gain": ("vector",), "square": ("scalar",), "meansq": ("vector", "gpsimd"), "newton": ("vector",), "added": ("vector",),
    "ev_kv": ("scalar",), "ev_q": ("scalar",), "ev_z": ("scalar",), "ev_x": ("scalar",),
    "ev_up": ("scalar", "vector"), "rope_k": ("vector",), "rope_q": ("vector",),
    "turn_k": ("tensor", "scalar"), "turn_q": ("tensor", "scalar"),
    "scores": ("tensor", "vector", "scalar"), "flip": ("tensor", "vector"), "pv": ("tensor",),
    "oev": ("scalar",), "sink": ("vector", "scalar"), "den": ("vector",), "gate": ("vector",),
    "soft1": ("vector", "scalar"), "soft2": ("vector", "scalar"), "soft3": ("vector",),
    "sums": ("tensor", "vector", "scalar"), "conv": ("tensor", "vector", "scalar"),
    "bback": ("tensor", "scalar"), "xback": ("tensor", "scalar", "gpsimd"), "state": ("tensor", "scalar"),
    "decay": ("tensor", "scalar", "vector"), "diag": ("tensor",), "off": ("tensor",),
    "join": ("vector", "scalar"), "ynorm": ("vector",), "final": ("vector",),
}


def build(nc, t):
    def w3(ap):
        return ap.rearrange("(k p) n -> p k n", p=P)

    w = {"in_a": w3(t["w_in_a"][0]), "in_b": w3(t["w_in_b"][0]), "out0": w3(t["w_out"][0]), "out1": w3(t["w_out"][1]),
         "h": [{"in": w3(t["w_in_2"][i]), "out": w3(t["w_out_2"][i]), "gate": w3(t["w_gate_2"][i]),
                "up": w3(t["w_up_2"][i]), "down": w3(t["w_down_2"][i])} for i in range(2)]}
    sc = build_schedule(w)
    chunks = [s for s in sc.steps if s.kind == "chunk"]
    gain_rows = {"norm_g": t["norm_g"], "norm_mix": t["norm_mix_2"], "ssm_norm": t["ssm_norm_2"],
                 "norm_ffn": t["norm_ffn_2"]}

    place = [16512]

    def at(name, shape, dt, where=None):
        size = math.prod(shape[1:]) * (2 if dt == BF16 else 4)
        size = -(-size // 32) * 32
        if where is None:
            where = place[0]
            place[0] += size
        else:
            at.end = max(at.end, where + size)
        return nc.alloc_sbuf_tensor_at(name, shape, dt, offset=where), where + size

    def keep(name, shape, dt=F32):
        return at(name, shape, dt)[0]

    at.end = 0
    h = keep("h", [P, M, D])
    xT = [keep("xT_hi", [P, KD, S], F32R), keep("xT_lo", [P, KD, S], F32R)]
    oT = [keep("oT_hi", [P, 12, S], F32R), keep("oT_lo", [P, 12, S], F32R)]
    raw = [keep(f"raw{i}", [P, CH]) for i in range(RAW)]
    hi = [keep(f"hi{i}", [P, CH], F32R) for i in range(SPLIT)]
    lo = [keep(f"lo{i}", [P, CH], F32R) for i in range(SPLIT)]
    quarter = [keep(f"quarter{i}", [P, 512]) for i in range(2)]
    gains = keep("gains", [P, D])
    cst = keep("cst", [P, C_KEEP])
    masks = keep("masks", [P, 3 * QC + P], BF16)
    identb = keep("identb", [P, P], BF16)
    ones = keep("ones", [P, P])
    junk = keep("junk", [P, 512], BF16)
    sumsq = keep("sumsq", [P, 4])
    rms = keep("rms", [P, 3, M])
    rmy = keep("rmy", [P, 3, 4])
    newt = keep("newt", [P, 3, 2])
    power = keep("power", [P, 2])
    posi = keep("posi", [P, M], I32)
    posf = keep("posf", [P, M])
    trig = keep("trig", [P, M, 2, 16])
    sinks = keep("sinks", [P, 2, 16])
    small = keep("small", [P, 2, 3, 16])
    convw = keep("convw", [P, 2, 4, NCT])
    convb = keep("convb", [P, 2, NCT])
    rowmax = keep("rowmax", [P, 2, 4])
    shift = keep("shift", [P, 16, M])
    esink = keep("esink", [P, 16, M])
    dens = keep("dens", [P, M, 8])
    ident, upper = cst[:, C_ID:C_ID + P], cst[:, C_U:C_U + P]
    mult = cst[:, C_CT:C_CT + QC]

    base = place[0]
    hT = []
    end = base
    for i in range(2):
        x, end = at(f"hT{i}", [P, KF, S], F32R, end)
        hT.append(x)
    sil = []
    for i in range(2):
        x, end = at(f"silu_gate{i}", [P, M, UPW], F32, end)
        sil.append(x)

    def plan(tag, hybrid_):
        b = {}
        p = [base]

        def put(name, shape, dt=F32, where=None):
            x, e = at(f"{tag}_{name}", shape, dt, p[0] if where is None else where)
            b[name + "_at"] = (p[0] if where is None else where)
            if where is None:
                p[0] = e
            b[name] = x
            return e

        nkv, heads = (2, 8) if hybrid_ else (4, 16)
        put("v1", [P, M, nkv, HD + 1])
        put("kT", [P, nkv, S])
        put("qT", [P, heads // 2, S])
        put("prob0", [P, QC])
        put("prob1", [P, QC])
        put("probT0", [P, QC])
        put("probT1", [P, QC])
        put("z", [P, M, D])
        e = put("k", [P, M, nkv, HD])
        e = put("kdup", [P, M, nkv, 2, HD])
        put("rot1", [P, 512])
        e = put("rot2", [P, 512])
        put("o", [P, M, heads, HD + 1], where=b["k_at"])
        e = b["k_at"] + 4 * M * heads * (HD + 1)
        p[0] = max(p[0], -(-e // 32) * 32)
        q_at = p[0]
        put("q", [P, M, heads * HD])
        if hybrid_:
            e = put("cb", [P, M, 2, P], where=q_at)
            put("bt", [P, 2, P], where=e)
            put("xin", [P, M, 512])
            put("st", [P, SSM], where=b["xin_at"])
            put("cT", [P, NCT, S])
            e = put("E0", [P, 4, P], where=b["prob0_at"])
            e = put("E1", [P, 4, P], where=e)
            put("MT0", [P, 4, P], where=e)
            e = put("xgd", [P, SSM], where=b["kT_at"])
            put("MT1", [P, 4, P], where=e)
            put("xs", [P, M, SSM])
            for i in range(2):
                put(f"acc{i}", [P, 2, S], where=b["xs_at"] + 4 * (512 + i * SSM))
            put("xg", [P, M, SSM])
            for name in ("dtr", "dt", "da", "sa", "sb", "sc", "sd"):
                put(name, [P, M, SH])
            put("ncs", [P, M, SH])
            put("dif", [P, SH])
            put("dec", [P, SH])
            put("ecs", [P, SH])
        return b

    A, Hb = plan("attn", False), plan("hyb", True)
    stage, _ = at("mask_stage", [P, C_ALL - C_KEEP], F32, base)
    angle, e = at("trig_stage", [P, M, 2, 8], F32, base + 8192)
    sine, e = at("trig_stage2", [P, M, 2, 8], F32, e)
    turns, _ = at("trig_stage3", [P, M, 2, 8], F32, e)
    mid_rows = [at(f"mid_row{i}", [P, D], F32, A["q_at"] + 4 * D * i)[0] for i in range(2)]
    assert max(place[0], at.end) <= 229344, (place[0], at.end)

    psum = [nc.alloc_psum_tensor(f"bank{i}", [P, 512], F32) for i in range(8)]

    sem = {}
    for kind, who in PARTS.items():
        for e in who:
            sem[kind, e] = nc.alloc_semaphore(f"{kind}_{e}")
    raw_in = [nc.alloc_semaphore(f"raw_in{i}") for i in range(RAW)]
    part_done = nc.alloc_semaphore("part_done")
    x_in = nc.alloc_semaphore("x_in")
    const_in = nc.alloc_semaphore("const_in")
    masks_in = nc.alloc_semaphore("masks_in")
    sinks_in = nc.alloc_semaphore("sinks_in")
    small_in = nc.alloc_semaphore("small_in")
    mid_in = nc.alloc_semaphore("mid_in")
    x_first = nc.alloc_semaphore("x_first")
    gain_in = nc.alloc_semaphore("gain_in")
    setup_dve = nc.alloc_semaphore("setup_vector")
    setup_act = nc.alloc_semaphore("setup_scalar")
    out_done = nc.alloc_semaphore("out_done")
    chain = {e: nc.alloc_semaphore(f"chain_{e}") for e in ("vector", "scalar", "gpsimd")}
    links = {"vector": 0, "scalar": 0, "gpsimd": 0}

    def ended(eng, step, who):
        eng.wait_ge(sem[step.kind, who], step.i + 1)

    def freed(eng, bank):
        if bank.before is not None:
            ended(eng, bank.before.freed[0], bank.before.freed[1])
        return psum[4 + bank.at]

    def ready(eng, block, m):
        name, v = block["ready"][m]
        eng.wait_ge(part_done if name == "part" else sem["chunk", "tensor"], v)
        return psum[2 * block["pair"] + m]

    def link(eng, who, ins):
        links[who] += 1
        ins.then_inc(chain[who], 1)
        eng.wait_ge(chain[who], links[who])

    def norm_parts(s):
        if s.what == "y":
            g = slice(2 * s.g, 2 * s.g + 2)
            return rmy[:, 0, g], rmy[:, 1, g], rmy[:, 2, g], newt[:, 1 + s.g, :]
        return sumsq, rms[:, 0, :], rms[:, 2 if s.what == "first" else 1, :], newt[:, 0, :]

    def spread(ap, shape):
        return ap.broadcast_to(shape)

    arrived, total = {}, [0] * RAW
    for c in chunks:
        total[c.i % RAW] += 16 * len(c.loads)
        arrived[c.i] = total[c.i % RAW]

    NSMALL = 1 + 2 * (3 + 4 + 1)
    program = ExitStack()
    blk = program.enter_context(nc.Block())

    @blk.sync
    def _(sp):
        with nc.allow_non_contiguous_dma("small rows and weights by columns"):
            x = t["x"][0].rearrange("(m p) d -> p m d", p=P)
            sp.dma_start(cst[:, 0:P], t["cst"][:, 0:P]).then_inc(const_in, 16)
            sp.dma_start(h[:, :, 0:512], x[:, :, 0:512]).then_inc(x_first, 16)

            def load(c):
                slot = raw[c.i % RAW]
                if c.i >= RAW:
                    sp.wait_ge(sem["chunk", "vector"], c.i - RAW + 1)
                off = 0
                for n, (size, (wt, c0, cw, ks)) in enumerate(c.loads):
                    src = wt[:, ks[0]:ks[-1] + 1, c0:c0 + cw]
                    if len(c.loads) == 1:
                        dst = slot[:, 0:size].rearrange("p (k n) -> p k n", n=cw)
                    else:
                        full = c.size // len(ks)
                        dst = slot[:, 0:c.size].rearrange("p (k n) -> p k n", n=full)[:, :, off:off + cw]
                        off += cw
                    sp.dma_start(dst, src).then_inc(raw_in[c.i % RAW], 16)

            load(chunks[0])
            sp.dma_start(h[:, :, 512:D], x[:, :, 512:D]).then_inc(x_in, 16)
            load(chunks[1])
            sp.dma_start(cst[:, P:C_KEEP], t["cst"][:, P:C_KEEP]).then_inc(const_in, 16)
            sp.dma_start(stage[:, :], t["cst"][:, C_KEEP:C_ALL]).then_inc(masks_in, 16)
            sp.dma_start(posi[:, :], t["positions_2"][0].rearrange("(m p) -> p m", p=P)).then_inc(small_in, 16)
            sp.dma_start(sinks[:, 0, :], t["sinks_a"][0].partition_broadcast(P)).then_inc(sinks_in, 16)
            load(chunks[2])
            for i in range(2):
                for n, name in enumerate(("dt_bias_2", "a_log_2", "d_skip_2")):
                    sp.dma_start(small[:, i, n, :], t[name][i].partition_broadcast(P)).then_inc(small_in, 16)
                for tap in range(4):
                    sp.dma_start(convw[:, i, tap, :], t["conv_w_2"][i, tap].rearrange("(c p) -> p c", p=P))\
                      .then_inc(small_in, 16)
                sp.dma_start(convb[:, i, :], t["conv_b_2"][i].rearrange("(c p) -> p c", p=P)).then_inc(small_in, 16)
            for s in sc.steps:
                if s.kind == "chunk" and s.i + RAW < len(chunks):
                    load(chunks[s.i + RAW])
            for i in range(M):
                sp.wait_ge(sem["final", "vector"], M + i + 1)
                sp.dma_start(t["out"][0, i * P:(i + 1) * P, :], h[:, i, :]).then_inc(out_done, 16)
            sp.wait_ge(out_done, 16 * M)

    @blk.tensor
    def _(pe):
        def transpose(out, in_):
            return nc.tensor.transpose(out, in_, ident)

        pe.wait_ge(const_in, 16)
        for s in sc.steps:
            if s.kind in ("chunk", "rest"):
                c, half = (s, 0) if s.kind == "chunk" else (s.of, 1)
                for x in c.needs[half]:
                    ended(pe, x, "vector")
                if half == 0:
                    pe.wait_ge(sem["chunk", "vector"], c.i + 1)
                src = {"x": xT, "o": oT, "h": hT}
                r = c.i % SPLIT
                per = len(c.outs) // 2
                for n, (b, wd, ts, m) in enumerate(c.outs[half * per:(half + 1) * per]):
                    if c.first and b["before"]:
                        e = b["before"]["evac"][m]
                        ended(pe, e, "vector" if e.kind in ("added", "ev_up") else "scalar")
                    bank = psum[2 * b["pair"] + m]
                    for i, (name, k, off) in enumerate(ts):
                        still = [x[:, k, m * P:(m + 1) * P] for x in src[name]]
                        for j, (a, mv) in enumerate(((0, hi), (0, lo), (1, hi))):
                            last = nc.tensor.matmul(
                                bank[:, 0:wd], still[a], mv[r][:, off:off + wd],
                                start=c.first and i == 0 and j == 0,
                                stop=c.last and i == len(ts) - 1 and j == 2)
                    if c.last and (half == 0 or n < per - 1):
                        last.then_inc(part_done, 1)
                if half:
                    last.then_inc(sem["chunk", "tensor"], 1)
            elif s.kind == "turn":
                ended(pe, s.src, "vector")
                bank = freed(pe, s.bank)
                q = quarter[s.src.buf]
                for i in range(4):
                    j = (i % 2) * 2 + i // 2 if s.dst == "h" else i
                    last = transpose(bank[:, i * P:(i + 1) * P], q[:, j * P:(j + 1) * P])
                last.then_inc(sem["turn", "tensor"], 1)
            elif s.kind == "turn_k":
                B = A if s.rope.kind_of != "h" else Hb
                ended(pe, s.rope, "vector")
                bank = freed(pe, s.bank)
                for g in range(2):
                    for m in range(M):
                        kd = B["kdup"][:, m, 2 * s.t + g, :, :].rearrange("p a d -> p (a d)")
                        last = transpose(bank[:, (2 * g + m) * P:(2 * g + m + 1) * P], kd)
                last.then_inc(sem["turn_k", "tensor"], 1)
            elif s.kind == "turn_q":
                B = A if s.rope.kind_of != "h" else Hb
                ended(pe, s.rope, "vector")
                bank = freed(pe, s.bank)
                for g in range(2):
                    for m in range(M):
                        c0 = s.j * 512 + (2 * s.t + g) * P
                        last = transpose(bank[:, (2 * g + m) * P:(2 * g + m + 1) * P], B["q"][:, m, c0:c0 + P])
                last.then_inc(sem["turn_q", "tensor"], 1)
            elif s.kind == "scores":
                a, hd = s.att, s.head
                B = Hb if a["kind"] == "h" else A
                kv = hd // (a["heads"] // a["nkv"])
                ended(pe, a["tk"][-1], "scalar")
                ended(pe, a["tq"][hd // 4], "scalar")
                bank = freed(pe, s.bank)
                mk = {"a": 0, "b": 1, "h": 2}[a["kind"]]
                nc.tensor.matmul(bank[:, 0:QC], identb[:, :], masks[:, mk * QC:(mk + 1) * QC], start=True, stop=False)
                r = 64 * (hd % 2)
                q, k = B["qT"], B["kT"]
                nc.tensor.matmul(bank[:, 0:P], q[r:r + 64, hd // 2, 0:P], k[r:r + 64, kv, 0:P], start=False, stop=False)
                nc.tensor.matmul(bank[:, P:QC], q[r:r + 64, hd // 2, P:S], k[r:r + 64, kv, 0:S],
                                 start=False, stop=True).then_inc(sem["scores", "tensor"], 1)
            elif s.kind == "flip":
                a = s.att
                B = Hb if a["kind"] == "h" else A
                ended(pe, a["scores"][s.head], "scalar")
                bank = freed(pe, s.bank)
                pr = B[f"prob{s.p % 2}"]
                for i in range(3):
                    last = transpose(bank[:, i * P:(i + 1) * P], pr[:, i * P:(i + 1) * P])
                last.then_inc(sem["flip", "tensor"], 1)
            elif s.kind == "pv":
                a, hd = s.att, s.head
                B = Hb if a["kind"] == "h" else A
                kv = hd // (a["heads"] // a["nkv"])
                ended(pe, a["flip"][hd], "vector")
                bank = freed(pe, s.bank) if hd % 2 == 0 else psum[4 + s.bank.at]
                pt, v = B[f"probT{s.p % 2}"], B["v1"]
                W1 = HD + 1
                c0 = (hd % 2) * 2 * W1
                nc.tensor.matmul(bank[:, c0:c0 + W1], pt[:, 0:P], v[:, 0, kv, :], start=True, stop=True)
                nc.tensor.matmul(bank[:, c0 + W1:c0 + 2 * W1], pt[:, P:2 * P], v[:, 0, kv, :], start=True, stop=False)
                nc.tensor.matmul(bank[:, c0 + W1:c0 + 2 * W1], pt[:, 2 * P:QC], v[:, 1, kv, :],
                                 start=False, stop=True).then_inc(sem["pv", "tensor"], 1)
            elif s.kind == "sums":
                ended(pe, s.before, "vector")
                bank = freed(pe, s.bank)
                da = Hb["da"][:, :, :].rearrange("p m s -> p (m s)")
                nc.tensor.matmul(bank[:, 0:32], upper, da, start=True, stop=True)
                nc.tensor.matmul(bank[:, 32:64], ones[:, :], da, start=True, stop=True)\
                  .then_inc(sem["sums", "tensor"], 1)
            elif s.kind == "conv":
                ended(pe, s.ev, "scalar")
                for u in range(2):
                    bank = freed(pe, s.banks[u])
                    for i in range(2):
                        for m in range(M):
                            c0 = (2 * u + i) * P
                            last = transpose(bank[:, (2 * i + m) * P:(2 * i + m + 1) * P], Hb["xin"][:, m, c0:c0 + P])
                last.then_inc(sem["conv", "tensor"], 1)
            elif s.kind == "bback":
                ended(pe, s.conv, "scalar")
                ct = Hb["cT"]
                bank = freed(pe, s.banks[0])
                for m in range(M):
                    for g in range(2):
                        c0 = (2 * m + g) * P
                        nc.tensor.matmul(bank[:, c0:c0 + P], ct[:, 8 + g, m * P:(m + 1) * P],
                                         ct[:, 10 + g, m * P:(m + 1) * P], start=True, stop=True)
                bank = freed(pe, s.banks[1])
                for g in range(2):
                    last = transpose(bank[:, g * P:(g + 1) * P], ct[:, 8 + g, 0:P])
                last.then_inc(sem["bback", "tensor"], 1)
            elif s.kind == "xback":
                ended(pe, s.conv, "scalar")
                for m in range(M):
                    bank = freed(pe, s.banks[m])
                    for i in range(4):
                        last = transpose(bank[:, i * P:(i + 1) * P], Hb["cT"][:, 4 * s.j + i, m * P:(m + 1) * P])
                last.then_inc(sem["xback", "tensor"], 1)
            elif s.kind == "state":
                ended(pe, s.xback, "gpsimd")
                ended(pe, s.bback, "scalar")
                bank = freed(pe, s.bank)
                nc.tensor.matmul(bank[:, :], Hb["bt"][:, s.g, :], Hb["xgd"][:, s.g * 512:(s.g + 1) * 512],
                                 start=True, stop=True).then_inc(sem["state", "tensor"], 1)
            elif s.kind == "decay":
                m, g = s.mg
                ended(pe, s.sums, "scalar")
                bank = freed(pe, s.bank)
                for i in range(4):
                    hh = 8 * g + 4 * (s.q % 2) + i
                    seg = bank[:, i * P:(i + 1) * P]
                    nc.tensor.matmul(seg, identb[:, :], masks[:, 3 * QC:3 * QC + P], start=True, stop=False)
                    last = nc.tensor.matmul(seg, spread(Hb["da"][:, m, hh:hh + 1], [P, P]), upper,
                                            start=False, stop=True)
                last.then_inc(sem["decay", "tensor"], 1)
            elif s.kind == "diag":
                ended(pe, s.decay, "vector")
                ended(pe, s.xback, "gpsimd")
                bank = freed(pe, s.bank) if s.i % 2 == 0 else psum[4 + s.bank.at]
                for i in range(4):
                    hh = 8 * s.g + 4 * (s.q % 2) + i
                    c0 = (4 * (s.q % 2) + i) * HD
                    last = nc.tensor.matmul(bank[:, c0:c0 + HD], Hb[f"MT{s.decay.i % 2}"][:, i, :],
                                            Hb["xg"][:, s.m, hh * HD:(hh + 1) * HD], start=True, stop=True)
                last.then_inc(sem["diag", "tensor"], 1)
            elif s.kind == "off":
                ended(pe, s.state, "scalar")
                bank = freed(pe, s.bank)
                nc.tensor.matmul(bank[:, :], Hb["cT"][:, 10 + s.g, P:S], Hb["st"][:, s.g * 512:(s.g + 1) * 512],
                                 start=True, stop=True).then_inc(sem["off", "tensor"], 1)

    @blk.scalar
    def _(act):
        def split(c):
            act.wait_ge(raw_in[c.i % RAW], arrived[c.i])
            if c.i >= SPLIT:
                act.wait_ge(sem["chunk", "tensor"], c.i - SPLIT + 1)
            nc.scalar.activation(hi[c.i % SPLIT][:, 0:c.size], raw[c.i % RAW][:, 0:c.size], ACT.Copy)\
              .then_inc(sem["chunk", "scalar"], 1)

        def done(ins, s):
            ins.then_inc(sem[s.kind, "scalar"], 1)

        junked = []

        def square_sum(x, out, s):
            if junked:
                ended(act, junked[-1], "scalar")
            done(nc.scalar.activation(junk[:, :], x, ACT.Square, accum_out=out), s)
            junked.append(s)

        act.wait_ge(x_first, 16)
        act.wait_ge(x_in, 16)
        for s in sc.steps:
            if s.kind in ("chunk", "rest"):
                if s.kind == "chunk" and s.i == SETUP_AT:
                    act.wait_ge(setup_dve, 2)
                    nc.scalar.activation(sine[:, :, :, :], angle[:, :, :, :], ACT.Sin).then_inc(setup_act, 1)
                    nc.scalar.activation(small[:, :, 1, :], small[:, :, 1, :], ACT.Exp).then_inc(setup_act, 1)
                for i in due(s):
                    if i < len(chunks):
                        split(chunks[i])
            elif s.kind == "turn":
                act.wait_ge(sem["turn", "tensor"], s.i + 1)
                bank = psum[4 + s.bank.at]
                if s.dst == "h":
                    out = hT[0][:, s.k0:s.k0 + 2, :].rearrange("p k t -> p (k t)")
                    done(nc.scalar.activation(out, bank[:, :], ACT.Copy), s)
                else:
                    dst = (xT if s.dst == "x" else oT)[0]
                    done(nc.scalar.activation(dst[:, s.k0:s.k0 + 4, s.m * P:(s.m + 1) * P],
                                              bank[:, :].rearrange("p (k t) -> p k t", k=4), ACT.Copy), s)
            elif s.kind == "square":
                if s.added is not None:
                    ended(act, s.added, "vector")
                square_sum(h[:, s.m, s.n * 512:(s.n + 1) * 512], sumsq[:, 2 * s.m + s.n:2 * s.m + s.n + 1], s)
            elif s.kind == "ev_kv":
                ended(act, s.rstd, "vector")
                bank = ready(act, s.block, s.m)
                B = Hb if s.dt is not None else A
                rs = rms[:, 1, s.m:s.m + 1]
                kw = s.nkv * HD
                nc.scalar.activation(B["k"][:, s.m, 0:s.nkv, :], bank[:, 0:kw].rearrange("p (g d) -> p g d", d=HD),
                                     ACT.Copy, scale=rs)
                if s.dt is not None:
                    nc.scalar.activation(B["dtr"][:, s.m, :], bank[:, 256:272], ACT.Copy, scale=rs)
                done(nc.scalar.activation(B["v1"][:, s.m, 0:s.nkv, 0:HD],
                                          bank[:, kw:2 * kw].rearrange("p (g d) -> p g d", d=HD),
                                          ACT.Copy, scale=rs), s)
            elif s.kind == "ev_q":
                ended(act, s.rstd, "vector")
                if s.i == 0:
                    act.wait_ge(setup_dve, 1)
                bank = ready(act, s.block, s.m)
                B = Hb if s.kind_of == "h" else A
                done(nc.scalar.activation(B["q"][:, s.m, s.j * 512:(s.j + 1) * 512], bank[:, :], ACT.Copy,
                                          scale=rms[:, 1, s.m:s.m + 1]), s)
            elif s.kind == "ev_z":
                bank = ready(act, s.block, s.m)
                B = Hb if s.kind_of == "h" else A
                done(nc.scalar.activation(B["z"][:, s.m, s.j * 512:(s.j + 1) * 512], bank[:, :], ACT.Silu,
                                          scale=rms[:, 1, s.m:s.m + 1]), s)
            elif s.kind == "ev_x":
                bank = ready(act, s.block, s.m)
                if s.conv is not None:
                    ended(act, s.conv, "tensor")
                done(nc.scalar.activation(Hb["xin"][:, s.m, :], bank[:, :], ACT.Copy,
                                          scale=rms[:, 1, s.m:s.m + 1]), s)
            elif s.kind == "ev_up":
                ended(act, s.rstd, "vector")
                if s.i >= 2:
                    act.wait_ge(sem["ev_up", "vector"], s.i - 1)
                for m in range(M):
                    bank = ready(act, s.block, m)
                    last = nc.scalar.activation(sil[s.i % 2][:, m, :], bank[:, 0:UPW], ACT.Silu,
                                                scale=rms[:, 1, m:m + 1])
                done(last, s)
            elif s.kind == "turn_k":
                B = A if s.rope.kind_of != "h" else Hb
                act.wait_ge(sem["turn_k", "tensor"], s.i + 1)
                done(nc.scalar.activation(B["kT"][:, 2 * s.t:2 * s.t + 2, :],
                                          psum[4 + s.bank.at][:, :].rearrange("p (g t) -> p g t", g=2), ACT.Copy), s)
            elif s.kind == "turn_q":
                B = A if s.rope.kind_of != "h" else Hb
                act.wait_ge(sem["turn_q", "tensor"], s.i + 1)
                c0 = 4 * s.j + 2 * s.t
                done(nc.scalar.activation(B["qT"][:, c0:c0 + 2, :],
                                          psum[4 + s.bank.at][:, :].rearrange("p (g t) -> p g t", g=2), ACT.Copy), s)
            elif s.kind == "scores":
                a, hd = s.att, s.head
                B = Hb if a["kind"] == "h" else A
                act.wait_ge(sem["scores", "vector"], s.i + 1)
                if s.i >= 2:
                    act.wait_ge(sem["flip", "tensor"], s.i - 1)
                bank, pr = psum[4 + s.bank.at], B[f"prob{s.p % 2}"]
                nc.scalar.activation(pr[:, 0:P], bank[:, 0:P], ACT.Exp, scale=SCALE, bias=shift[:, hd, 0:1])
                done(nc.scalar.activation(pr[:, P:QC], bank[:, P:QC], ACT.Exp, scale=SCALE,
                                          bias=shift[:, hd, 1:2]), s)
            elif s.kind == "oev":
                a = s.att
                B = Hb if a["kind"] == "h" else A
                ended(act, s.pv, "tensor")
                W1 = HD + 1
                src = psum[4 + s.bank.at][:, 0:4 * W1].rearrange("p (g m d) -> p m g d", g=2, m=2)
                done(nc.scalar.activation(B["o"][:, :, 2 * s.pair:2 * s.pair + 2, :], src, ACT.Copy), s)
            elif s.kind == "sink":
                act.wait_ge(sem["sink", "vector"], s.i + 1)
                e = esink[:, 8 * s.half:8 * s.half + 8, :]
                done(nc.scalar.activation(e, e, ACT.Exp), s)
            elif s.kind == "soft1":
                act.wait_ge(sem["soft1", "vector"], s.i + 1)
                done(nc.scalar.activation(Hb["sb"][:, :, :], Hb["sb"][:, :, :], ACT.Exp, scale=-1.0), s)
            elif s.kind == "soft2":
                act.wait_ge(sem["soft2", "vector"], s.i + 1)
                done(nc.scalar.activation(Hb["sd"][:, :, :], Hb["sc"][:, :, :], ACT.Ln), s)
            elif s.kind == "sums":
                act.wait_ge(sem["sums", "vector"], s.i + 1)
                nc.scalar.activation(Hb["dec"][:, :], Hb["dif"][:, :], ACT.Exp)
                done(nc.scalar.activation(Hb["ecs"][:, :], Hb["ncs"][:, 1, :], ACT.Exp, scale=-1.0), s)
            elif s.kind == "conv":
                act.wait_ge(sem["conv", "vector"], s.i + 1)
                for i in range(4):
                    ct = (8 + i) if s.j == 0 else 4 * (s.j - 1) + i
                    last = nc.scalar.activation(Hb["cT"][:, ct, :], Hb[f"acc{i // 2}"][:, i % 2, :], ACT.Silu,
                                                bias=convb[:, s.layer, ct:ct + 1])
                done(last, s)
            elif s.kind == "bback":
                act.wait_ge(sem["bback", "tensor"], s.i + 1)
                nc.scalar.activation(Hb["cb"][:, :, :, :].rearrange("p m g l -> p (m g l)"),
                                     psum[4 + s.banks[0].at][:, :], ACT.Copy)
                done(nc.scalar.activation(Hb["bt"][:, :, :].rearrange("p g n -> p (g n)"),
                                          psum[4 + s.banks[1].at][:, 0:2 * P], ACT.Copy), s)
            elif s.kind == "xback":
                act.wait_ge(sem["xback", "tensor"], s.i + 1)
                for m in range(M):
                    last = nc.scalar.activation(Hb["xs"][:, m, s.j * 512:(s.j + 1) * 512],
                                                psum[4 + s.banks[m].at][:, :], ACT.Copy)
                done(last, s)
            elif s.kind == "state":
                act.wait_ge(sem["state", "tensor"], s.i + 1)
                done(nc.scalar.activation(Hb["st"][:, s.g * 512:(s.g + 1) * 512], psum[4 + s.bank.at][:, :],
                                          ACT.Copy), s)
            elif s.kind == "decay":
                m, g = s.mg
                act.wait_ge(sem["decay", "tensor"], s.i + 1)
                if s.i >= 2:
                    act.wait_ge(sem["decay", "vector"], s.i - 1)
                for i in range(4):
                    hh = 8 * g + 4 * (s.q % 2) + i
                    last = nc.scalar.activation(Hb[f"E{s.i % 2}"][:, i, :], psum[4 + s.bank.at][:, i * P:(i + 1) * P],
                                                ACT.Exp, bias=Hb["ncs"][:, m, hh:hh + 1])
                done(last, s)
            elif s.kind == "join":
                act.wait_ge(sem["join", "vector"], s.i + 1)
                square_sum(Hb["xs"][:, s.m, s.g * 512:(s.g + 1) * 512], rmy[:, 0, 2 * s.g + s.m:2 * s.g + s.m + 1], s)

    @blk.gpsimd
    def _(pool):
        def row(name, layer):
            whole = {"final": t["final_norm_2"], "final_g": t["final_g"]}
            return (whole[name] if name in whole else gain_rows[name][layer]).partition_broadcast(P)

        def load_gain(g):
            if g["i"]:
                ended(pool, sc.gains[g["i"] - 1]["users"][-1], "vector")
            pool.dma_start(gains[:, :], row(*g["src"])).then_inc(gain_in, 16)

        load_gain(sc.gains[0])
        nc.gpsimd.memset(power[:, :], -0.5).then_inc(chain["gpsimd"], 1)
        links["gpsimd"] += 1
        pool.wait_ge(chain["gpsimd"], links["gpsimd"])
        after = {id(sc.gains[g["i"] - 1]["users"][-1]): g for g in sc.gains[1:] if g["src"] is not None}
        for s in sc.steps:
            if id(s) in after:
                load_gain(after[id(s)])
            if s.kind == "mid_load":
                ended(pool, s.before, "tensor")
                for i, name in enumerate(("final_g", "norm_mix")):
                    pool.dma_start(mid_rows[i][:, :], row(name, 0)).then_inc(mid_in, 16)
            if s.kind == "meansq":
                pool.wait_ge(sem["meansq", "vector"], s.i + 1)
                _, ms, rs, _ = norm_parts(s)
                nc.gpsimd.tensor_tensor(rs, ms, power[:, :], ALU.pow).then_inc(sem["meansq", "gpsimd"], 1)
            if s.kind != "xback":
                continue
            pool.wait_ge(sem["xback", "scalar"], s.i + 1)
            ended(pool, s.sums, "scalar")
            hs, cols = slice(8 * s.j, 8 * s.j + 8), slice(s.j * 512, (s.j + 1) * 512)
            for m in range(M):
                xs = Hb["xs"][:, m, cols].rearrange("p (s d) -> p s d", d=HD)
                xg = Hb["xg"][:, m, cols].rearrange("p (s d) -> p s d", d=HD)
                link(pool, "gpsimd", nc.gpsimd.tensor_tensor(
                    xg, xs, spread(Hb["dt"][:, m, hs].unsqueeze(2), [P, 8, HD]), ALU.mult))
                link(pool, "gpsimd", nc.gpsimd.tensor_tensor(
                    xs, xs, spread(small[:, s.conv.layer, 2, hs].unsqueeze(2), [P, 8, HD]), ALU.mult))
            nc.gpsimd.tensor_tensor(
                Hb["xgd"][:, cols].rearrange("p (s d) -> p s d", d=HD),
                Hb["xg"][:, 0, cols].rearrange("p (s d) -> p s d", d=HD),
                spread(Hb["dec"][:, hs].unsqueeze(2), [P, 8, HD]), ALU.mult).then_inc(sem["xback", "gpsimd"], 1)

    @blk.vector
    def _(dve):
        tt, ts, stt = nc.vector.tensor_tensor, nc.vector.tensor_scalar, nc.vector.scalar_tensor_tensor

        def chained(ins):
            link(dve, "vector", ins)

        def split(c):
            dve.wait_ge(sem["chunk", "scalar"], c.i + 1)
            r = c.i % SPLIT
            tt(lo[r][:, 0:c.size], raw[c.i % RAW][:, 0:c.size], hi[r][:, 0:c.size].bitcast(F32), ALU.subtract)\
              .then_inc(sem["chunk", "vector"], 1)

        def done(ins, s):
            ins.then_inc(sem[s.kind, "vector"], 1)

        def rope(x, cos, sin, t1, t2, half):
            tt(t1, x, cos, ALU.mult)
            tt(t2[..., 0:half], x[..., half:2 * half], sin[..., 0:half], ALU.mult)
            chained(tt(t2[..., half:2 * half], x[..., 0:half], sin[..., half:2 * half], ALU.mult))
            return tt(x, t1, t2, ALU.add)

        rotated = [None]

        def rotate(B, x, m, n, kind):
            if kind == "h":
                cos = spread(trig[:, m, 0, :].unsqueeze(1), [P, n, 16])
                sin = spread(trig[:, m, 1, :].unsqueeze(1), [P, n, 16])
                x, wd, half = x[:, :, 0:16], 16, 8
            else:
                cos = spread(cst[:, C_COS + m * HD:C_COS + (m + 1) * HD].unsqueeze(1), [P, n, HD])
                sin = spread(cst[:, C_SIN + m * HD:C_SIN + (m + 1) * HD].unsqueeze(1), [P, n, HD])
                wd, half = HD, HD // 2
            if rotated[0] is not None:
                ended(dve, rotated[0], "vector")
                rotated[0] = None
            t1 = B["rot1"][:, 0:n * wd].rearrange("p (a d) -> p a d", d=wd)
            t2 = B["rot2"][:, 0:n * wd].rearrange("p (a d) -> p a d", d=wd)
            return rope(x, cos, sin, t1, t2, half)

        def set_up():
            dve.wait_ge(const_in, 32)
            dve.wait_ge(masks_in, 16)
            dve.wait_ge(sinks_in, 16)
            nc.vector.memset(ones[:, :], 1.0)
            ts(sinks[:, 1, :], sinks[:, 0, :], -1.0, None, ALU.mult)
            nc.vector.tensor_copy(identb[:, :], ident)
            chained(nc.vector.tensor_copy(masks[:, :], stage[:, :]))
            nc.vector.memset(A["v1"][:, :, :, :], 1.0).then_inc(setup_dve, 1)

        def angles():
            dve.wait_ge(small_in, 16 * NSMALL)
            chained(nc.vector.tensor_copy(posf[:, :], posi[:, :]))
            two_pi = 2 * math.pi
            c1 = 6.28125
            c2 = float(np.float32(two_pi - c1))
            for m in range(M):
                for f in range(2):
                    last = ts(angle[:, m, f, :], cst[:, C_INV:C_INV + 8], posf[:, m:m + 1], None, ALU.mult)
            chained(last)
            for f in range(2):
                last = ts(turns[:, :, f, :], angle[:, :, f, :], 1.0 / two_pi, 0.25 * (1 - f), ALU.mult, ALU.add)
            chained(last)
            chained(ts(turns[:, :, :, :], turns[:, :, :, :], 12582912.0, None, ALU.add))
            chained(ts(turns[:, :, :, :], turns[:, :, :, :], 12582912.0, None, ALU.subtract))
            for c in (c1, c2, two_pi - c1 - c2):
                chained(stt(angle[:, :, :, :], turns[:, :, :, :], -c, angle[:, :, :, :], ALU.mult, ALU.add))
            chained(ts(angle[:, :, 0, :], angle[:, :, 0, :], math.pi / 2, None, ALU.add))
            lim = float(np.nextafter(np.float32(math.pi), np.float32(0)))
            ts(angle[:, :, :, :], angle[:, :, :, :], lim, -lim, ALU.min, ALU.max).then_inc(setup_dve, 1)

        def tables():
            dve.wait_ge(setup_act, 2)
            for f, sign in enumerate((1.0, -1.0)):
                ts(trig[:, :, f, 0:8], sine[:, :, f, :], sign, None, ALU.mult)
                ts(trig[:, :, f, 8:16], sine[:, :, f, :], 1.0, None, ALU.mult)
            chained(ts(small[:, :, 1, :], small[:, :, 1, :], -1.0, None, ALU.mult))

        dve.wait_ge(x_first, 16)
        for s in sc.steps:
            if s.kind in ("chunk", "rest"):
                if s.kind == "rest" and s.i == 1:
                    set_up()
                if s.kind == "chunk" and s.i == SETUP_AT:
                    angles()
                if s.kind == "chunk" and s.i == SETUP_AT + 1:
                    tables()
                for i in due(s):
                    if i < len(chunks):
                        split(chunks[i])
            elif s.kind == "mid_gain":
                dve.wait_ge(mid_in, 32)
                done(tt(gains[:, :], mid_rows[0][:, :], mid_rows[1][:, :], ALU.mult), s)
            elif s.kind == "gained":
                if s.gain["made"]:
                    ended(dve, s.gain["made"], "vector")
                else:
                    dve.wait_ge(gain_in, 16 * s.gain["loaded"])
                if s.i == 2:
                    dve.wait_ge(x_in, 16)
                if s.added is not None:
                    ended(dve, s.added, "vector")
                if s.before is not None:
                    ended(dve, s.before, "tensor")
                c = slice(s.n * 512, (s.n + 1) * 512)
                done(tt(quarter[s.buf][:, :], h[:, s.m, c], gains[:, c], ALU.mult), s)
            elif s.kind == "turn":
                dve.wait_ge(sem["turn", "scalar"], s.i + 1)
                bank = psum[4 + s.bank.at]
                if s.dst == "h":
                    a, b = (x[:, s.k0:s.k0 + 2, :].rearrange("p k t -> p (k t)") for x in hT)
                    done(tt(b, bank[:, :], a.bitcast(F32), ALU.subtract), s)
                else:
                    a, b = (x[:, s.k0:s.k0 + 4, s.m * P:(s.m + 1) * P] for x in (xT if s.dst == "x" else oT))
                    done(tt(b, bank[:, :].rearrange("p (k t) -> p k t", k=4), a.bitcast(F32), ALU.subtract), s)
            elif s.kind == "meansq":
                sq, ms, _, _ = norm_parts(s)
                if s.what == "y":
                    dve.wait_ge(sem["join", "scalar"], s.of)
                    done(ts(ms, sq, 1.0 / 512, EPS, ALU.mult, ALU.add), s)
                else:
                    dve.wait_ge(sem["square", "scalar"], s.of)
                    q = sumsq[:, :].rearrange("p (m n) -> p m n", n=2)
                    chained(tt(ms, q[:, :, 0], q[:, :, 1], ALU.add))
                    done(ts(ms, ms, 1.0 / D, EPS, ALU.mult, ALU.add), s)
            elif s.kind == "newton":
                ended(dve, s.before, "gpsimd")
                _, ms, rs, y = norm_parts(s)
                chained(tt(y, rs, rs, ALU.mult))
                chained(tt(y, y, ms, ALU.mult))
                chained(ts(y, y, -0.5, 1.5, ALU.mult, ALU.add))
                last = tt(rs, rs, y, ALU.mult)
                if s.what == "both":
                    chained(last)
                    last = tt(rs, rs, rms[:, 2, :], ALU.mult)
                done(last, s)
            elif s.kind == "added":
                bank = ready(dve, s.block, s.m)
                x = h[:, s.m, s.n * 512:(s.n + 1) * 512]
                done(tt(x, bank[:, :], x, ALU.add), s)
            elif s.kind == "ev_up":
                dve.wait_ge(sem["ev_up", "scalar"], s.i + 1)
                if s.before is not None:
                    ended(dve, s.before, "tensor")
                for m in range(M):
                    last = stt(quarter[s.buf][:, m * UPW:(m + 1) * UPW], psum[2 * s.block["pair"] + m][:, UPW:2 * UPW],
                               rms[:, 1, m:m + 1], sil[s.i % 2][:, m, :], ALU.mult, ALU.mult)
                done(last, s)
            elif s.kind == "rope_k":
                B = Hb if s.kind_of == "h" else A
                ended(dve, s.ev, "scalar")
                if s.kind_of == "h":
                    nc.vector.memset(B["v1"][:, :, :, HD:HD + 1], 1.0)
                for m in range(M):
                    x = B["k"][:, m, 0:s.nkv, :]
                    chained(rotate(B, x, m, s.nkv, s.kind_of))
                    for a in range(2):
                        last = nc.vector.tensor_copy(B["kdup"][:, m, 0:s.nkv, a, :], x)
                done(last, s)
            elif s.kind == "rope_q":
                B = Hb if s.kind_of == "h" else A
                ended(dve, s.ev, "scalar")
                for m in range(M):
                    x = B["q"][:, m, s.j * 512:(s.j + 1) * 512].rearrange("p (a d) -> p a d", d=HD)
                    last = rotate(B, x, m, 8, s.kind_of)
                    if m == 0:
                        chained(last)
                done(last, s)
                rotated[0] = s
            elif s.kind == "scores":
                a, hd = s.att, s.head
                dve.wait_ge(sem["scores", "tensor"], s.i + 1)
                rm = rowmax[:, s.i % 2, :]
                chained(nc.vector.tensor_reduce(rm[:, 0:3], psum[4 + s.bank.at][:, 0:QC].rearrange("p (a k) -> p a k", a=3),
                                                AXX, ALU.max))
                chained(tt(rm[:, 1:2], rm[:, 1:2], rm[:, 2:3], ALU.max))
                if a["kind"] == "a":
                    done(ts(shift[:, hd, :], rm[:, 0:2], -SCALE, sinks[:, 1, hd:hd + 1], ALU.mult, ALU.min), s)
                else:
                    done(ts(shift[:, hd, :], rm[:, 0:2], -SCALE, None, ALU.mult), s)
            elif s.kind == "flip":
                a = s.att
                B = Hb if a["kind"] == "h" else A
                dve.wait_ge(sem["flip", "tensor"], s.i + 1)
                if s.i >= 2:
                    dve.wait_ge(sem["pv", "tensor"], s.i - 1)
                pt, bank = B[f"probT{s.p % 2}"], psum[4 + s.bank.at]
                if a["kind"] == "h":
                    done(tt(pt[:, :], bank[:, 0:QC], mult, ALU.mult), s)
                else:
                    done(nc.vector.tensor_copy(pt[:, :], bank[:, 0:QC]), s)
            elif s.kind == "sink":
                dve.wait_ge(sem["scores", "vector"], s.att["scores"][8 * s.half + 7].i + 1)
                e = slice(8 * s.half, 8 * s.half + 8)
                done(tt(esink[:, e, :], shift[:, e, :], spread(sinks[:, 0, e].unsqueeze(2), [P, 8, M]), ALU.add), s)
            elif s.kind == "den":
                B = Hb if s.att["kind"] == "h" else A
                ended(dve, s.oev, "scalar")
                d = B["o"][:, :, 8 * s.half:8 * s.half + 8, HD]
                if s.es is not None:
                    ended(dve, s.es, "scalar")
                    e = esink[:, 8 * s.half:8 * s.half + 8, :].rearrange("p s m -> p m s")
                    chained(tt(dens[:, :, :], d, e, ALU.add))
                    d = dens[:, :, :]
                done(nc.vector.reciprocal(dens[:, :, :], d), s)
            elif s.kind == "gate":
                B = Hb if s.att["kind"] == "h" else A
                if s.before is not None:
                    ended(dve, s.before, "tensor")
                ended(dve, s.den, "vector")
                q = quarter[s.buf][:, :]
                o = B["o"][:, s.m, 8 * s.half:8 * s.half + 8, 0:HD]
                first = tt(q.rearrange("p (a d) -> p a d", d=HD), o, spread(dens[:, s.m, :].unsqueeze(2), [P, 8, HD]),
                           ALU.mult)
                if s.z is None:
                    done(first, s)
                else:
                    chained(first)
                    ended(dve, s.z, "scalar")
                    done(tt(q, q, B["z"][:, s.m, s.half * 512:(s.half + 1) * 512], ALU.mult), s)
            elif s.kind == "soft1":
                ended(dve, s.ev, "scalar")
                for m in range(M):
                    last = tt(Hb["dtr"][:, m, :], Hb["dtr"][:, m, :], small[:, s.layer, 0, :], ALU.add)
                chained(last)
                ts(Hb["sa"][:, :, :], Hb["dtr"][:, :, :], 0.0, None, ALU.max)
                done(stt(Hb["sb"][:, :, :], Hb["dtr"][:, :, :], -1.0, Hb["dtr"][:, :, :], ALU.mult, ALU.max), s)
            elif s.kind == "soft2":
                ended(dve, s.before, "scalar")
                done(ts(Hb["sc"][:, :, :], Hb["sb"][:, :, :], 1.0, None, ALU.add), s)
            elif s.kind == "soft3":
                ended(dve, s.before, "scalar")
                e, u, l, dt = (Hb[x][:, :, :] for x in ("sb", "sc", "sd", "dt"))
                same = Hb["dtr"][:, :, :]
                ts(same, u, 1.0, None, ALU.is_equal)
                chained(ts(dt, u, 1.0, None, ALU.subtract))
                chained(tt(dt, dt, same, ALU.add))
                chained(tt(l, l, same, ALU.add))
                chained(nc.vector.reciprocal(dt, dt))
                chained(tt(l, l, e, ALU.mult))
                chained(tt(dt, dt, l, ALU.mult))
                chained(tt(dt, dt, Hb["sa"][:, :, :], ALU.add))
                for m in range(M):
                    last = tt(Hb["da"][:, m, :], Hb["dt"][:, m, :], small[:, s.layer, 1, :], ALU.mult)
                done(last, s)
            elif s.kind == "sums":
                dve.wait_ge(sem["sums", "tensor"], s.i + 1)
                bank = psum[4 + s.bank.at]
                chained(ts(Hb["ncs"][:, :, :].rearrange("p m s -> p (m s)"), bank[:, 0:32], -1.0, None, ALU.mult))
                done(tt(Hb["dif"][:, :], bank[:, 32:48], Hb["ncs"][:, 0, :], ALU.add), s)
            elif s.kind == "conv":
                dve.wait_ge(sem["conv", "tensor"], s.i + 1)
                if s.i % 3:
                    dve.wait_ge(sem["conv", "scalar"], s.i)
                cw = convw[:, s.layer, :, :]

                def bank_of(i):
                    return psum[4 + s.banks[i // 2].at][:, (i % 2) * S:(i % 2 + 1) * S]

                for tap in range(4):
                    for i in range(4):
                        ct = (8 + i) if s.j == 0 else 4 * (s.j - 1) + i
                        acc = Hb[f"acc{i // 2}"][:, i % 2, :]
                        if tap:
                            dve.wait_ge(chain["vector"], links["vector"] - 3)
                            ins = stt(acc[:, tap:S], bank_of(i)[:, 0:S - tap], cw[:, 3 - tap, ct:ct + 1],
                                      acc[:, tap:S], ALU.mult, ALU.add)
                        else:
                            ins = ts(acc, bank_of(i), cw[:, 3, ct:ct + 1], None, ALU.mult)
                        if tap < 3 or i < 3:
                            ins.then_inc(chain["vector"], 1)
                            links["vector"] += 1
                        else:
                            done(ins, s)
            elif s.kind == "decay":
                m, g = s.mg
                ended(dve, s.bback, "scalar")
                dve.wait_ge(sem["decay", "scalar"], s.i + 1)
                if s.i >= 2:
                    dve.wait_ge(sem["diag", "tensor"], s.i - 1)
                done(tt(Hb[f"MT{s.i % 2}"][:, :, :], Hb[f"E{s.i % 2}"][:, :, :],
                        spread(Hb["cb"][:, m, g, :].unsqueeze(1), [P, 4, P]), ALU.mult), s)
            elif s.kind == "join":
                ended(dve, s.last, "tensor")
                ended(dve, s.xback, "gpsimd")
                c = slice(s.g * 512, (s.g + 1) * 512)
                y = Hb["xs"][:, s.m, c]
                chained(tt(y, psum[4 + s.bank.at][:, :], y, ALU.add))
                if s.obank is not None:
                    t_ = Hb["rot1"][:, :]
                    chained(tt(t_.rearrange("p (s d) -> p s d", d=HD),
                               psum[4 + s.obank.at][:, :].rearrange("p (s d) -> p s d", d=HD),
                               spread(Hb["ecs"][:, 8 * s.g:8 * s.g + 8].unsqueeze(2), [P, 8, HD]), ALU.mult))
                    chained(tt(y, y, t_, ALU.add))
                ended(dve, s.z, "scalar")
                done(tt(y, y, Hb["z"][:, s.m, c], ALU.mult), s)
            elif s.kind == "ynorm":
                ended(dve, s.rstd, "vector")
                dve.wait_ge(gain_in, 16 * s.gain["loaded"])
                if s.before is not None:
                    ended(dve, s.before, "tensor")
                c = slice(s.g * 512, (s.g + 1) * 512)
                n = 2 * s.g + s.m
                done(stt(quarter[s.buf][:, :], Hb["xs"][:, s.m, c], rmy[:, 2, n:n + 1], gains[:, c],
                         ALU.mult, ALU.mult), s)
            elif s.kind == "final":
                ended(dve, s.rstd, "vector")
                if s.what == "mid":
                    rs, g = rms[:, 2, s.m:s.m + 1], mid_rows[0]
                else:
                    dve.wait_ge(gain_in, 16 * s.gain["loaded"])
                    rs, g = rms[:, 1, s.m:s.m + 1], gains
                done(stt(h[:, s.m, :], h[:, s.m, :], rs, g[:, :], ALU.mult, ALU.mult), s)

    program.close()


_INS = ["x", "norm_g", "w_in_a", "sinks_a", "w_in_b", "w_out", "positions_2", "norm_mix_2", "w_in_2", "conv_w_2",
        "conv_b_2", "dt_bias_2", "a_log_2", "d_skip_2", "ssm_norm_2", "w_out_2", "norm_ffn_2", "w_gate_2",
        "w_up_2", "w_down_2", "final_norm_2", "final_g"]


def kernel(**inputs):
    from concourse import bacc
    from concourse.bass_utils import run_bass_kernel_spmd

    nc = bacc.Bacc("TRN2", target_bir_lowering=False, num_devices=1)
    arrays, t = {}, {}
    for name in _INS:
        a = np.ascontiguousarray(inputs[name])
        arrays[f"in_{name}"] = a
        t[name] = nc.dram_tensor(f"in_{name}", a.shape, mybir.dt.from_np(a.dtype), kind="ExternalInput").ap()
    c = constants()
    arrays["in_cst"] = c
    t["cst"] = nc.dram_tensor("in_cst", c.shape, F32, kind="ExternalInput").ap()
    t["out"] = nc.dram_tensor("out", (1, S, D), F32, kind="ExternalOutput").ap()
    build(nc, t)
    r = run_bass_kernel_spmd(nc, [arrays], core_ids=[0])
    return r.results[0]["out"]
```

```python
import math
from contextlib import ExitStack

import numpy as np
import concourse.bass as bass
from concourse import mybir

F32 = mybir.dt.float32
F32R = mybir.dt.float32r
BF16 = mybir.dt.bfloat16
I32 = mybir.dt.int32
ALU = mybir.AluOpType
ACT = mybir.ActivationFunctionType
AXX = mybir.AxisListType.X

S, D, P = 256, 1024, 128
M = S // P
KD = D // P
HD = 64
NEG = -1e30
EPS = 1e-5
SCALE = HD ** -0.5
FF = 2816
KF = FF // P
UPW = 256
NUP = FF // UPW
SSM = 1024
CONV = SSM + 512
NST = 128
SH = 16
NCT = CONV // P
RAW, SPLIT = 3, 3
SETUP_AT = 15
AHEAD = 2
CH = 8 * 272
NSCR = 4
QC = 3 * P

C_ID, C_U, C_CT = 0, P, 2 * P
C_COS, C_SIN, C_INV = C_CT + QC, C_CT + QC + 2 * HD, C_CT + QC + 4 * HD
C_KEEP = C_INV + 8
C_MASK = C_KEEP
C_SEL = C_MASK + 3 * QC + P
C_ALL = C_SEL + 32
M_SCAN, M_SEL = 3 * QC, 3 * QC + P


def constants():
    t, u = np.arange(P)[:, None], np.arange(P)[None, :]
    tiles = ((0, 0), (1, 0), (1, 1))
    delta = [t + P * q - u - P * k for q, k in tiles]
    c = np.zeros((P, C_ALL), np.float32)
    c[:, C_ID:C_ID + P] = np.eye(P)
    c[:, C_U:C_U + P] = t <= u
    mult = [(d >= 0) * ((d <= 128).astype(np.float32) + (d % 4 == 0) + (d % 16 == 0)) for d in delta]
    for i, x in enumerate(mult):
        c[:, C_CT + i * P:C_CT + (i + 1) * P] = x.T
    inv = np.float32(10000.0) ** (-np.arange(0, HD, 2, dtype=np.float32) / np.float32(HD))
    for m in range(M):
        ang = (np.arange(P, dtype=np.float32) + P * m)[:, None] * inv[None, :]
        cos, sin = np.cos(ang), np.sin(ang)
        c[:, C_COS + m * HD:C_COS + (m + 1) * HD] = np.concatenate([cos, cos], 1)
        c[:, C_SIN + m * HD:C_SIN + (m + 1) * HD] = np.concatenate([-sin, sin], 1)
    c[:, C_INV:C_INV + 8] = np.float32(500000.0) ** (-np.arange(0, 16, 2, dtype=np.float32) / np.float32(16))
    seen = (
        [(d >= 0) & (d < 128) for d in delta],
        [d >= 0 for d in delta],
        [x > 0 for x in mult],
    )
    for n, per in enumerate(seen):
        for i, x in enumerate(per):
            at = C_MASK + n * QC + i * P
            c[:, at:at + P] = np.where(x, 0.0, NEG)
    c[:, C_MASK + 3 * QC:C_SEL] = np.where(t > u, NEG, 0.0)
    for part in range(3):
        c[32 * part:32 * part + 32, C_SEL:] = np.eye(32)
    return c


class Step:

    def __init__(self, kind, i, *, loads=None, outs=None, needs=None, first=None, last=None, size=None,
                 buf=None, before=None, src=None, dst=None, k0=None, m=None, n=None, u=None, g=None, j=None,
                 t=None, q=None, bank=None, banks=None, obank=None, block=None, gain=None, added=None,
                 of=None, what=None, rstd=None, att=None, head=None, pair=None, half=None, p=None, pv=None,
                 oev=None, den=None, es=None, z=None, nkv=None, dt=None, kind_of=None, ev=None, rope=None,
                 layer=None, conv=None, soft=None, sums=None, xback=None, bback=None, state=None,
                 decay=None, mg=None):
        self.kind, self.i = kind, i
        self.loads, self.outs, self.needs, self.size = loads, outs, needs, size
        self.first, self.last = first, last
        self.buf, self.before, self.src, self.dst, self.k0 = buf, before, src, dst, k0
        self.bank, self.banks, self.obank, self.block = bank, banks, obank, block
        self.m, self.n, self.u, self.g, self.j, self.t, self.q, self.mg = m, n, u, g, j, t, q, mg
        self.gain, self.added, self.of, self.what, self.rstd = gain, added, of, what, rstd
        self.att, self.head, self.pair, self.half, self.p, self.pv = att, head, pair, half, p, pv
        self.oev, self.den, self.es, self.z = oev, den, es, z
        self.nkv, self.dt, self.kind_of, self.ev, self.rope = nkv, dt, kind_of, ev, rope
        self.layer, self.conv, self.soft, self.sums = layer, conv, soft, sums
        self.xback, self.bback, self.state, self.decay = xback, bback, state, decay


class Bank:

    def __init__(self, at, before):
        self.at, self.before, self.freed = at, before, None


class Schedule:

    def __init__(self):
        self.steps, self.count, self.blocks, self.banks = [], {}, [], []
        self.parts, self.quarters, self.gains = 0, [], []
        self.soon, self.filled, self.added, self.turned, self.oturned = [], {}, {}, {}, {}
        self.heads, self.loaded, self.mult_flips, self.plain_flips = 0, 0, 0, 0

    def step(self, kind, **of):
        s = Step(kind, self.count.get(kind, 0), **of)
        self.count[kind] = s.i + 1
        self.steps.append(s)
        return s

    def bank(self):
        n = len(self.banks)
        b = Bank(n % NSCR, self.banks[n - NSCR] if n >= NSCR else None)
        assert b.before is None or b.before.freed is not None, "a bank is taken before it is freed"
        self.banks.append(b)
        return b

    def block(self, width):
        g = len(self.blocks)
        b = {"pair": g % 2, "width": width, "before": self.blocks[g - 2] if g >= 2 else None,
             "evac": [None, None], "ready": [None, None]}
        self.blocks.append(b)
        return b

    def goes_on(self, work=()):
        if self.soon:
            self.soon.pop(0)()
        for f in work:
            f()

    def chunk(self, loads, outs, needs, first, last, beside=()):
        order = [(b, wd, ts, m) for b, wd, ts in outs for m in range(M)]
        s = self.step("chunk", loads=loads, outs=order, needs=needs, first=first, last=last,
                      size=sum(x[0] for x in loads))
        self.goes_on(beside)
        assert self.step("rest", of=s).i == s.i
        if last:
            for b, _, _, m in order[:-1]:
                self.parts += 1
                b["ready"][m] = ("part", self.parts)
            order[-1][0]["ready"][M - 1] = ("chunk_tensor", s.i + 1)
        return s

    def quarter(self, kind, **of):
        n = len(self.quarters)
        s = self.step(kind, buf=n % 2, before=self.quarters[n - 2] if n >= 2 else None, **of)
        self.quarters.append(None)
        return s

    def turn(self, src, dst, k0, m):
        b = self.bank()
        s = self.step("turn", src=src, dst=dst, k0=k0, m=m, bank=b)
        b.freed = (s, "vector")
        self.quarters[self.quarters.index(None)] = s
        return s

    def gain(self, src):
        if src is not None:
            self.loaded += 1
        g = {"src": src, "i": len(self.gains), "loaded": self.loaded, "users": [], "made": None}
        self.gains.append(g)
        return g


def attention(sc, n):
    a = sc.att
    if 2 <= n <= a["heads"] + 1:
        b = sc.bank()
        s = sc.step("flip", head=n - 2, att=a, bank=b, p=a["base"] + n - 2,
                    n=len(a["flip"]) + (sc.mult_flips if a["kind"] == "h" else sc.plain_flips))
        b.freed = (s, "vector" if a["kind"] == "h" else "scalar")
        a["flip"].append(s)
    if n < a["heads"]:
        b = sc.bank()
        s = sc.step("scores", head=n, att=a, bank=b, p=a["base"] + n)
        b.freed = (s, "scalar")
        a["scores"].append(s)
    if 3 <= n <= a["heads"] + 2:
        head = n - 3
        if head % 2 == 0:
            a["obank"] = sc.bank()
        s = sc.step("pv", head=head, att=a, bank=a["obank"], p=a["base"] + head)
        a["pv"].append(s)
        if head % 2 == 1:
            o = sc.step("oev", att=a, pair=head // 2, bank=a["obank"], pv=s)
            a["obank"].freed = (o, "scalar")
            a["oev"].append(o)


def add(sc, block, n, m):
    block["evac"][m] = sc.added[n, m] = sc.step("added", n=n, m=m, block=block)


def times_gain(sc, n, m):
    gain = sc.gain_now
    s = sc.quarter("gained", n=n, m=m, gain=gain, added=sc.added.get((n, m)))
    gain["users"].append(s)
    sc.filled[n, m] = s


def turn_x(sc, n, *ms):
    for m in ms or range(M):
        sc.turned[n, m] = sc.turn(sc.filled[n, m], "x", 4 * n, m)


def squares(sc, n):
    for m in range(M):
        sc.step("square", n=n, m=m, added=sc.added.get((n, m)))


def factor(sc, what):
    a = sc.step("meansq", what=what, of=sc.count["square"])
    sc.rstd = sc.step("newton", what=what, before=a)


def norm_goes_on(sc, mid):
    def second_half():
        turn_x(sc, 1, 0)
        squares(sc, 0)
        if mid:
            squares(sc, 1)
            factor(sc, "first")

    def factors():
        turn_x(sc, 1, 1)
        if mid:
            normed_residual(sc, "mid")
            squares(sc, 0)
            squares(sc, 1)
            factor(sc, "both")
        else:
            squares(sc, 1)
            factor(sc, "h")

    sc.soon += [second_half, factors]


def normed_residual(sc, what):
    for m in range(M):
        s = sc.step("final", m=m, what=what, gain=sc.gain_now, rstd=sc.rstd)
        for n in range(2):
            sc.added[n, m] = s


def project_chunk(sc, w, cols, ks, block, first, last, beside=(), then=()):
    src = [(len(ks) * cw, (w, c0, cw, ks)) for c0, cw in cols]
    width = sum(cw for _, cw in cols)
    outs = [(block, width, [("x", k, i * width) for i, k in enumerate(ks)])]
    need = [[sc.turned[n, m] for n in range(2) if 4 * n in ks] for m in range(M)]
    sc.chunk(src, outs, need, first, last, beside)
    sc.goes_on(then)


def halves(sc, w, cols, a=(), b=(), c=()):
    blk = sc.block(sum(cw for _, cw in cols))
    project_chunk(sc, w, cols, [0, 1, 2, 3], blk, True, False, a, b)
    project_chunk(sc, w, cols, [4, 5, 6, 7], blk, False, True, c)
    return blk


def out_product(sc, w, kt, beside, mid=False):
    bs = [sc.block(512), sc.block(512)]
    c = 0
    for k0 in range(0, kt, 4):
        ks = list(range(k0, k0 + 4))
        end = k0 + 4 == kt
        for n in range(2):
            need = [[sc.oturned[k0 // 4, m]] for m in range(M)]

            def begin(n=n):
                if n == 0:
                    add(sc, bs[0], 0, 0)
                    times_gain(sc, 0, 0)
                else:
                    turn_x(sc, 0, 0)
                    add(sc, bs[1], 1, 0)
                    times_gain(sc, 1, 0)

            between, after = beside.get(c, ((), ()))
            if end:
                between = list(between) + [begin]
            sc.chunk([(4 * 512, (w, n * 512, 512, ks))],
                     [(bs[n], 512, [("o", k, i * 512) for i, k in enumerate(ks)])],
                     need, k0 == 0, end, between)
            sc.goes_on(after)
            c += 1
            if end:
                if n:
                    turn_x(sc, 0, 1)
                add(sc, bs[n], n, 1)
                times_gain(sc, n, 1)
    norm_goes_on(sc, mid)


def evacs(sc, b, kind, **of):
    for m in range(M):
        b["evac"][m] = sc.step(kind, m=m, block=b, rstd=sc.rstd, **of)
    return b["evac"][1]


def turn_keys(sc, a, kr):
    for t in range(a["nkv"] // 2):
        bk = sc.bank()
        s = sc.step("turn_k", t=t, rope=kr, bank=bk)
        bk.freed = (s, "scalar")
        a["tk"].append(s)


def turn_queries(sc, a, j, rq):
    for t in range(2):
        bk = sc.bank()
        s = sc.step("turn_q", j=j, t=t, rope=rq, bank=bk)
        bk.freed = (s, "scalar")
        a["tq"].append(s)


def fill_gates(sc, a, half, z):
    es = sc.step("sink", att=a, half=half) if a["kind"] == "a" else None
    den = sc.step("den", att=a, half=half, es=es, oev=a["oev"][4 * half + 3])
    a["gates"][half] = [sc.quarter("gate" if half and m else "pool_gate", att=a, half=half, m=m, z=z, den=den) for m in range(M)]


def turn_gates(sc, a, half, *ms):
    for m in ms or range(M):
        sc.oturned[half, m] = sc.turn(a["gates"][half][m], "o", 4 * half, m)


def new_attention(sc, which, heads, nkv):
    if sc.heads:
        count_flips(sc)
    a = sc.att = {"kind": which, "heads": heads, "nkv": nkv, "scores": [], "flip": [], "pv": [], "oev": [],
                  "base": sc.heads, "tk": [], "tq": [], "gates": {}}
    sc.heads += heads
    return a


def count_flips(sc):
    if sc.att["kind"] == "h":
        sc.mult_flips += len(sc.att["flip"])
    else:
        sc.plain_flips += len(sc.att["flip"])


def mixer_ab(sc, which, w_in, w_out, nkv, mid=False):
    kvw = nkv * HD
    a = new_attention(sc, which, 16, nkv)

    def att(*ns):
        return [lambda n=n: attention(sc, n) for n in ns]

    kv = [(D, 2 * kvw)]
    b = halves(sc, w_in, [(0, 512)])
    ev = evacs(sc, b, "ev_q", j=0, kind_of=which)
    rq0 = sc.step("pool_rope" if nkv > 2 else "rope_q", j=0, kind_of=which, ev=ev)
    if nkv == 2:
        b = sc.block(2 * kvw)
        project_chunk(sc, w_in, kv, list(range(KD)), b, True, True)
    else:
        b = halves(sc, w_in, kv)
    ev = evacs(sc, b, "ev_kv", nkv=nkv, dt=None)
    kr = sc.step("rope_k", nkv=nkv, kind_of=which, ev=ev)
    if sc.heads == 16:
        bk = sc.bank()
        s = sc.step("taps", bank=bk)
        bk.freed = (s, "scalar")
    b = halves(sc, w_in, [(512, 512)], (), [lambda: turn_queries(sc, a, 0, rq0)], [lambda: turn_keys(sc, a, kr)])
    ev = evacs(sc, b, "ev_q", j=1, kind_of=which)
    rq1 = sc.step("pool_rope", j=1, kind_of=which, ev=ev)
    sc.goes_on(att(0))

    def queries():
        turn_queries(sc, a, 1, rq1)
        if mid:
            sc.step("mid_load", before=a["tq"][-1])

    b = halves(sc, w_in, [(D + 2 * kvw, 512)], att(1, 2), att(3, 4), [queries] + att(5, 6))
    za = evacs(sc, b, "ev_z", j=0, kind_of=which)
    sc.goes_on(att(7, 8))
    if mid:
        sc.gain_now = sc.gain(None)
        sc.gain_now["made"] = sc.step("mid_gain")
    b = halves(sc, w_in, [(D + 2 * kvw + 512, 512)], att(9, 10) + [lambda: fill_gates(sc, a, 0, za)], att(11, 12),
               att(13, 14, 15))
    zb = evacs(sc, b, "ev_z", j=1, kind_of=which)
    sc.goes_on([lambda: turn_gates(sc, a, 0)] + att(16, 17))
    out_product(sc, w_out, KD, {
        0: (att(18) + [lambda: fill_gates(sc, a, 1, zb)], ()),
        1: ([lambda: turn_gates(sc, a, 1, 0)], [lambda: turn_gates(sc, a, 1, 1)])}, mid)


def hybrid(sc, layer, w, last_gain):
    a = new_attention(sc, "h", 8, 2)
    w_in, q0, kv0, z0, x0, dt0 = w["in"], 0, 512, 768, 1792, 3328
    scan = {}

    def att(*ns):
        return [lambda n=n: attention(sc, n) for n in ns]

    def conv(j, u):
        bk = sc.bank()
        s = sc.step("conv", j=j, u=u, bank=bk, ev=scan["ev", j], layer=layer,
                    conv=scan["silu", j - 1] if j else None)
        bk.freed = (s, "vector")
        scan["conv", j] = s

    def conv_silu(j):
        scan["silu", j] = sc.step("conv_silu", j=j, layer=layer, conv=scan["conv", j])

    def evac_x(b, j):
        scan["ev", j] = evacs(sc, b, "ev_x", j=j, conv=scan["conv", j - 1] if j else None)

    def back(j):
        b1, b2 = sc.bank(), sc.bank()
        s = sc.step("xback", j=j, banks=(b1, b2), conv=scan["silu", j + 1], sums=scan["sums"])
        b1.freed = b2.freed = (s, "scalar")
        scan["xback", j] = s

    def bback():
        b1, b2 = sc.bank(), sc.bank()
        s = sc.step("bback", banks=(b1, b2), conv=scan["silu", 0])
        b1.freed = b2.freed = (s, "scalar")
        scan["bback"] = s

    def sums():
        bk = sc.bank()
        scan["sums"] = sc.step("sums", bank=bk, before=scan["soft3"])
        bk.freed = (scan["sums"], "vector")

    def decay(g, m, i):
        bk = sc.bank()
        s = sc.step("decay", q=i, mg=(m, g), bank=bk, sums=scan["sums"], bback=scan["bback"])
        bk.freed = (s, "scalar")
        scan["decay", g, m, i] = s

    def state(g):
        bk = sc.bank()
        s = sc.step("state", g=g, bank=bk, xback=scan["xback", g], bback=scan["bback"])
        bk.freed = (s, "scalar")
        scan["state", g] = s

    def scanned(g, m):
        yb = sc.bank()
        for i in range(2):
            last = sc.step("diag", q=i, m=m, g=g, bank=yb, decay=scan["decay", g, m, i], xback=scan["xback", g])
        ob = None
        if m == 1:
            ob = sc.bank()
            last = sc.step("off", g=g, bank=ob, state=scan["state", g])
        y = sc.step("join", m=m, g=g, bank=yb, obank=ob, last=last, z=scan["z", g], xback=scan["xback", g])
        yb.freed = (y, "vector")
        if ob:
            ob.freed = (y, "vector")

    def group_norm(g):
        ra = sc.step("meansq", what="y", g=g, of=sc.count["join"])
        rb = sc.step("newton", what="y", g=g, before=ra)
        scan["y", g] = []
        for m in range(M):
            s = sc.quarter("ynorm", m=m, g=g, rstd=rb, gain=scan["gain"])
            scan["gain"]["users"].append(s)
            scan["y", g].append(s)

    def turn_y(g, *ms):
        for m in ms or range(M):
            sc.oturned[1 + g, m] = sc.turn(scan["y", g][m], "o", 4 + 4 * g, m)

    def do(f, *x):
        return [lambda: f(*x)]

    b = halves(sc, w_in, [(q0, 512)])
    ev = evacs(sc, b, "ev_q", j=0, kind_of="h")
    rq = sc.step("rope_q", j=0, kind_of="h", ev=ev)
    b = sc.block(272)
    project_chunk(sc, w_in, [(kv0, 256), (dt0, 16)], list(range(8)), b, True, True)
    ev = evacs(sc, b, "ev_kv", nkv=2, dt=layer)
    kr = sc.step("rope_k", nkv=2, kind_of="h", ev=ev)

    def soft(n):
        before = scan.get(f"soft{n - 1}")
        scan[f"soft{n}"] = sc.step(f"soft{n}", layer=layer, ev=ev, before=before)

    b = halves(sc, w_in, [(x0 + SSM, 512)], do(turn_queries, sc, a, 0, rq) + do(soft, 1),
               do(turn_keys, sc, a, kr) + do(soft, 2), att(0) + do(soft, 3))
    evac_x(b, 0)
    sc.goes_on(att(1))
    b = halves(sc, w_in, [(x0, 512)], att(2) + do(sums), do(conv, 0, 0) + att(3), att(4) + do(conv, 0, 1))
    evac_x(b, 1)
    sc.goes_on(att(5))
    b = halves(sc, w_in, [(x0 + 512, 512)], do(conv_silu, 0) + att(6), do(conv, 1, 0) + att(7), att(8) + do(conv, 1, 1))
    evac_x(b, 2)
    sc.goes_on(att(9))
    scan["gain"] = sc.gain(("ssm_norm", layer))
    b = halves(sc, w_in, [(z0, 512)], do(conv_silu, 1) + att(10) + do(fill_gates, sc, a, 0, None), do(conv, 2, 0) + do(bback),
               do(back, 0) + do(conv, 2, 1))
    scan["z", 0] = evacs(sc, b, "ev_z", j=0, kind_of="h")
    sc.goes_on(do(conv_silu, 2) + do(turn_gates, sc, a, 0))
    b = halves(sc, w_in, [(z0 + 512, 512)], do(decay, 0, 0, 0) + do(decay, 0, 0, 1) + do(state, 0),
               do(back, 1) + do(scanned, 0, 0), do(decay, 0, 1, 0) + do(decay, 0, 1, 1))
    scan["z", 1] = evacs(sc, b, "ev_z", j=1, kind_of="h")
    sc.goes_on(do(scanned, 0, 1) + do(group_norm, 0))

    def next_gain():
        sc.gain_now = sc.gain(("norm_ffn", layer))

    out_product(sc, w["out"], 12, {
        0: (do(decay, 1, 0, 0) + do(state, 1), do(decay, 1, 0, 1)),
        1: (do(scanned, 1, 0) + do(turn_y, 0, 0), do(turn_y, 0, 1) + do(decay, 1, 1, 0) + do(decay, 1, 1, 1)),
        2: (do(scanned, 1, 1) + do(group_norm, 1) + do(next_gain), ()),
        3: (do(turn_y, 1, 0), do(turn_y, 1, 1))})

    pend = None
    hturn = []
    for u in range(NUP):
        b = sc.block(2 * UPW)
        for half in range(2):
            ks = list(range(4 * half, 4 * half + 4))
            sc.chunk([(4 * UPW, (w["gate"], u * UPW, UPW, ks)), (4 * UPW, (w["up"], u * UPW, UPW, ks))],
                     [(b, 2 * UPW, [("x", k, i * 2 * UPW) for i, k in enumerate(ks)])],
                     [[sc.turned[half, m]] for m in range(M)], half == 0, half == 1)
            sc.goes_on()
            if half == 0 and pend is not None:
                hturn.append(sc.turn(pend, "h", 2 * pend.u, 0))
                pend = None
        pend = sc.quarter("ev_up", u=u, block=b, rstd=sc.rstd)
        b["evac"] = [pend, pend]
    sc.gain_now = sc.gain(last_gain)
    b0, b1 = sc.block(512), sc.block(512)
    for j in range(KF // 2):
        if j == 1:
            hturn.append(sc.turn(pend, "h", 2 * pend.u, 0))

        def first_block_ends():
            for m in range(M):
                add(sc, b0, 0, m)
            for m in range(M):
                if layer == 0:
                    times_gain(sc, 0, m)

        last = j == KF // 2 - 1
        sc.chunk([(2 * D, (w["down"], 0, D, [2 * j, 2 * j + 1]))],
                 [(b, 512, [("h", 2 * j + i, i * D + n * 512) for i in range(2)]) for n, b in enumerate((b0, b1))],
                 [[hturn[j]], []], j == 0, last, [first_block_ends] if last else ())
    if layer == 0:
        add(sc, b1, 1, 0)
        turn_x(sc, 0)
        add(sc, b1, 1, 1)
        for m in range(M):
            times_gain(sc, 1, m)
        norm_goes_on(sc, False)
    else:
        squares(sc, 0)
        for m in range(M):
            add(sc, b1, 1, m)
        squares(sc, 1)
        factor(sc, "h")
        normed_residual(sc, "end")


def build_schedule(w):
    sc = Schedule()
    sc.gain_now = sc.gain(("norm_g", 0))
    for m in range(M):
        times_gain(sc, 0, m)
    turn_x(sc, 0)
    sc.step("begin")
    for m in range(M):
        times_gain(sc, 1, m)
    sc.soon += [lambda: (turn_x(sc, 1), squares(sc, 0)), lambda: (squares(sc, 1), factor(sc, "h"))]
    sc.gain_now = sc.gain(("norm_g", 1))
    mixer_ab(sc, "a", w["in_a"], w["out0"], 2)
    mixer_ab(sc, "b", w["in_b"], w["out1"], 4, True)
    hybrid(sc, 0, w["h"][0], ("norm_mix", 1))
    hybrid(sc, 1, w["h"][1], ("final", 0))
    return sc


def due(s):
    if s.kind == "begin":
        return [(0, 0), (0, 1)]
    if s.i < 2:
        return {("chunk", 0): [(1, 0), (1, 1)], ("rest", 0): [(2, 0)],
                ("chunk", 1): [(2, 1), (3, 0)], ("rest", 1): [(3, 1)]}[s.kind, s.i]
    return [(s.i + AHEAD, 0 if s.kind == "chunk" else 1)]


def half_of(c, half):
    return slice(half * c.size // 2, (half + 1) * c.size // 2)


PARTS = {
    "chunk": ("tensor", "scalar", "vector"), "gained": ("vector",), "turn": ("tensor", "scalar", "vector"),
    "taps": ("tensor", "scalar"), "mid_gain": ("vector",), "square": ("scalar",), "meansq": ("vector", "gpsimd"), "newton": ("vector",), "added": ("vector",),
    "ev_kv": ("scalar",), "ev_q": ("scalar",), "ev_z": ("scalar",), "ev_x": ("scalar",),
    "ev_up": ("scalar", "vector"), "rope_k": ("vector",), "rope_q": ("vector",),
    "turn_k": ("tensor", "scalar"), "turn_q": ("tensor", "scalar"),
    "scores": ("tensor", "vector", "scalar"), "flip": ("tensor", "scalar", "vector"), "pv": ("tensor",),
    "oev": ("scalar",), "sink": ("vector", "scalar"), "den": ("vector",), "gate": ("vector",), "pool_gate": ("gpsimd",), "pool_rope": ("gpsimd",),
    "soft1": ("vector", "scalar"), "soft2": ("vector", "scalar"), "soft3": ("vector",),
    "sums": ("tensor", "vector", "scalar"), "conv": ("tensor", "scalar", "vector"), "conv_silu": ("scalar",),
    "bback": ("tensor", "scalar"), "xback": ("tensor", "scalar", "gpsimd"), "state": ("tensor", "scalar"),
    "decay": ("tensor", "scalar", "vector"), "diag": ("tensor",), "off": ("tensor",),
    "join": ("vector", "scalar"), "ynorm": ("vector",), "final": ("vector",),
}


def build(nc, t):
    def w3(ap):
        return ap.rearrange("(k p) n -> p k n", p=P)

    w = {"in_a": w3(t["w_in_a"][0]), "in_b": w3(t["w_in_b"][0]), "out0": w3(t["w_out"][0]), "out1": w3(t["w_out"][1]),
         "h": [{"in": w3(t["w_in_2"][i]), "out": w3(t["w_out_2"][i]), "gate": w3(t["w_gate_2"][i]),
                "up": w3(t["w_up_2"][i]), "down": w3(t["w_down_2"][i])} for i in range(2)]}
    sc = build_schedule(w)
    chunks = [s for s in sc.steps if s.kind == "chunk"]
    gain_rows = {"norm_g": t["norm_g"], "norm_mix": t["norm_mix_2"], "ssm_norm": t["ssm_norm_2"],
                 "norm_ffn": t["norm_ffn_2"]}

    place = [16512]

    def at(name, shape, dt, where=None):
        size = math.prod(shape[1:]) * (2 if dt == BF16 else 4)
        size = -(-size // 32) * 32
        if where is None:
            where = place[0]
            place[0] += size
        else:
            at.end = max(at.end, where + size)
        return nc.alloc_sbuf_tensor_at(name, shape, dt, offset=where), where + size

    def keep(name, shape, dt=F32):
        return at(name, shape, dt)[0]

    at.end = 0
    h = keep("h", [P, M, D])
    xT = [keep("xT_hi", [P, KD, S], F32R), keep("xT_lo", [P, KD, S], F32R)]
    oT = [keep("oT_hi", [P, 12, S], F32R), keep("oT_lo", [P, 12, S], F32R)]
    raw = [keep(f"raw{i}", [P, CH]) for i in range(RAW)]
    hi = [keep(f"hi{i}", [P, CH], F32R) for i in range(SPLIT)]
    lo = [keep(f"lo{i}", [P, CH], F32R) for i in range(SPLIT)]
    quarter = [keep(f"quarter{i}", [P, 512]) for i in range(2)]
    gains = keep("gains", [P, D])
    cst = keep("cst", [P, C_KEEP])
    masks = keep("masks", [P, 3 * QC + P + 32], BF16)
    csum = keep("csum", [P, P], BF16)
    identb = keep("identb", [P, P], BF16)
    ones = keep("ones", [P, P])
    junk = keep("junk", [P, 512], BF16)
    sumsq = keep("sumsq", [P, 4])
    rms = keep("rms", [P, 3, M])
    rmy = keep("rmy", [P, 3, 4])
    newt = keep("newt", [P, 3, 2])
    power = keep("power", [P, 2])
    posi = keep("posi", [P, M], I32)
    posf = keep("posf", [P, M])
    trig = keep("trig", [P, M, 2, 16])
    sinks = keep("sinks", [P, 2, 16])
    small = keep("small", [P, 2, 3, 16])
    taps = keep("taps", [P, 10 * NCT])
    convw = taps[:, 0:8 * NCT].rearrange("p (l t c) -> p l t c", l=2, t=4)
    convb = taps[:, 8 * NCT:10 * NCT].rearrange("p (l c) -> p l c", l=2)
    rowmax = keep("rowmax", [P, 2, 4])
    shift = keep("shift", [P, 16, M])
    esink = keep("esink", [P, 16, M])
    dens = keep("dens", [P, M, 8])
    ident, upper = cst[:, C_ID:C_ID + P], cst[:, C_U:C_U + P]
    mult = cst[:, C_CT:C_CT + QC]

    base = place[0]
    hT = []
    end = base
    for i in range(2):
        x, end = at(f"hT{i}", [P, KF, S], F32R, end)
        hT.append(x)
    sil = []
    for i in range(2):
        x, end = at(f"silu_gate{i}", [P, M, UPW], F32, end)
        sil.append(x)

    def plan(tag, hybrid_):
        b = {}
        p = [base]

        def put(name, shape, dt=F32, where=None):
            x, e = at(f"{tag}_{name}", shape, dt, p[0] if where is None else where)
            b[name + "_at"] = (p[0] if where is None else where)
            if where is None:
                p[0] = e
            b[name] = x
            return e

        nkv, heads = (2, 8) if hybrid_ else (4, 16)
        put("v1", [P, M, nkv, HD + 1])
        put("kT", [P, nkv, S])
        put("qT", [P, heads // 2, S])
        put("prob0", [P, QC])
        put("prob1", [P, QC])
        put("probT0", [P, QC])
        put("probT1", [P, QC])
        put("z", [P, M, D])
        e = put("k", [P, M, nkv, HD])
        e = put("kdup", [P, M, nkv, 2, HD])
        put("rot1", [P, 512])
        e = put("rot2", [P, 512])
        put("o", [P, M, heads, HD + 1], where=b["k_at"])
        e = b["k_at"] + 4 * M * heads * (HD + 1)
        p[0] = max(p[0], -(-e // 32) * 32)
        q_at = p[0]
        put("q", [P, M, heads * HD])
        if not hybrid_:
            put("pool_rot1", [P, 512])
            put("pool_rot2", [P, 512])
        if hybrid_:
            e = put("cb", [P, M, 2, P], where=q_at)
            put("bt", [P, 2, P], where=e)
            put("xin", [P, M, 512])
            put("st", [P, SSM], where=b["xin_at"])
            put("cT", [P, NCT, S])
            e = put("E0", [P, 4, P], where=b["prob0_at"])
            e = put("E1", [P, 4, P], where=e)
            put("MT0", [P, 4, P], where=e)
            e = put("xgd", [P, SSM], where=b["kT_at"])
            put("MT1", [P, 4, P], where=e)
            put("da", [P, 3, M * SH], where=b["z_at"])
            put("rest", [P, P], where=b["rot2_at"])
            put("xs", [P, M, SSM])
            for i in range(2):
                put(f"acc{i}", [P, 2, S], where=b["xs_at"] + 4 * (512 + i * SSM))
            put("xg", [P, M, SSM])
            for name in ("dtr", "dt", "sa", "sb", "sc", "sd"):
                put(name, [P, M, SH])
            put("ncs", [P, M, SH])
            put("dif", [P, SH])
            put("dec", [P, SH])
            put("ecs", [P, SH])
        return b

    A, Hb = plan("attn", False), plan("hyb", True)
    stage, e = at("mask_stage", [P, C_ALL - C_KEEP], F32, A["pool_rot2_at"] + 2048)
    taps_in, e = at("taps_stage", [P, P], F32, e)
    angle, e = at("trig_stage", [P, M, 2, 8], F32, e)
    sine, e = at("trig_stage2", [P, M, 2, 8], F32, e)
    turns, _ = at("trig_stage3", [P, M, 2, 8], F32, e)
    mid_rows = [at(f"mid_row{i}", [P, D], F32, A["q_at"] + 4 * D * i)[0] for i in range(2)]
    assert max(place[0], at.end) <= 229344, (place[0], at.end)

    psum = [nc.alloc_psum_tensor(f"bank{i}", [P, 512], F32) for i in range(8)]

    sem = {}
    for kind, who in PARTS.items():
        for e in who:
            sem[kind, e] = nc.alloc_semaphore(f"{kind}_{e}")
    raw_in = [nc.alloc_semaphore(f"raw_in{i}") for i in range(RAW)]
    part_done = nc.alloc_semaphore("part_done")
    x_in = nc.alloc_semaphore("x_in")
    const_in = nc.alloc_semaphore("const_in")
    masks_in = nc.alloc_semaphore("masks_in")
    sinks_in = nc.alloc_semaphore("sinks_in")
    small_in = nc.alloc_semaphore("small_in")
    mid_in = nc.alloc_semaphore("mid_in")
    x_first = [nc.alloc_semaphore(f"x_first{m}") for m in range(M)]
    raw_first = nc.alloc_semaphore("raw_first")
    gain_in = nc.alloc_semaphore("gain_in")
    setup_dve = nc.alloc_semaphore("setup_vector")
    setup_act = nc.alloc_semaphore("setup_scalar")
    out_done = nc.alloc_semaphore("out_done")
    chain = {e: nc.alloc_semaphore(f"chain_{e}") for e in ("vector", "scalar", "gpsimd")}
    links = {"vector": 0, "scalar": 0, "gpsimd": 0}

    def ended(eng, step, who):
        eng.wait_ge(sem[step.kind, who], step.i + 1)

    def freed(eng, bank):
        if bank.before is not None:
            step, who = bank.before.freed
            if step.kind == "flip":
                eng.wait_ge(sem["flip", who], step.n + 1)
            else:
                ended(eng, step, who)
        return psum[4 + bank.at]

    def ready(eng, block, m):
        name, v = block["ready"][m]
        eng.wait_ge(part_done if name == "part" else sem["chunk", "tensor"], v)
        return psum[2 * block["pair"] + m]

    def link(eng, who, ins):
        links[who] += 1
        ins.then_inc(chain[who], 1)
        eng.wait_ge(chain[who], links[who])

    def norm_parts(s):
        if s.what == "y":
            g = slice(2 * s.g, 2 * s.g + 2)
            return rmy[:, 0, g], rmy[:, 1, g], rmy[:, 2, g], newt[:, 1 + s.g, :]
        return sumsq, rms[:, 0, :], rms[:, 2 if s.what == "first" else 1, :], newt[:, 0, :]

    def spread(ap, shape):
        return ap.broadcast_to(shape)

    arrived, total = {}, [0] * RAW
    for c in chunks:
        total[c.i % RAW] += 16 * len(c.loads)
        arrived[c.i] = total[c.i % RAW]

    NSMALL = 6
    program = ExitStack()
    blk = program.enter_context(nc.Block())

    @blk.sync
    def _(sp):
        with nc.allow_non_contiguous_dma("small rows and weights by columns"):
            x = t["x"][0].rearrange("(m p) d -> p m d", p=P)
            sp.dma_start(cst[:, 0:P], t["cst"][:, 0:P]).then_inc(const_in, 16)
            for m in range(M):
                sp.dma_start(h[:, m, 0:512], x[:, m, 0:512]).then_inc(x_first[m], 16)

            def load(c):
                slot = raw[c.i % RAW]
                if c.i >= RAW:
                    sp.wait_ge(sem["chunk", "vector"], 2 * (c.i - RAW + 1))
                off = 0
                if c.i == 0:
                    _, (wt, c0, cw, ks) = c.loads[0]
                    for half in range(2):
                        dst = slot[:, half_of(c, half)].rearrange("p (k n) -> p k n", n=cw)
                        n = len(ks) // 2
                        sp.dma_start(dst, wt[:, n * half:n * (half + 1), c0:c0 + cw]).then_inc(raw_in[0] if half else raw_first, 16)
                    return
                for n, (size, (wt, c0, cw, ks)) in enumerate(c.loads):
                    src = wt[:, ks[0]:ks[-1] + 1, c0:c0 + cw]
                    if len(c.loads) == 1:
                        dst = slot[:, 0:size].rearrange("p (k n) -> p k n", n=cw)
                    else:
                        full = c.size // len(ks)
                        dst = slot[:, 0:c.size].rearrange("p (k n) -> p k n", n=full)[:, :, off:off + cw]
                        off += cw
                    sp.dma_start(dst, src).then_inc(raw_in[c.i % RAW], 16)

            load(chunks[0])
            sp.dma_start(h[:, :, 512:D], x[:, :, 512:D]).then_inc(x_in, 16)
            load(chunks[1])
            load(chunks[2])
            for s in sc.steps:
                if s.kind == "chunk" and s.i + RAW < len(chunks):
                    load(chunks[s.i + RAW])
            for i in range(M):
                sp.wait_ge(sem["final", "vector"], M + i + 1)
                sp.dma_start(t["out"][0, i * P:(i + 1) * P, :], h[:, i, :]).then_inc(out_done, 16)
            sp.wait_ge(out_done, 16 * M)

    @blk.tensor
    def _(pe):
        def transpose(out, in_):
            return nc.tensor.transpose(out, in_, ident)

        pe.wait_ge(const_in, 16)
        for s in sc.steps:
            if s.kind in ("chunk", "rest"):
                c, half = (s, 0) if s.kind == "chunk" else (s.of, 1)
                for x in c.needs[half]:
                    ended(pe, x, "vector")
                if half == 0:
                    pe.wait_ge(sem["chunk", "vector"], 2 * c.i + 1)
                src = {"x": xT, "o": oT, "h": hT}
                r = c.i % SPLIT
                per = len(c.outs) // 2
                for n, (b, wd, ts, m) in enumerate(c.outs[half * per:(half + 1) * per]):
                    if c.first and b["before"]:
                        e = b["before"]["evac"][m]
                        ended(pe, e, "vector" if e.kind in ("added", "ev_up") else "scalar")
                    bank = psum[2 * b["pair"] + m]
                    for i, (name, k, off) in enumerate(ts):
                        if half == 0 and n == 0 and 2 * i == len(ts):
                            pe.wait_ge(sem["chunk", "vector"], 2 * c.i + 2)
                        still = [x[:, k, m * P:(m + 1) * P] for x in src[name]]
                        for j, (a, mv) in enumerate(((0, hi), (0, lo), (1, hi))):
                            last = nc.tensor.matmul(
                                bank[:, 0:wd], still[a], mv[r][:, off:off + wd],
                                start=c.first and i == 0 and j == 0,
                                stop=c.last and i == len(ts) - 1 and j == 2)
                    if c.last and (half == 0 or n < per - 1):
                        last.then_inc(part_done, 1)
                if half:
                    last.then_inc(sem["chunk", "tensor"], 1)
            elif s.kind == "turn":
                ended(pe, s.src, PARTS[s.src.kind][-1])
                bank = freed(pe, s.bank)
                q = quarter[s.src.buf]
                for i in range(4):
                    j = (i % 2) * 2 + i // 2 if s.dst == "h" else i
                    last = transpose(bank[:, i * P:(i + 1) * P], q[:, j * P:(j + 1) * P])
                last.then_inc(sem["turn", "tensor"], 1)
            elif s.kind == "taps":
                pe.wait_ge(small_in, 16 * NSMALL)
                n = 10 * NCT
                nc.tensor.transpose(freed(pe, s.bank)[:, 0:n], taps_in[0:n, :], cst[0:n, C_ID:C_ID + n])\
                  .then_inc(sem["taps", "tensor"], 1)
            elif s.kind == "turn_k":
                B = A if s.rope.kind_of != "h" else Hb
                ended(pe, s.rope, "vector")
                bank = freed(pe, s.bank)
                for g in range(2):
                    for m in range(M):
                        kd = B["kdup"][:, m, 2 * s.t + g, :, :].rearrange("p a d -> p (a d)")
                        last = transpose(bank[:, (2 * g + m) * P:(2 * g + m + 1) * P], kd)
                last.then_inc(sem["turn_k", "tensor"], 1)
            elif s.kind == "turn_q":
                B = A if s.rope.kind_of != "h" else Hb
                ended(pe, s.rope, PARTS[s.rope.kind][-1])
                bank = freed(pe, s.bank)
                for g in range(2):
                    for m in range(M):
                        c0 = s.j * 512 + (2 * s.t + g) * P
                        last = transpose(bank[:, (2 * g + m) * P:(2 * g + m + 1) * P], B["q"][:, m, c0:c0 + P])
                last.then_inc(sem["turn_q", "tensor"], 1)
            elif s.kind == "scores":
                a, hd = s.att, s.head
                B = Hb if a["kind"] == "h" else A
                kv = hd // (a["heads"] // a["nkv"])
                ended(pe, a["tk"][-1], "scalar")
                ended(pe, a["tq"][hd // 4], "scalar")
                bank = freed(pe, s.bank)
                mk = {"a": 0, "b": 1, "h": 2}[a["kind"]]
                nc.tensor.matmul(bank[:, 0:QC], identb[:, :], masks[:, mk * QC:(mk + 1) * QC], start=True, stop=False)
                r = 64 * (hd % 2)
                q, k = B["qT"], B["kT"]
                nc.tensor.matmul(bank[:, 0:P], q[r:r + 64, hd // 2, 0:P], k[r:r + 64, kv, 0:P], start=False, stop=False)
                nc.tensor.matmul(bank[:, P:QC], q[r:r + 64, hd // 2, P:S], k[r:r + 64, kv, 0:S],
                                 start=False, stop=True).then_inc(sem["scores", "tensor"], 1)
            elif s.kind == "flip":
                a = s.att
                B = Hb if a["kind"] == "h" else A
                ended(pe, a["scores"][s.head], "scalar")
                bank = freed(pe, s.bank)
                pr = B[f"prob{s.p % 2}"]
                for i in range(3):
                    last = transpose(bank[:, i * P:(i + 1) * P], pr[:, i * P:(i + 1) * P])
                last.then_inc(sem["flip", "tensor"], 1)
            elif s.kind == "pv":
                a, hd = s.att, s.head
                B = Hb if a["kind"] == "h" else A
                kv = hd // (a["heads"] // a["nkv"])
                pe.wait_ge(sem["flip", "vector" if a["kind"] == "h" else "scalar"], a["flip"][hd].n + 1)
                bank = freed(pe, s.bank) if hd % 2 == 0 else psum[4 + s.bank.at]
                pt, v = B[f"probT{s.p % 2}"], B["v1"]
                W1 = HD + 1
                c0 = (hd % 2) * 2 * W1
                nc.tensor.matmul(bank[:, c0:c0 + W1], pt[:, 0:P], v[:, 0, kv, :], start=True, stop=True)
                nc.tensor.matmul(bank[:, c0 + W1:c0 + 2 * W1], pt[:, P:2 * P], v[:, 0, kv, :], start=True, stop=False)
                nc.tensor.matmul(bank[:, c0 + W1:c0 + 2 * W1], pt[:, 2 * P:QC], v[:, 1, kv, :],
                                 start=False, stop=True).then_inc(sem["pv", "tensor"], 1)
            elif s.kind == "sums":
                ended(pe, s.before, "vector")
                bank = freed(pe, s.bank)
                da = Hb["da"][:, 0, :]
                nc.tensor.matmul(bank[:, 0:32], upper, da, start=True, stop=True)
                nc.tensor.matmul(bank[:, 32:64], ones[:, :], da, start=True, stop=True)
                nc.tensor.matmul(bank[0:96, 64:64 + P], Hb["da"][:, :, :].rearrange("p a s -> p (a s)"), upper,
                                 start=True, stop=True).then_inc(sem["sums", "tensor"], 1)
            elif s.kind == "conv":
                ended(pe, s.ev, "scalar")
                bank = freed(pe, s.bank)
                for i in range(2):
                    for m in range(M):
                        c0 = (2 * s.u + i) * P
                        last = transpose(bank[:, (2 * i + m) * P:(2 * i + m + 1) * P], Hb["xin"][:, m, c0:c0 + P])
                last.then_inc(sem["conv", "tensor"], 1)
            elif s.kind == "bback":
                ended(pe, s.conv, "scalar")
                ct = Hb["cT"]
                bank = freed(pe, s.banks[0])
                for m in range(M):
                    for g in range(2):
                        c0 = (2 * m + g) * P
                        nc.tensor.matmul(bank[:, c0:c0 + P], ct[:, 8 + g, m * P:(m + 1) * P],
                                         ct[:, 10 + g, m * P:(m + 1) * P], start=True, stop=True)
                bank = freed(pe, s.banks[1])
                for g in range(2):
                    last = transpose(bank[:, g * P:(g + 1) * P], ct[:, 8 + g, 0:P])
                last.then_inc(sem["bback", "tensor"], 1)
            elif s.kind == "xback":
                ended(pe, s.conv, "scalar")
                for m in range(M):
                    bank = freed(pe, s.banks[m])
                    for i in range(4):
                        last = transpose(bank[:, i * P:(i + 1) * P], Hb["cT"][:, 4 * s.j + i, m * P:(m + 1) * P])
                last.then_inc(sem["xback", "tensor"], 1)
            elif s.kind == "state":
                ended(pe, s.xback, "gpsimd")
                ended(pe, s.bback, "scalar")
                bank = freed(pe, s.bank)
                nc.tensor.matmul(bank[:, :], Hb["bt"][:, s.g, :], Hb["xgd"][:, s.g * 512:(s.g + 1) * 512],
                                 start=True, stop=True).then_inc(sem["state", "tensor"], 1)
            elif s.kind == "decay":
                m, g = s.mg
                ended(pe, s.sums, "scalar")
                bank = freed(pe, s.bank)
                for i in range(4):
                    hh = 8 * g + 4 * (s.q % 2) + i
                    seg = bank[:, i * P:(i + 1) * P]
                    nc.tensor.matmul(seg, identb[:, :], masks[:, M_SCAN:M_SCAN + P], start=True, stop=False)
                    pick = masks[0:96, M_SEL + SH * m + hh:M_SEL + SH * m + hh + 1]
                    last = nc.tensor.matmul(seg, spread(pick, [96, P]), csum[0:96, :], start=False, stop=True)
                last.then_inc(sem["decay", "tensor"], 1)
            elif s.kind == "diag":
                ended(pe, s.decay, "vector")
                ended(pe, s.xback, "gpsimd")
                bank = freed(pe, s.bank) if s.i % 2 == 0 else psum[4 + s.bank.at]
                for i in range(4):
                    hh = 8 * s.g + 4 * (s.q % 2) + i
                    c0 = (4 * (s.q % 2) + i) * HD
                    last = nc.tensor.matmul(bank[:, c0:c0 + HD], Hb[f"MT{s.decay.i % 2}"][:, i, :],
                                            Hb["xg"][:, s.m, hh * HD:(hh + 1) * HD], start=True, stop=True)
                last.then_inc(sem["diag", "tensor"], 1)
            elif s.kind == "off":
                ended(pe, s.state, "scalar")
                bank = freed(pe, s.bank)
                nc.tensor.matmul(bank[:, :], Hb["cT"][:, 10 + s.g, P:S], Hb["st"][:, s.g * 512:(s.g + 1) * 512],
                                 start=True, stop=True).then_inc(sem["off", "tensor"], 1)

    @blk.scalar
    def _(act):
        def split(c, half):
            if c.i == 0:
                act.wait_ge(raw_in[0] if half else raw_first, 16)
            elif half == 0:
                act.wait_ge(raw_in[c.i % RAW], arrived[c.i])
            if half == 0 and c.i >= SPLIT:
                act.wait_ge(sem["chunk", "tensor"], c.i - SPLIT + 1)
            cols = half_of(c, half)
            nc.scalar.activation(hi[c.i % SPLIT][:, cols], raw[c.i % RAW][:, cols], ACT.Copy)\
              .then_inc(sem["chunk", "scalar"], 1)

        def done(ins, s):
            ins.then_inc(sem[s.kind, "scalar"], 1)

        def load_small():
            act.dma_start(cst[:, P:C_KEEP], t["cst"][:, P:C_KEEP]).then_inc(const_in, 16)
            act.dma_start(sinks[:, 0, :], t["sinks_a"][0].partition_broadcast(P)).then_inc(sinks_in, 16)
            with nc.allow_non_contiguous_dma("a column of positions"):
                act.dma_start(posi[:, :], t["positions_2"][0].rearrange("(m p) -> p m", p=P)).then_inc(small_in, 16)
            for n, name in enumerate(("dt_bias_2", "a_log_2", "d_skip_2")):
                act.dma_start(small[:, :, n, :], t[name].partition_broadcast(P)).then_inc(small_in, 16)
            act.dma_start(stage[:, :], t["cst"][:, C_KEEP:C_ALL]).then_inc(masks_in, 16)
            act.dma_start(taps_in[0:8 * NCT, :], t["conv_w_2"].rearrange("l t (c p) -> (l t c) p", p=P))\
               .then_inc(small_in, 16)
            act.dma_start(taps_in[8 * NCT:10 * NCT, :], t["conv_b_2"].rearrange("l (c p) -> (l c) p", p=P))\
               .then_inc(small_in, 16)

        junked = []

        def square_sum(x, out, s):
            if junked:
                ended(act, junked[-1], "scalar")
            done(nc.scalar.activation(junk[:, :], x, ACT.Square, accum_out=out), s)
            junked.append(s)

        for s in sc.steps:
            if s.kind in ("begin", "chunk", "rest"):
                if s.kind == "rest" and s.i == 0:
                    load_small()
                if s.kind == "chunk" and s.i == SETUP_AT:
                    act.wait_ge(setup_dve, 2)
                    nc.scalar.activation(sine[:, :, :, :], angle[:, :, :, :], ACT.Sin).then_inc(setup_act, 1)
                    nc.scalar.activation(small[:, :, 1, :], small[:, :, 1, :], ACT.Exp).then_inc(setup_act, 1)
                for i, half in due(s):
                    if i < len(chunks):
                        split(chunks[i], half)
            elif s.kind == "turn":
                act.wait_ge(sem["turn", "tensor"], s.i + 1)
                bank = psum[4 + s.bank.at]
                if s.dst == "h":
                    out = hT[0][:, s.k0:s.k0 + 2, :].rearrange("p k t -> p (k t)")
                    done(nc.scalar.activation(out, bank[:, :], ACT.Copy), s)
                else:
                    dst = (xT if s.dst == "x" else oT)[0]
                    done(nc.scalar.activation(dst[:, s.k0:s.k0 + 4, s.m * P:(s.m + 1) * P],
                                              bank[:, :].rearrange("p (k t) -> p k t", k=4), ACT.Copy), s)
            elif s.kind == "square":
                if s.added is not None:
                    ended(act, s.added, "vector")
                else:
                    act.wait_ge(x_in if s.n else x_first[s.m], 16)
                square_sum(h[:, s.m, s.n * 512:(s.n + 1) * 512], sumsq[:, 2 * s.m + s.n:2 * s.m + s.n + 1], s)
            elif s.kind == "ev_kv":
                ended(act, s.rstd, "vector")
                bank = ready(act, s.block, s.m)
                B = Hb if s.dt is not None else A
                rs = rms[:, 1, s.m:s.m + 1]
                kw = s.nkv * HD
                nc.scalar.activation(B["k"][:, s.m, 0:s.nkv, :], bank[:, 0:kw].rearrange("p (g d) -> p g d", d=HD),
                                     ACT.Copy, scale=rs)
                if s.dt is not None:
                    nc.scalar.activation(B["dtr"][:, s.m, :], bank[:, 256:272], ACT.Copy, scale=rs)
                done(nc.scalar.activation(B["v1"][:, s.m, 0:s.nkv, 0:HD],
                                          bank[:, kw:2 * kw].rearrange("p (g d) -> p g d", d=HD),
                                          ACT.Copy, scale=rs), s)
            elif s.kind == "ev_q":
                ended(act, s.rstd, "vector")
                if s.i == 0:
                    act.wait_ge(setup_dve, 1)
                bank = ready(act, s.block, s.m)
                B = Hb if s.kind_of == "h" else A
                done(nc.scalar.activation(B["q"][:, s.m, s.j * 512:(s.j + 1) * 512], bank[:, :], ACT.Copy,
                                          scale=rms[:, 1, s.m:s.m + 1]), s)
            elif s.kind == "ev_z":
                bank = ready(act, s.block, s.m)
                B = Hb if s.kind_of == "h" else A
                done(nc.scalar.activation(B["z"][:, s.m, s.j * 512:(s.j + 1) * 512], bank[:, :], ACT.Silu,
                                          scale=rms[:, 1, s.m:s.m + 1]), s)
            elif s.kind == "ev_x":
                bank = ready(act, s.block, s.m)
                if s.conv is not None:
                    ended(act, s.conv, "tensor")
                done(nc.scalar.activation(Hb["xin"][:, s.m, :], bank[:, :], ACT.Copy,
                                          scale=rms[:, 1, s.m:s.m + 1]), s)
            elif s.kind == "ev_up":
                ended(act, s.rstd, "vector")
                if s.i >= 2:
                    act.wait_ge(sem["ev_up", "vector"], s.i - 1)
                for m in range(M):
                    bank = ready(act, s.block, m)
                    last = nc.scalar.activation(sil[s.i % 2][:, m, :], bank[:, 0:UPW], ACT.Silu,
                                                scale=rms[:, 1, m:m + 1])
                done(last, s)
            elif s.kind == "taps":
                act.wait_ge(sem["taps", "tensor"], 1)
                done(nc.scalar.activation(taps[:, :], psum[4 + s.bank.at][:, 0:10 * NCT], ACT.Copy), s)
            elif s.kind == "turn_k":
                B = A if s.rope.kind_of != "h" else Hb
                act.wait_ge(sem["turn_k", "tensor"], s.i + 1)
                done(nc.scalar.activation(B["kT"][:, 2 * s.t:2 * s.t + 2, :],
                                          psum[4 + s.bank.at][:, :].rearrange("p (g t) -> p g t", g=2), ACT.Copy), s)
            elif s.kind == "turn_q":
                B = A if s.rope.kind_of != "h" else Hb
                act.wait_ge(sem["turn_q", "tensor"], s.i + 1)
                c0 = 4 * s.j + 2 * s.t
                done(nc.scalar.activation(B["qT"][:, c0:c0 + 2, :],
                                          psum[4 + s.bank.at][:, :].rearrange("p (g t) -> p g t", g=2), ACT.Copy), s)
            elif s.kind == "scores":
                a, hd = s.att, s.head
                B = Hb if a["kind"] == "h" else A
                act.wait_ge(sem["scores", "vector"], s.i + 1)
                if s.i >= 2:
                    act.wait_ge(sem["flip", "tensor"], s.i - 1)
                bank, pr = psum[4 + s.bank.at], B[f"prob{s.p % 2}"]
                nc.scalar.activation(pr[:, 0:P], bank[:, 0:P], ACT.Exp, scale=SCALE, bias=shift[:, hd, 0:1])
                done(nc.scalar.activation(pr[:, P:QC], bank[:, P:QC], ACT.Exp, scale=SCALE,
                                          bias=shift[:, hd, 1:2]), s)
            elif s.kind == "flip" and s.att["kind"] != "h":
                act.wait_ge(sem["flip", "tensor"], s.i + 1)
                if s.i >= 2:
                    act.wait_ge(sem["pv", "tensor"], s.i - 1)
                done(nc.scalar.activation(A[f"probT{s.p % 2}"][:, :], psum[4 + s.bank.at][:, 0:QC], ACT.Copy), s)
            elif s.kind == "oev":
                a = s.att
                B = Hb if a["kind"] == "h" else A
                ended(act, s.pv, "tensor")
                W1 = HD + 1
                src = psum[4 + s.bank.at][:, 0:4 * W1].rearrange("p (g m d) -> p m g d", g=2, m=2)
                done(nc.scalar.activation(B["o"][:, :, 2 * s.pair:2 * s.pair + 2, :], src, ACT.Copy), s)
            elif s.kind == "sink":
                act.wait_ge(sem["sink", "vector"], s.i + 1)
                e = esink[:, 8 * s.half:8 * s.half + 8, :]
                done(nc.scalar.activation(e, e, ACT.Exp), s)
            elif s.kind == "soft1":
                act.wait_ge(sem["soft1", "vector"], s.i + 1)
                done(nc.scalar.activation(Hb["sb"][:, :, :], Hb["sb"][:, :, :], ACT.Exp, scale=-1.0), s)
            elif s.kind == "soft2":
                act.wait_ge(sem["soft2", "vector"], s.i + 1)
                done(nc.scalar.activation(Hb["sd"][:, :, :], Hb["sc"][:, :, :], ACT.Ln), s)
            elif s.kind == "sums":
                act.wait_ge(sem["sums", "vector"], s.i + 1)
                nc.scalar.activation(Hb["dec"][:, :], Hb["dif"][:, :], ACT.Exp)
                done(nc.scalar.activation(Hb["ecs"][:, :], Hb["ncs"][:, 1, :], ACT.Exp, scale=-1.0), s)
            elif s.kind == "conv":
                if s.i == 0:
                    act.wait_ge(sem["taps", "scalar"], 1)
                act.wait_ge(sem["conv", "tensor"], s.i + 1)
                if s.conv is not None:
                    ended(act, s.conv, "scalar")
                for i in range(2):
                    ct = 2 * s.u + i + (8 if s.j == 0 else 4 * (s.j - 1))
                    last = nc.scalar.activation(Hb[f"acc{s.u}"][:, i, :], psum[4 + s.bank.at][:, i * S:(i + 1) * S],
                                                ACT.Copy, scale=convw[:, s.layer, 3, ct:ct + 1])
                done(last, s)
            elif s.kind == "conv_silu":
                ended(act, s.conv, "vector")
                for i in range(4):
                    ct = (8 + i) if s.j == 0 else 4 * (s.j - 1) + i
                    last = nc.scalar.activation(Hb["cT"][:, ct, :], Hb[f"acc{i // 2}"][:, i % 2, :], ACT.Silu,
                                                bias=convb[:, s.layer, ct:ct + 1])
                done(last, s)
            elif s.kind == "bback":
                act.wait_ge(sem["bback", "tensor"], s.i + 1)
                nc.scalar.activation(Hb["cb"][:, :, :, :].rearrange("p m g l -> p (m g l)"),
                                     psum[4 + s.banks[0].at][:, :], ACT.Copy)
                done(nc.scalar.activation(Hb["bt"][:, :, :].rearrange("p g n -> p (g n)"),
                                          psum[4 + s.banks[1].at][:, 0:2 * P], ACT.Copy), s)
            elif s.kind == "xback":
                act.wait_ge(sem["xback", "tensor"], s.i + 1)
                for m in range(M):
                    last = nc.scalar.activation(Hb["xs"][:, m, s.j * 512:(s.j + 1) * 512],
                                                psum[4 + s.banks[m].at][:, :], ACT.Copy)
                done(last, s)
            elif s.kind == "state":
                act.wait_ge(sem["state", "tensor"], s.i + 1)
                done(nc.scalar.activation(Hb["st"][:, s.g * 512:(s.g + 1) * 512], psum[4 + s.bank.at][:, :],
                                          ACT.Copy), s)
            elif s.kind == "decay":
                m, g = s.mg
                act.wait_ge(sem["decay", "tensor"], s.i + 1)
                if s.i >= 2:
                    act.wait_ge(sem["decay", "vector"], s.i - 1)
                for i in range(4):
                    hh = 8 * g + 4 * (s.q % 2) + i
                    last = nc.scalar.activation(Hb[f"E{s.i % 2}"][:, i, :], psum[4 + s.bank.at][:, i * P:(i + 1) * P],
                                                ACT.Exp, bias=Hb["ncs"][:, m, hh:hh + 1])
                done(last, s)
            elif s.kind == "join":
                act.wait_ge(sem["join", "vector"], s.i + 1)
                square_sum(Hb["xs"][:, s.m, s.g * 512:(s.g + 1) * 512], rmy[:, 0, 2 * s.g + s.m:2 * s.g + s.m + 1], s)

    @blk.gpsimd
    def _(pool):
        def row(name, layer):
            whole = {"final": t["final_norm_2"], "final_g": t["final_g"]}
            return (whole[name] if name in whole else gain_rows[name][layer]).partition_broadcast(P)

        def load_gain(g):
            if g["i"]:
                ended(pool, sc.gains[g["i"] - 1]["users"][-1], "vector")
            pool.dma_start(gains[:, :], row(*g["src"])).then_inc(gain_in, 16)

        load_gain(sc.gains[0])
        nc.gpsimd.memset(power[:, :], -0.5).then_inc(chain["gpsimd"], 1)
        links["gpsimd"] += 1
        pool.wait_ge(chain["gpsimd"], links["gpsimd"])
        after = {id(sc.gains[g["i"] - 1]["users"][-1]): g for g in sc.gains[1:] if g["src"] is not None}
        for s in sc.steps:
            if id(s) in after:
                load_gain(after[id(s)])
            if s.kind == "mid_load":
                ended(pool, s.before, "tensor")
                for i, name in enumerate(("final_g", "norm_mix")):
                    pool.dma_start(mid_rows[i][:, :], row(name, 0)).then_inc(mid_in, 16)
            if s.kind == "meansq":
                pool.wait_ge(sem["meansq", "vector"], s.i + 1)
                _, ms, rs, _ = norm_parts(s)
                nc.gpsimd.tensor_tensor(rs, ms, power[:, :], ALU.pow).then_inc(sem["meansq", "gpsimd"], 1)
            if s.kind == "pool_rope":
                ended(pool, s.ev, "scalar")
                if s.i == 0:
                    pool.wait_ge(const_in, 32)
                t1, t2 = (A[x][:, :].rearrange("p (a d) -> p a d", d=HD) for x in ("pool_rot1", "pool_rot2"))
                gt = nc.gpsimd.tensor_tensor
                for m in range(M):
                    x = A["q"][:, m, s.j * 512:(s.j + 1) * 512].rearrange("p (a d) -> p a d", d=HD)
                    cos, sin = (spread(cst[:, c + m * HD:c + (m + 1) * HD].unsqueeze(1), [P, 8, HD])
                                for c in (C_COS, C_SIN))
                    gt(t1, x, cos, ALU.mult)
                    gt(t2[:, :, 0:HD // 2], x[:, :, HD // 2:HD], sin[:, :, 0:HD // 2], ALU.mult)
                    link(pool, "gpsimd", gt(t2[:, :, HD // 2:HD], x[:, :, 0:HD // 2], sin[:, :, HD // 2:HD], ALU.mult))
                    last = gt(x, t1, t2, ALU.add)
                    if m == 0:
                        link(pool, "gpsimd", last)
                last.then_inc(sem["pool_rope", "gpsimd"], 1)
            if s.kind == "pool_gate":
                B = Hb if s.att["kind"] == "h" else A
                if s.before is not None:
                    ended(pool, s.before, "tensor")
                ended(pool, s.den, "vector")
                q = quarter[s.buf][:, :]
                o = B["o"][:, s.m, 8 * s.half:8 * s.half + 8, 0:HD]
                last = nc.gpsimd.tensor_tensor(q.rearrange("p (a d) -> p a d", d=HD), o,
                                               spread(dens[:, s.m, :].unsqueeze(2), [P, 8, HD]), ALU.mult)
                if s.z is not None:
                    link(pool, "gpsimd", last)
                    ended(pool, s.z, "scalar")
                    last = nc.gpsimd.tensor_tensor(q, q, B["z"][:, s.m, s.half * 512:(s.half + 1) * 512], ALU.mult)
                last.then_inc(sem["pool_gate", "gpsimd"], 1)
            if s.kind != "xback":
                continue
            pool.wait_ge(sem["xback", "scalar"], s.i + 1)
            ended(pool, s.sums, "scalar")
            hs, cols = slice(8 * s.j, 8 * s.j + 8), slice(s.j * 512, (s.j + 1) * 512)
            for m in range(M):
                xs = Hb["xs"][:, m, cols].rearrange("p (s d) -> p s d", d=HD)
                xg = Hb["xg"][:, m, cols].rearrange("p (s d) -> p s d", d=HD)
                link(pool, "gpsimd", nc.gpsimd.tensor_tensor(
                    xg, xs, spread(Hb["dt"][:, m, hs].unsqueeze(2), [P, 8, HD]), ALU.mult))
                link(pool, "gpsimd", nc.gpsimd.tensor_tensor(
                    xs, xs, spread(small[:, s.conv.layer, 2, hs].unsqueeze(2), [P, 8, HD]), ALU.mult))
            nc.gpsimd.tensor_tensor(
                Hb["xgd"][:, cols].rearrange("p (s d) -> p s d", d=HD),
                Hb["xg"][:, 0, cols].rearrange("p (s d) -> p s d", d=HD),
                spread(Hb["dec"][:, hs].unsqueeze(2), [P, 8, HD]), ALU.mult).then_inc(sem["xback", "gpsimd"], 1)

    @blk.vector
    def _(dve):
        tt, ts, stt = nc.vector.tensor_tensor, nc.vector.tensor_scalar, nc.vector.scalar_tensor_tensor

        def chained(ins):
            link(dve, "vector", ins)

        def split(c, half):
            dve.wait_ge(sem["chunk", "scalar"], 2 * c.i + half + 1)
            r, cols = c.i % SPLIT, half_of(c, half)
            tt(lo[r][:, cols], raw[c.i % RAW][:, cols], hi[r][:, cols].bitcast(F32), ALU.subtract)\
              .then_inc(sem["chunk", "vector"], 1)

        def done(ins, s):
            ins.then_inc(sem[s.kind, "vector"], 1)

        def rope(x, cos, sin, t1, t2, half):
            tt(t1, x, cos, ALU.mult)
            tt(t2[..., 0:half], x[..., half:2 * half], sin[..., 0:half], ALU.mult)
            chained(tt(t2[..., half:2 * half], x[..., 0:half], sin[..., half:2 * half], ALU.mult))
            return tt(x, t1, t2, ALU.add)

        rotated = [None]

        def rotate(B, x, m, n, kind):
            if kind == "h":
                cos = spread(trig[:, m, 0, :].unsqueeze(1), [P, n, 16])
                sin = spread(trig[:, m, 1, :].unsqueeze(1), [P, n, 16])
                x, wd, half = x[:, :, 0:16], 16, 8
            else:
                cos = spread(cst[:, C_COS + m * HD:C_COS + (m + 1) * HD].unsqueeze(1), [P, n, HD])
                sin = spread(cst[:, C_SIN + m * HD:C_SIN + (m + 1) * HD].unsqueeze(1), [P, n, HD])
                wd, half = HD, HD // 2
            if rotated[0] is not None:
                ended(dve, rotated[0], "vector")
                rotated[0] = None
            t1 = B["rot1"][:, 0:n * wd].rearrange("p (a d) -> p a d", d=wd)
            t2 = B["rot2"][:, 0:n * wd].rearrange("p (a d) -> p a d", d=wd)
            return rope(x, cos, sin, t1, t2, half)

        def set_up():
            dve.wait_ge(const_in, 32)
            dve.wait_ge(masks_in, 16)
            dve.wait_ge(sinks_in, 16)
            nc.vector.memset(ones[:, :], 1.0)
            ts(sinks[:, 1, :], sinks[:, 0, :], -1.0, None, ALU.mult)
            nc.vector.tensor_copy(identb[:, :], ident)
            chained(nc.vector.tensor_copy(masks[:, :], stage[:, :]))
            nc.vector.memset(A["v1"][:, :, :, :], 1.0).then_inc(setup_dve, 1)

        def angles():
            dve.wait_ge(small_in, 16 * NSMALL)
            chained(nc.vector.tensor_copy(posf[:, :], posi[:, :]))
            two_pi = 2 * math.pi
            c1 = 6.28125
            c2 = float(np.float32(two_pi - c1))
            for m in range(M):
                for f in range(2):
                    last = ts(angle[:, m, f, :], cst[:, C_INV:C_INV + 8], posf[:, m:m + 1], None, ALU.mult)
            chained(last)
            for f in range(2):
                last = ts(turns[:, :, f, :], angle[:, :, f, :], 1.0 / two_pi, 0.25 * (1 - f), ALU.mult, ALU.add)
            chained(last)
            chained(ts(turns[:, :, :, :], turns[:, :, :, :], 12582912.0, None, ALU.add))
            chained(ts(turns[:, :, :, :], turns[:, :, :, :], 12582912.0, None, ALU.subtract))
            for c in (c1, c2, two_pi - c1 - c2):
                chained(stt(angle[:, :, :, :], turns[:, :, :, :], -c, angle[:, :, :, :], ALU.mult, ALU.add))
            chained(ts(angle[:, :, 0, :], angle[:, :, 0, :], math.pi / 2, None, ALU.add))
            lim = float(np.nextafter(np.float32(math.pi), np.float32(0)))
            ts(angle[:, :, :, :], angle[:, :, :, :], lim, -lim, ALU.min, ALU.max).then_inc(setup_dve, 1)

        def tables():
            dve.wait_ge(setup_act, 2)
            for f, sign in enumerate((1.0, -1.0)):
                ts(trig[:, :, f, 0:8], sine[:, :, f, :], sign, None, ALU.mult)
                ts(trig[:, :, f, 8:16], sine[:, :, f, :], 1.0, None, ALU.mult)
            chained(ts(small[:, :, 1, :], small[:, :, 1, :], -1.0, None, ALU.mult))

        for s in sc.steps:
            if s.kind in ("begin", "chunk", "rest"):
                if s.kind == "rest" and s.i == 1:
                    set_up()
                if s.kind == "chunk" and s.i == SETUP_AT:
                    angles()
                if s.kind == "chunk" and s.i == SETUP_AT + 1:
                    tables()
                for i, half in due(s):
                    if i < len(chunks):
                        split(chunks[i], half)
            elif s.kind == "mid_gain":
                dve.wait_ge(mid_in, 32)
                done(tt(gains[:, :], mid_rows[0][:, :], mid_rows[1][:, :], ALU.mult), s)
            elif s.kind == "gained":
                if s.gain["made"]:
                    ended(dve, s.gain["made"], "vector")
                else:
                    dve.wait_ge(gain_in, 16 * s.gain["loaded"])
                if s.i < M:
                    dve.wait_ge(x_first[s.m], 16)
                elif s.i == M:
                    dve.wait_ge(x_in, 16)
                if s.added is not None:
                    ended(dve, s.added, "vector")
                if s.before is not None:
                    ended(dve, s.before, "tensor")
                c = slice(s.n * 512, (s.n + 1) * 512)
                done(tt(quarter[s.buf][:, :], h[:, s.m, c], gains[:, c], ALU.mult), s)
            elif s.kind == "turn":
                dve.wait_ge(sem["turn", "scalar"], s.i + 1)
                bank = psum[4 + s.bank.at]
                if s.dst == "h":
                    a, b = (x[:, s.k0:s.k0 + 2, :].rearrange("p k t -> p (k t)") for x in hT)
                    done(tt(b, bank[:, :], a.bitcast(F32), ALU.subtract), s)
                else:
                    a, b = (x[:, s.k0:s.k0 + 4, s.m * P:(s.m + 1) * P] for x in (xT if s.dst == "x" else oT))
                    done(tt(b, bank[:, :].rearrange("p (k t) -> p k t", k=4), a.bitcast(F32), ALU.subtract), s)
            elif s.kind == "meansq":
                sq, ms, _, _ = norm_parts(s)
                if s.what == "y":
                    dve.wait_ge(sem["join", "scalar"], s.of)
                    done(ts(ms, sq, 1.0 / 512, EPS, ALU.mult, ALU.add), s)
                else:
                    dve.wait_ge(sem["square", "scalar"], s.of)
                    q = sumsq[:, :].rearrange("p (m n) -> p m n", n=2)
                    chained(tt(ms, q[:, :, 0], q[:, :, 1], ALU.add))
                    done(ts(ms, ms, 1.0 / D, EPS, ALU.mult, ALU.add), s)
            elif s.kind == "newton":
                ended(dve, s.before, "gpsimd")
                _, ms, rs, y = norm_parts(s)
                chained(tt(y, rs, rs, ALU.mult))
                chained(tt(y, y, ms, ALU.mult))
                chained(ts(y, y, -0.5, 1.5, ALU.mult, ALU.add))
                last = tt(rs, rs, y, ALU.mult)
                if s.what == "both":
                    chained(last)
                    last = tt(rs, rs, rms[:, 2, :], ALU.mult)
                done(last, s)
            elif s.kind == "added":
                bank = ready(dve, s.block, s.m)
                x = h[:, s.m, s.n * 512:(s.n + 1) * 512]
                done(tt(x, bank[:, :], x, ALU.add), s)
            elif s.kind == "ev_up":
                dve.wait_ge(sem["ev_up", "scalar"], s.i + 1)
                if s.before is not None:
                    ended(dve, s.before, "tensor")
                for m in range(M):
                    last = stt(quarter[s.buf][:, m * UPW:(m + 1) * UPW], psum[2 * s.block["pair"] + m][:, UPW:2 * UPW],
                               rms[:, 1, m:m + 1], sil[s.i % 2][:, m, :], ALU.mult, ALU.mult)
                done(last, s)
            elif s.kind == "rope_k":
                B = Hb if s.kind_of == "h" else A
                ended(dve, s.ev, "scalar")
                if s.kind_of == "h":
                    nc.vector.memset(B["v1"][:, :, :, HD:HD + 1], 1.0)
                for m in range(M):
                    x = B["k"][:, m, 0:s.nkv, :]
                    chained(rotate(B, x, m, s.nkv, s.kind_of))
                    for a in range(2):
                        last = nc.vector.tensor_copy(B["kdup"][:, m, 0:s.nkv, a, :], x)
                done(last, s)
            elif s.kind == "rope_q":
                B = Hb if s.kind_of == "h" else A
                ended(dve, s.ev, "scalar")
                for m in range(M):
                    x = B["q"][:, m, s.j * 512:(s.j + 1) * 512].rearrange("p (a d) -> p a d", d=HD)
                    last = rotate(B, x, m, 8, s.kind_of)
                    if m == 0:
                        chained(last)
                done(last, s)
                rotated[0] = s
            elif s.kind == "scores":
                a, hd = s.att, s.head
                dve.wait_ge(sem["scores", "tensor"], s.i + 1)
                rm = rowmax[:, s.i % 2, :]
                nc.vector.tensor_reduce(rm[:, 0:1], psum[4 + s.bank.at][:, 0:P], AXX, ALU.max)
                chained(nc.vector.tensor_reduce(rm[:, 1:2], psum[4 + s.bank.at][:, P:QC], AXX, ALU.max))
                if a["kind"] == "a":
                    done(ts(shift[:, hd, :], rm[:, 0:2], -SCALE, sinks[:, 1, hd:hd + 1], ALU.mult, ALU.min), s)
                else:
                    done(ts(shift[:, hd, :], rm[:, 0:2], -SCALE, None, ALU.mult), s)
            elif s.kind == "flip" and s.att["kind"] == "h":
                dve.wait_ge(sem["flip", "tensor"], s.i + 1)
                if s.i >= 2:
                    dve.wait_ge(sem["pv", "tensor"], s.i - 1)
                done(tt(Hb[f"probT{s.p % 2}"][:, :], psum[4 + s.bank.at][:, 0:QC], mult, ALU.mult), s)
            elif s.kind == "sink":
                dve.wait_ge(sem["scores", "vector"], s.att["scores"][8 * s.half + 7].i + 1)
                e = slice(8 * s.half, 8 * s.half + 8)
                done(tt(esink[:, e, :], shift[:, e, :], spread(sinks[:, 0, e].unsqueeze(2), [P, 8, M]), ALU.add), s)
            elif s.kind == "den":
                B = Hb if s.att["kind"] == "h" else A
                ended(dve, s.oev, "scalar")
                d = B["o"][:, :, 8 * s.half:8 * s.half + 8, HD]
                if s.es is not None:
                    ended(dve, s.es, "scalar")
                    e = esink[:, 8 * s.half:8 * s.half + 8, :].rearrange("p s m -> p m s")
                    chained(tt(dens[:, :, :], d, e, ALU.add))
                    d = dens[:, :, :]
                done(nc.vector.reciprocal(dens[:, :, :], d), s)
            elif s.kind == "gate":
                B = Hb if s.att["kind"] == "h" else A
                if s.before is not None:
                    ended(dve, s.before, "tensor")
                ended(dve, s.den, "vector")
                q = quarter[s.buf][:, :]
                o = B["o"][:, s.m, 8 * s.half:8 * s.half + 8, 0:HD]
                first = tt(q.rearrange("p (a d) -> p a d", d=HD), o, spread(dens[:, s.m, :].unsqueeze(2), [P, 8, HD]),
                           ALU.mult)
                if s.z is None:
                    done(first, s)
                else:
                    chained(first)
                    ended(dve, s.z, "scalar")
                    done(tt(q, q, B["z"][:, s.m, s.half * 512:(s.half + 1) * 512], ALU.mult), s)
            elif s.kind == "soft1":
                ended(dve, s.ev, "scalar")
                for m in range(M):
                    last = tt(Hb["dtr"][:, m, :], Hb["dtr"][:, m, :], small[:, s.layer, 0, :], ALU.add)
                chained(last)
                ts(Hb["sa"][:, :, :], Hb["dtr"][:, :, :], 0.0, None, ALU.max)
                done(stt(Hb["sb"][:, :, :], Hb["dtr"][:, :, :], -1.0, Hb["dtr"][:, :, :], ALU.mult, ALU.max), s)
            elif s.kind == "soft2":
                ended(dve, s.before, "scalar")
                done(ts(Hb["sc"][:, :, :], Hb["sb"][:, :, :], 1.0, None, ALU.add), s)
            elif s.kind == "soft3":
                ended(dve, s.before, "scalar")
                e, u, l, dt = (Hb[x][:, :, :] for x in ("sb", "sc", "sd", "dt"))
                same = Hb["dtr"][:, :, :]
                ts(same, u, 1.0, None, ALU.is_equal)
                chained(ts(dt, u, 1.0, None, ALU.subtract))
                chained(tt(dt, dt, same, ALU.add))
                chained(tt(l, l, same, ALU.add))
                chained(nc.vector.reciprocal(dt, dt))
                chained(tt(l, l, e, ALU.mult))
                chained(tt(dt, dt, l, ALU.mult))
                chained(tt(dt, dt, Hb["sa"][:, :, :], ALU.add))
                for m in range(M):
                    last = tt(Hb["da"][:, :, SH * m:SH * (m + 1)], spread(Hb["dt"][:, m, :].unsqueeze(1), [P, 3, SH]),
                              spread(small[:, s.layer, 1, :].unsqueeze(1), [P, 3, SH]), ALU.mult)
                done(last, s)
            elif s.kind == "sums":
                dve.wait_ge(sem["sums", "tensor"], s.i + 1)
                bank = psum[4 + s.bank.at]
                chained(ts(Hb["ncs"][:, :, :].rearrange("p m s -> p (m s)"), bank[:, 0:32], -1.0, None, ALU.mult))
                tt(Hb["dif"][:, :], bank[:, 32:48], Hb["ncs"][:, 0, :], ALU.add)
                copy, left, by_head = nc.vector.tensor_copy, Hb["rest"], bank[0:96, 64:64 + P]
                chained(copy(csum[0:96, :], by_head))
                chained(tt(left[0:96, :], by_head, csum[0:96, :], ALU.subtract))
                copy(csum[32:64, :], left[32:64, :])
                chained(copy(csum[64:96, :], left[64:96, :]))
                chained(tt(left[64:96, :], left[64:96, :], csum[64:96, :], ALU.subtract))
                done(copy(csum[64:96, :], left[64:96, :]), s)
            elif s.kind == "conv":
                dve.wait_ge(sem["conv", "scalar"], s.i + 1)
                cw, bank = convw[:, s.layer, :, :], psum[4 + s.bank.at]
                for tap in range(1, 4):
                    for i in range(2):
                        ct = 2 * s.u + i + (8 if s.j == 0 else 4 * (s.j - 1))
                        acc, x = Hb[f"acc{s.u}"][:, i, :], bank[:, i * S:(i + 1) * S]
                        if tap > 1:
                            dve.wait_ge(chain["vector"], links["vector"] - 1)
                        ins = stt(acc[:, tap:S], x[:, 0:S - tap], cw[:, 3 - tap, ct:ct + 1], acc[:, tap:S],
                                  ALU.mult, ALU.add)
                        if tap < 3 or i == 0:
                            ins.then_inc(chain["vector"], 1)
                            links["vector"] += 1
                        else:
                            done(ins, s)
            elif s.kind == "decay":
                m, g = s.mg
                ended(dve, s.bback, "scalar")
                dve.wait_ge(sem["decay", "scalar"], s.i + 1)
                if s.i >= 2:
                    dve.wait_ge(sem["diag", "tensor"], s.i - 1)
                done(tt(Hb[f"MT{s.i % 2}"][:, :, :], Hb[f"E{s.i % 2}"][:, :, :],
                        spread(Hb["cb"][:, m, g, :].unsqueeze(1), [P, 4, P]), ALU.mult), s)
            elif s.kind == "join":
                ended(dve, s.last, "tensor")
                ended(dve, s.xback, "gpsimd")
                c = slice(s.g * 512, (s.g + 1) * 512)
                y = Hb["xs"][:, s.m, c]
                chained(tt(y, psum[4 + s.bank.at][:, :], y, ALU.add))
                if s.obank is not None:
                    t_ = Hb["rot1"][:, :]
                    chained(tt(t_.rearrange("p (s d) -> p s d", d=HD),
                               psum[4 + s.obank.at][:, :].rearrange("p (s d) -> p s d", d=HD),
                               spread(Hb["ecs"][:, 8 * s.g:8 * s.g + 8].unsqueeze(2), [P, 8, HD]), ALU.mult))
                    chained(tt(y, y, t_, ALU.add))
                ended(dve, s.z, "scalar")
                done(tt(y, y, Hb["z"][:, s.m, c], ALU.mult), s)
            elif s.kind == "ynorm":
                ended(dve, s.rstd, "vector")
                dve.wait_ge(gain_in, 16 * s.gain["loaded"])
                if s.before is not None:
                    ended(dve, s.before, "tensor")
                c = slice(s.g * 512, (s.g + 1) * 512)
                n = 2 * s.g + s.m
                done(stt(quarter[s.buf][:, :], Hb["xs"][:, s.m, c], rmy[:, 2, n:n + 1], gains[:, c],
                         ALU.mult, ALU.mult), s)
            elif s.kind == "final":
                ended(dve, s.rstd, "vector")
                if s.what == "mid":
                    rs, g = rms[:, 2, s.m:s.m + 1], mid_rows[0]
                else:
                    dve.wait_ge(gain_in, 16 * s.gain["loaded"])
                    rs, g = rms[:, 1, s.m:s.m + 1], gains
                done(stt(h[:, s.m, :], h[:, s.m, :], rs, g[:, :], ALU.mult, ALU.mult), s)

    program.close()


_INS = ["x", "norm_g", "w_in_a", "sinks_a", "w_in_b", "w_out", "positions_2", "norm_mix_2", "w_in_2", "conv_w_2",
        "conv_b_2", "dt_bias_2", "a_log_2", "d_skip_2", "ssm_norm_2", "w_out_2", "norm_ffn_2", "w_gate_2",
        "w_up_2", "w_down_2", "final_norm_2", "final_g"]


def kernel(**inputs):
    from concourse import bacc
    from concourse.bass_utils import run_bass_kernel_spmd

    nc = bacc.Bacc("TRN2", target_bir_lowering=False, num_devices=1)
    arrays, t = {}, {}
    for name in _INS:
        a = np.ascontiguousarray(inputs[name])
        arrays[f"in_{name}"] = a
        t[name] = nc.dram_tensor(f"in_{name}", a.shape, mybir.dt.from_np(a.dtype), kind="ExternalInput").ap()
    c = constants()
    arrays["in_cst"] = c
    t["cst"] = nc.dram_tensor("in_cst", c.shape, F32, kind="ExternalInput").ap()
    t["out"] = nc.dram_tensor("out", (1, S, D), F32, kind="ExternalOutput").ap()
    build(nc, t)
    r = run_bass_kernel_spmd(nc, [arrays], core_ids=[0])
    return r.results[0]["out"]
```
